# Optimizing a Trainium2 kernel written in Bass

```python
import math
import jax, jax.numpy as jnp
from jax import lax
import numpy as np

D_MODEL = 2048
BATCH = 1
SEQ = 256
DEPTH = 1

HEAD_DIM = 64
N_HEADS_TOTAL = D_MODEL // HEAD_DIM
N_HEADS_A = N_HEADS_TOTAL // 4
N_KV_A = N_HEADS_A // 4
N_HEADS_B = N_HEADS_TOTAL // 4
N_HEADS_C = N_HEADS_TOTAL // 2
BLOCK = 128
WINDOW_A = 128
DILATED_PAIRS = ((128, 1), (512, 4), (2048, 16))
N_BUCKETS = 32
T5_MAX_DIST = 2048
D_FF = 256 * (-(-(8 * D_MODEL // 3) // 256))
CONV_WIDTH = 3
EPS = 1e-6
NEG_INF = -1e30

A_Q = N_HEADS_A * HEAD_DIM
A_KV = N_KV_A * HEAD_DIM
B_W = N_HEADS_B * HEAD_DIM
C_W = N_HEADS_C * HEAD_DIM
IN_WIDTH = A_Q + 2 * A_KV + 3 * B_W + 3 * C_W
MIX_WIDTH = A_Q + B_W + C_W


def rmsnorm(x, g):
    xf = x.astype(jnp.float32)
    y = xf * lax.rsqrt(jnp.mean(xf * xf, axis=-1, keepdims=True) + EPS)
    return (y * g.astype(jnp.float32)).astype(x.dtype)

def t5_bucket(dist):
    max_exact = N_BUCKETS // 2
    d = jnp.maximum(dist, 0)
    large = max_exact + (jnp.log(jnp.maximum(d, 1).astype(jnp.float32) / max_exact)
                         / math.log(T5_MAX_DIST / max_exact) * (N_BUCKETS - max_exact)).astype(jnp.int32)
    large = jnp.minimum(large, N_BUCKETS - 1)
    return jnp.where(d < max_exact, d, large)

def block_rel_bias(table, dil):
    rel = jnp.arange(BLOCK)[:, None] + BLOCK - jnp.arange(2 * BLOCK)[None, :]
    buckets = t5_bucket(rel * dil)
    return jnp.transpose(table[buckets], (2, 0, 1)).astype(jnp.float32)

def banded_attention(q, k, v, bias, max_dist, sinks=None):
    n, length, hq, hd = q.shape
    hk = k.shape[2]
    grp = hq // hk
    lp = -(-length // BLOCK) * BLOCK
    if lp != length:
        padw = ((0, 0), (0, lp - length), (0, 0), (0, 0))
        q, k, v = jnp.pad(q, padw), jnp.pad(k, padw), jnp.pad(v, padw)
    nb = lp // BLOCK
    qb = q.reshape(n, nb, BLOCK, hk, grp, hd).astype(jnp.float32)
    kb = k.reshape(n, nb, BLOCK, hk, hd).astype(jnp.float32)
    vb = v.reshape(n, nb, BLOCK, hk, hd).astype(jnp.float32)
    prev = ((0, 0), (1, 0), (0, 0), (0, 0), (0, 0))
    kk = jnp.concatenate([jnp.pad(kb[:, :-1], prev), kb], axis=2)
    vv = jnp.concatenate([jnp.pad(vb[:, :-1], prev), vb], axis=2)
    logits = (jnp.einsum('nbqhgd,nbkhd->nbhgqk', qb, kk) * (hd ** -0.5)
              + bias.reshape(hk, grp, BLOCK, 2 * BLOCK))
    rel = jnp.arange(BLOCK)[:, None] + BLOCK - jnp.arange(2 * BLOCK)[None, :]
    key_abs = (jnp.arange(nb)[:, None] - 1) * BLOCK + jnp.arange(2 * BLOCK)[None, :]
    mask = ((rel >= 0) & (rel <= max_dist))[None] & (key_abs >= 0)[:, None, :]
    logits = jnp.where(mask[None, :, None, None], logits, NEG_INF)
    m = jnp.max(logits, axis=-1, keepdims=True)
    if sinks is not None:
        s = sinks.astype(jnp.float32).reshape(hk, grp, 1, 1)
        m = jnp.maximum(m, s)
    p = jnp.exp(logits - m)
    denom = jnp.sum(p, axis=-1, keepdims=True)
    if sinks is not None:
        denom = denom + jnp.exp(s - m)
    out = jnp.einsum('nbhgqk,nbkhd->nbhgqd', p / denom, vv)
    out = jnp.transpose(out, (0, 1, 4, 2, 3, 5)).reshape(n, lp, hq, hd)[:, :length]
    lse = jnp.transpose((m + jnp.log(denom))[..., 0], (0, 1, 4, 2, 3)).reshape(n, lp, hq)[:, :length]
    return out, lse

def stick_breaking_attention(q, k, v):
    b_, s_, h, hd = q.shape
    nb = s_ // BLOCK
    qb = jnp.transpose(q.reshape(b_, nb, BLOCK, h, hd), (1, 0, 2, 3, 4))
    kf = k.astype(jnp.float32)
    vf = v.astype(jnp.float32)
    s_pos = jnp.arange(s_)

    def one_block(args):
        qblk, blk = args
        z = jnp.einsum('bqhd,bkhd->bhqk', qblk.astype(jnp.float32), kf) * (hd ** -0.5)
        t_pos = blk * BLOCK + jnp.arange(BLOCK)
        causal = s_pos[None, :] < t_pos[:, None]
        log_rem = jnp.where(causal, jax.nn.log_sigmoid(-z), 0.0)
        suffix = lax.cumsum(log_rem, axis=3, reverse=True) - log_rem
        a = jnp.where(causal, jnp.exp(jax.nn.log_sigmoid(z) + suffix), 0.0)
        return jnp.einsum('bhqk,bkhd->bqhd', a, vf)

    out = lax.map(one_block, (qb, jnp.arange(nb)))
    return jnp.transpose(out, (1, 0, 2, 3, 4)).reshape(b_, s_, h, hd)

def dilated_attention(q, k, v, table_c):
    b_, s_, h, hd = q.shape
    outs, lses = [], []
    for window, dil in DILATED_PAIRS:
        def to_sub(t):
            return jnp.transpose(t.reshape(b_, s_ // dil, dil, h, hd), (0, 2, 1, 3, 4)).reshape(b_ * dil, s_ // dil, h, hd)
        o, lse = banded_attention(to_sub(q), to_sub(k), to_sub(v), block_rel_bias(table_c, dil), window // dil)
        outs.append(jnp.transpose(o.reshape(b_, dil, s_ // dil, h, hd), (0, 2, 1, 3, 4)).reshape(b_, s_, h, hd))
        lses.append(jnp.transpose(lse.reshape(b_, dil, s_ // dil, h), (0, 2, 1, 3)).reshape(b_, s_, h))
    w = jax.nn.softmax(jnp.stack(lses, axis=0), axis=0)
    return jnp.sum(w[..., None] * jnp.stack(outs, axis=0), axis=0)

def causal_dwconv(u, w, b):
    up = jnp.pad(u, ((0, 0), (CONV_WIDTH - 1, 0), (0, 0)))
    s_ = u.shape[1]
    acc = b
    for i in range(CONV_WIDTH):
        acc = acc + w[i] * up[:, i:i + s_]
    return acc

def first_inputs(seed: int = 0) -> dict:
    key = jax.random.key(seed)
    ks = jax.random.split(key, 20)
    f32 = jnp.float32

    def nrm(k, shape, scale):
        return jax.random.normal(k, shape, f32) * scale

    return {
        "x": nrm(ks[0], (BATCH, SEQ, D_MODEL), 1.0),
        "attn_norm": 1.0 + nrm(ks[1], (DEPTH, D_MODEL), 0.02),
        "w_in": nrm(ks[2], (DEPTH, D_MODEL, IN_WIDTH), D_MODEL ** -0.5),
        "a_q_gain": 1.0 + nrm(ks[3], (DEPTH, HEAD_DIM), 0.02),
        "a_k_gain": 1.0 + nrm(ks[4], (DEPTH, HEAD_DIM), 0.02),
        "a_sinks": nrm(ks[5], (DEPTH, N_HEADS_A), 0.5),
        "c_q_gain": 1.0 + nrm(ks[6], (DEPTH, HEAD_DIM), 0.02),
        "c_k_gain": 1.0 + nrm(ks[7], (DEPTH, HEAD_DIM), 0.02),
        "rel_bias_table": nrm(ks[8], (N_BUCKETS, N_HEADS_A + N_HEADS_C), 0.5),
        "mix_out_gain": 1.0 + nrm(ks[9], (DEPTH, MIX_WIDTH), 0.02),
        "w_out": nrm(ks[10], (DEPTH, MIX_WIDTH, D_MODEL), MIX_WIDTH ** -0.5),
        "ffn_norm": 1.0 + nrm(ks[11], (DEPTH, D_MODEL), 0.02),
        "w_up": nrm(ks[12], (DEPTH, D_MODEL, 2 * D_FF), D_MODEL ** -0.5),
        "conv_w": nrm(ks[13], (DEPTH, CONV_WIDTH, 2 * D_FF), CONV_WIDTH ** -0.5),
        "conv_b": nrm(ks[14], (DEPTH, 2 * D_FF), 0.02),
        "w_down": nrm(ks[15], (DEPTH, D_FF, D_MODEL), D_FF ** -0.5),
    }

def first_block(x, attn_norm, w_in, a_q_gain, a_k_gain, a_sinks, c_q_gain, c_k_gain, rel_bias_table,
              mix_out_gain, w_out, ffn_norm, w_up, conv_w, conv_b, w_down):
    b_, s_, _ = x.shape
    sizes = [A_Q, A_KV, A_KV, B_W, B_W, B_W, C_W, C_W, C_W]
    offsets = [int(o) for o in np.cumsum(sizes)[:-1]]
    table_a = rel_bias_table[:, :N_HEADS_A]
    table_c = rel_bias_table[:, N_HEADS_A:]
    bias_a = block_rel_bias(table_a, 1)
    for l in range(DEPTH):
        h = rmsnorm(x, attn_norm[l])
        proj = jnp.einsum('bsd,de->bse', h, w_in[l])
        aq, ak, av, bq, bk, bv, cq, ck, cv = jnp.split(proj, offsets, axis=-1)
        heads = lambda t, n: t.reshape(b_, s_, n, HEAD_DIM)
        out_a, _ = banded_attention(rmsnorm(heads(aq, N_HEADS_A), a_q_gain[l]),
                                    rmsnorm(heads(ak, N_KV_A), a_k_gain[l]),
                                    heads(av, N_KV_A), bias_a, WINDOW_A - 1, sinks=a_sinks[l])
        out_b = stick_breaking_attention(heads(bq, N_HEADS_B), heads(bk, N_HEADS_B), heads(bv, N_HEADS_B))
        out_c = dilated_attention(rmsnorm(heads(cq, N_HEADS_C), c_q_gain[l]),
                                  rmsnorm(heads(ck, N_HEADS_C), c_k_gain[l]),
                                  heads(cv, N_HEADS_C), table_c)
        g = mix_out_gain[l]
        ya = rmsnorm(out_a.reshape(b_, s_, A_Q), g[:A_Q])
        yb = rmsnorm(out_b.reshape(b_, s_, B_W), g[A_Q:A_Q + B_W])
        yc = rmsnorm(out_c.reshape(b_, s_, C_W), g[A_Q + B_W:])
        mix = jnp.concatenate([ya, yb, yc], axis=-1).astype(x.dtype)
        x = x + jnp.einsum('bse,ed->bsd', mix, w_out[l])
        h = rmsnorm(x, ffn_norm[l])
        u = causal_dwconv(jnp.einsum('bsd,df->bsf', h, w_up[l]), conv_w[l], conv_b[l])
        gate, up = jnp.split(u, [D_FF], axis=-1)
        x = x + jnp.einsum('bsf,fd->bsd', jax.nn.silu(gate) * up, w_down[l])
    return x


DEPTH_2 = 2

GRID_W = 64
CTX_LEN = 256
N_MIXERS = 2
N_POOL_LAYERS = (DEPTH_2 + N_MIXERS - 1) // N_MIXERS
N_MLA_LAYERS = DEPTH_2 // N_MIXERS
POOL_WIDTH = D_MODEL
POOL_GROUPS = 4
POOL_GROUP_DIM = POOL_WIDTH // POOL_GROUPS
POOL_WINDOWS = (2, 4, 8, 16)
MLA_HEADS = 16
Q_LORA_RANK = 512
KV_LORA_RANK = 512
QK_NOPE_DIM = 128
QK_ROPE_DIM = 64
V_HEAD_DIM = 128
MLA_WIDTH = MLA_HEADS * V_HEAD_DIM
MLA_IN_WIDTH = Q_LORA_RANK + KV_LORA_RANK + QK_ROPE_DIM + MLA_WIDTH
MLA_SCALE = (QK_NOPE_DIM + QK_ROPE_DIM) ** -0.5
ROPE_BASE = 10000.0
Q_BLOCK = 128
NORM_EPS = 1e-6


def rms_norm(x, g):
    xf = x.astype(jnp.float32)
    y = xf * lax.rsqrt(jnp.mean(xf * xf, axis=-1, keepdims=True) + NORM_EPS)
    return (y * g.astype(jnp.float32)).astype(x.dtype)

def centred_multiscale_pool(u):
    L = u.shape[1]
    uf = u.astype(jnp.float32)
    cs = jnp.concatenate([jnp.zeros_like(uf[:, :1]), jnp.cumsum(uf, axis=1)], axis=1)
    win = jnp.array(POOL_WINDOWS, dtype=jnp.int32)
    left = win // 2
    right = win - 1 - left
    t = jnp.arange(L, dtype=jnp.int32)[:, None]
    hi = jnp.minimum(t + right + 1, L)
    lo = jnp.maximum(t - left, 0)
    g = jnp.arange(POOL_GROUPS, dtype=jnp.int32)[None, :]
    s = cs[:, hi, g] - cs[:, lo, g]
    mean = s / (hi - lo).astype(jnp.float32)[None, :, :, None]
    return (mean - uf).astype(u.dtype)

def pool_branch(h, w_in, w_grp, b_grp, scale, w_out):
    B, L, _ = h.shape
    u, gate = jnp.split(h @ w_in, 2, axis=-1)
    p = centred_multiscale_pool(u.reshape(B, L, POOL_GROUPS, POOL_GROUP_DIM))
    p = jnp.einsum('blgc,gcd->blgd', p, w_grp) + b_grp
    y = p.reshape(B, L, POOL_WIDTH) * scale
    return (y * jax.nn.silu(gate)) @ w_out

def axial_rope_tables(L):
    rows = L // GRID_W
    row = jnp.repeat(jnp.arange(rows, dtype=jnp.float32), GRID_W)
    col = jnp.tile(jnp.arange(GRID_W, dtype=jnp.float32), rows)
    n = QK_ROPE_DIM // 4
    freqs = ROPE_BASE ** (-jnp.arange(n, dtype=jnp.float32) / n)
    ang = jnp.stack([row[:, None] * freqs, col[:, None] * freqs], axis=1)
    return jnp.cos(ang), jnp.sin(ang)

def apply_axial_rope(x, cos, sin):
    xs = x.reshape(x.shape[:-1] + (2, 2, QK_ROPE_DIM // 4))
    x1, x2 = xs[..., 0, :], xs[..., 1, :]
    cos = cos.astype(x.dtype)
    sin = sin.astype(x.dtype)
    out = jnp.stack([x1 * cos - x2 * sin, x1 * sin + x2 * cos], axis=-2)
    return out.reshape(x.shape)

def mla_project(h, w_in, q_norm, kv_norm, w_uq, w_ukv, rope):
    B, L, _ = h.shape
    proj = h @ w_in
    c_q, c_kv, k_r, gate = jnp.split(
        proj, [Q_LORA_RANK, Q_LORA_RANK + KV_LORA_RANK, Q_LORA_RANK + KV_LORA_RANK + QK_ROPE_DIM], axis=-1)
    q = (rms_norm(c_q, q_norm) @ w_uq).reshape(B, L, MLA_HEADS, QK_NOPE_DIM + QK_ROPE_DIM)
    q_nope, q_rope = q[..., :QK_NOPE_DIM], q[..., QK_NOPE_DIM:]
    kv = (rms_norm(c_kv, kv_norm) @ w_ukv).reshape(B, L, MLA_HEADS, QK_NOPE_DIM + V_HEAD_DIM)
    k_nope, v = kv[..., :QK_NOPE_DIM], kv[..., QK_NOPE_DIM:]
    if rope is not None:
        cos, sin = rope
        q_rope = apply_axial_rope(q_rope, cos[:, None], sin[:, None])
        k_r = apply_axial_rope(k_r, cos, sin)
    return q_nope, q_rope, k_nope, k_r, v, gate

def mla_attend(q_nope, q_rope, k_nope, k_rope, v):
    s = (jnp.einsum('bqhd,bkhd->bhqk', q_nope, k_nope)
         + jnp.einsum('bqhr,bkr->bhqk', q_rope, k_rope)).astype(jnp.float32) * MLA_SCALE
    p = jax.nn.softmax(s, axis=-1).astype(v.dtype)
    return jnp.einsum('bhqk,bkhd->bqhd', p, v)

def blocked_mla_attend(q_nope, q_rope, k_nope, k_rope, v):
    B, L, H, _ = q_nope.shape
    nb = L // Q_BLOCK
    qn = q_nope.reshape(B, nb, Q_BLOCK, H, QK_NOPE_DIM).transpose(1, 0, 2, 3, 4)
    qr = q_rope.reshape(B, nb, Q_BLOCK, H, QK_ROPE_DIM).transpose(1, 0, 2, 3, 4)
    out = lax.map(lambda qb: mla_attend(qb[0], qb[1], k_nope, k_rope, v), (qn, qr))
    return out.transpose(1, 0, 2, 3, 4).reshape(B, L, H * V_HEAD_DIM)

def mla_branch(h_lat, h_ctx, w_in, q_norm, kv_norm, w_uq, w_ukv, w_out, need_ctx_out):
    L = h_lat.shape[1]
    rope = axial_rope_tables(L)
    qn_l, qr_l, kn_l, kr_l, v_l, g_l = mla_project(h_lat, w_in, q_norm, kv_norm, w_uq, w_ukv, rope)
    qn_c, qr_c, kn_c, kr_c, v_c, g_c = mla_project(h_ctx, w_in, q_norm, kv_norm, w_uq, w_ukv, None)
    kn = jnp.concatenate([kn_c, kn_l], axis=1)
    kr = jnp.concatenate([kr_c, kr_l], axis=1)
    v = jnp.concatenate([v_c, v_l], axis=1)
    o_lat = blocked_mla_attend(qn_l, qr_l, kn, kr, v)
    y_lat = (o_lat * jax.nn.silu(g_l)) @ w_out
    if not need_ctx_out:
        return y_lat, None
    B, Lc = h_ctx.shape[:2]
    o_ctx = mla_attend(qn_c, qr_c, kn_c, kr_c, v_c).reshape(B, Lc, MLA_WIDTH)
    y_ctx = (o_ctx * jax.nn.silu(g_c)) @ w_out
    return y_lat, y_ctx

def second_inputs(seed: int = 0) -> dict:
    key = jax.random.key(seed)
    ks = jax.random.split(key, 20)
    nrm = jax.random.normal
    f32 = jnp.float32
    return {
        "x": nrm(ks[0], (BATCH, SEQ, D_MODEL), f32),
        "c": nrm(ks[1], (BATCH, D_MODEL), f32),
        "ctx": nrm(ks[2], (BATCH, CTX_LEN, D_MODEL), f32),
        "c_ctx": nrm(ks[3], (D_MODEL,), f32),
        "ada_w": nrm(ks[4], (DEPTH_2, D_MODEL, 3 * D_MODEL), f32) * D_MODEL ** -0.5,
        "ada_b": nrm(ks[5], (DEPTH_2, 3 * D_MODEL), f32) * 0.01,
        "pre_norm": 1.0 + 0.1 * nrm(ks[6], (DEPTH_2, D_MODEL), f32),
        "post_norm": 1.0 + 0.1 * nrm(ks[7], (DEPTH_2, D_MODEL), f32),
        "pool_w_in": nrm(ks[8], (N_POOL_LAYERS, D_MODEL, 2 * POOL_WIDTH), f32) * D_MODEL ** -0.5,
        "pool_w_grp": nrm(ks[9], (N_POOL_LAYERS, POOL_GROUPS, POOL_GROUP_DIM, POOL_GROUP_DIM), f32) * POOL_GROUP_DIM ** -0.5,
        "pool_b_grp": nrm(ks[10], (N_POOL_LAYERS, POOL_GROUPS, POOL_GROUP_DIM), f32) * 0.01,
        "pool_scale": 1.0 + 0.1 * nrm(ks[11], (N_POOL_LAYERS, POOL_WIDTH), f32),
        "pool_w_out": nrm(ks[12], (N_POOL_LAYERS, POOL_WIDTH, D_MODEL), f32) * POOL_WIDTH ** -0.5,
        "mla_w_in": nrm(ks[13], (N_MLA_LAYERS, D_MODEL, MLA_IN_WIDTH), f32) * D_MODEL ** -0.5,
        "mla_q_norm": 1.0 + 0.1 * nrm(ks[14], (N_MLA_LAYERS, Q_LORA_RANK), f32),
        "mla_kv_norm": 1.0 + 0.1 * nrm(ks[15], (N_MLA_LAYERS, KV_LORA_RANK), f32),
        "mla_w_uq": nrm(ks[16], (N_MLA_LAYERS, Q_LORA_RANK, MLA_HEADS * (QK_NOPE_DIM + QK_ROPE_DIM)), f32) * Q_LORA_RANK ** -0.5,
        "mla_w_ukv": nrm(ks[17], (N_MLA_LAYERS, KV_LORA_RANK, MLA_HEADS * (QK_NOPE_DIM + V_HEAD_DIM)), f32) * KV_LORA_RANK ** -0.5,
        "mla_w_out": nrm(ks[18], (N_MLA_LAYERS, MLA_WIDTH, D_MODEL), f32) * MLA_WIDTH ** -0.5,
    }

def second_block(x, c, ctx, c_ctx, ada_w, ada_b, pre_norm, post_norm,
              pool_w_in, pool_w_grp, pool_b_grp, pool_scale, pool_w_out,
              mla_w_in, mla_q_norm, mla_kv_norm, mla_w_uq, mla_w_ukv, mla_w_out):
    for i in range(DEPTH_2):
        last = i == DEPTH_2 - 1
        j = i // N_MIXERS
        is_pool = (i % N_MIXERS) == 0
        need_ctx_out = not last
        need_ctx_in = need_ctx_out or not is_pool
        shift, scale, gate = jnp.split(jax.nn.silu(c) @ ada_w[i] + ada_b[i], 3, axis=-1)
        h_lat = rms_norm(x, pre_norm[i]) * (1 + scale[:, None]) + shift[:, None]
        h_ctx = None
        gate_c = None
        if need_ctx_in:
            shift_c, scale_c, gate_c = jnp.split(jax.nn.silu(c_ctx) @ ada_w[i] + ada_b[i], 3, axis=-1)
            h_ctx = rms_norm(ctx, pre_norm[i]) * (1 + scale_c) + shift_c
        if is_pool:
            y_lat = pool_branch(h_lat, pool_w_in[j], pool_w_grp[j], pool_b_grp[j], pool_scale[j], pool_w_out[j])
            y_ctx = (pool_branch(h_ctx, pool_w_in[j], pool_w_grp[j], pool_b_grp[j], pool_scale[j], pool_w_out[j])
                     if need_ctx_out else None)
        else:
            y_lat, y_ctx = mla_branch(h_lat, h_ctx, mla_w_in[j], mla_q_norm[j], mla_kv_norm[j],
                                      mla_w_uq[j], mla_w_ukv[j], mla_w_out[j], need_ctx_out)
        x = x + gate[:, None] * rms_norm(y_lat, post_norm[i])
        if need_ctx_out:
            ctx = ctx + gate_c * rms_norm(y_ctx, post_norm[i])
    return x


def setup_inputs(seed=0):
    out = dict(first_inputs(seed))
    for name, value in second_inputs(seed + 1).items():
        if name != "x":
            out[name + "_2"] = value
    return out


def reference(
    x, attn_norm, w_in, a_q_gain, a_k_gain, a_sinks, c_q_gain, c_k_gain, rel_bias_table,
    mix_out_gain, w_out, ffn_norm, w_up, conv_w, conv_b, w_down, c_2, ctx_2, c_ctx_2, ada_w_2,
    ada_b_2, pre_norm_2, post_norm_2, pool_w_in_2, pool_w_grp_2, pool_b_grp_2, pool_scale_2,
    pool_w_out_2, mla_w_in_2, mla_q_norm_2, mla_kv_norm_2, mla_w_uq_2, mla_w_ukv_2, mla_w_out_2,
):
    x = first_block(
        x, attn_norm, w_in, a_q_gain, a_k_gain, a_sinks, c_q_gain, c_k_gain, rel_bias_table,
        mix_out_gain, w_out, ffn_norm, w_up, conv_w, conv_b, w_down,
    )
    return second_block(
        x, c_2, ctx_2, c_ctx_2, ada_w_2, ada_b_2, pre_norm_2, post_norm_2, pool_w_in_2,
        pool_w_grp_2, pool_b_grp_2, pool_scale_2, pool_w_out_2, mla_w_in_2, mla_q_norm_2,
        mla_kv_norm_2, mla_w_uq_2, mla_w_ukv_2, mla_w_out_2,
    )


_drawn_inputs = setup_inputs


def setup_inputs(seed=0):
    import zlib

    import numpy as np

    out = dict(_drawn_inputs(seed))
    spreads = {}
    factors = {'a_q_gain': 6.169,
     'a_k_gain': 7.846,
     'a_sinks': 40.955,
     'c_q_gain': 4.794,
     'c_k_gain': 5.183,
     'mix_out_gain': 3.412,
     'ffn_norm': 4.783,
     'conv_b': 4.823,
     'ada_b_2': 35.284,
     'pool_b_grp_2': 64.0,
     'mla_q_norm_2': 34.713,
     'ctx_2': 2.82,
     'pre_norm_2': 5.004,
     'post_norm_2': 8.0,
     'pool_scale_2': 8.0,
     'mla_kv_norm_2': 8.0}
    for name, (base, spread) in spreads.items():
        noise = np.random.default_rng([zlib.crc32(name.encode()), seed]).standard_normal(out[name].shape)
        drawn = base * np.exp(spread * noise) if base else spread * noise
        out[name] = __import__('jax').numpy.asarray(drawn.astype(out[name].dtype))
    for name, factor in factors.items():
        out[name] = (out[name] * factor).astype(out[name].dtype)
    return out
```

```python
import math
from contextlib import ExitStack

import numpy as np

import concourse.bass as bass
from concourse import mybir

F32 = mybir.dt.float32
F32R = mybir.dt.float32r
ALU = mybir.AluOpType
ACT = mybir.ActivationFunctionType
AX_X = mybir.AxisListType.X

P = 128
KIB = 1024
D = 2048
KT = D // P
SEQ = 256
TT = SEQ // P
NT = 2 * TT
HD = 64
HEADS_A, KV_A, HEADS_B, HEADS_C = 8, 2, 8, 16
IN_W = 5376
AQ, AK, AV = 0, 512, 640
BQ, BK, BV = 768, 1280, 1792
CQ, CK, CV = 2304, 3328, 4352
D_FF = 5632
FT = D_FF // P
N_BUCKETS, T5_MAX = 32, 2048
N_TAB = HEADS_A + HEADS_C
EPS = 1e-6
NEG = -1e30
W = 512
W_IN = 448
RING = 4
CK_T = 2
CH = KT // CK_T
PAIR = 2
FREE = 1
Q_RANK, KV_RANK, NOPE, ROPE, VD, MLA_H = 512, 512, 128, 64, 128, 16
RT = Q_RANK // P
MLA_W = Q_RANK + KV_RANK + ROPE + D
QH = NOPE + ROPE
POOL_G, POOL_WINDOWS = 4, (2, 4, 8, 16)
GRID_W = 64
MLA_SCALE = (NOPE + ROPE) ** -0.5
LAT, CTX = 0, 1

C_IN = 0
C_OUT = C_IN + (IN_W // W_IN) * 2 * CH
C_UP = C_OUT + (D // W) * CH
C_ADA_LAST = C_UP + (D_FF // W) * 3 * CH
C_DOWN = C_ADA_LAST + CH
C_POOL = C_DOWN + (D // W) * (FT // CK_T)
POOL_CH = 2 * CH + RT // CK_T
C_POOL_OUT = C_POOL + POOL_G * POOL_CH
C_MLA = C_POOL_OUT + (D // W) * CH
C_HEADS = C_MLA + (MLA_W // W_IN) * CH
C_MLA_OUT = C_HEADS + (MLA_H // 2) * 4
N_CHUNKS = C_MLA_OUT + (D // W) * CH

VEC_TILES = 6
V_CONV = [(0, 0), (1, 0), (2, 0)]
V_CONV_B = (3, 0)
V_ATTN, V_FFN, V_QN, V_KVN = (0, 88), (0, 104), (0, 120), (0, 124)
V_MIX, V_PRE0 = (1, 88), (1, 104)
V_PRE1, V_POST0 = (2, 88), (2, 104)
V_POST1, V_POOL_B = (3, 88), (3, 104)
V_ADA_B, V_POOL_S = [(4, 0), (4, 48)], (4, 96)
V_GAINS = (4, 112)
V_C, V_CCTX = (5, 0), (5, 16)


def vectors(t):
    return ([(V_CONV[m], D_FF * 2 // P, t["conv_w"][0, m]) for m in range(3)]
            + [(V_CONV_B, D_FF * 2 // P, t["conv_b"][0]), (V_ATTN, KT, t["attn_norm"][0]), (V_FFN, KT, t["ffn_norm"][0]),
               (V_QN, RT, t["mla_q_norm_2"][0]), (V_KVN, RT, t["mla_kv_norm_2"][0]), (V_MIX, KT, t["mix_out_gain"][0]),
               (V_PRE0, KT, t["pre_norm_2"][0]), (V_PRE1, KT, t["pre_norm_2"][1]),
               (V_POST0, KT, t["post_norm_2"][0]), (V_POST1, KT, t["post_norm_2"][1]),
               (V_POOL_B, KT, t["pool_b_grp_2"][0].rearrange("g c -> (g c)")), (V_POOL_S, KT, t["pool_scale_2"][0]),
               (V_ADA_B[0], 3 * KT, t["ada_b_2"][0]), (V_ADA_B[1], 3 * KT, t["ada_b_2"][1]),
               (V_C, KT, t["c_2"][0]), (V_CCTX, KT, t["c_ctx_2"])])


GAINS = ["a_q_gain", "a_k_gain", "c_q_gain", "c_k_gain"]


def shape_constants():
    dist = 255 - np.arange(384)
    max_exact = N_BUCKETS // 2
    large = max_exact + (np.log(np.maximum(dist, 1).astype(np.float32) / np.float32(max_exact))
                         / np.float32(math.log(T5_MAX / max_exact)) * np.float32(N_BUCKETS - max_exact)).astype(np.int32)
    bucket = np.where(dist < max_exact, np.maximum(dist, 0), np.minimum(large, N_BUCKETS - 1))
    onehot = np.zeros((N_BUCKETS + 1, 2, 384), np.float32)
    seen_a = (dist >= 0) & (dist <= 127)
    times_c = np.where(dist >= 0, (dist <= 128).astype(int) + (dist % 4 == 0) + (dist % 16 == 0), 0)
    for n, seen in enumerate((seen_a, times_c > 0)):
        onehot[bucket[seen], n, np.nonzero(seen)[0]] = 1.0
    onehot[N_BUCKETS, 0] = np.where(seen_a, 0.0, NEG)
    onehot[N_BUCKETS, 1] = np.where(times_c > 0, np.log(np.maximum(times_c, 1)), NEG)
    i = np.arange(P)
    ident = np.concatenate([np.eye(P), -np.ones((P, P))], 1).astype(np.float32)
    before = np.where(i[:, None] < i[None, :], 0.0, NEG)
    stick = np.concatenate([before, np.zeros((P, P)), before, np.where(i[:, None] >= i[None, :], -1.0, 0.0)], 1)
    pool = np.zeros((POOL_G, SEQ, SEQ), np.float64)
    for g, win in enumerate(POOL_WINDOWS):
        left = win // 2
        right = win - 1 - left
        for t in range(SEQ):
            lo, hi = max(t - left, 0), min(t + right + 1, SEQ)
            pool[g, lo:hi, t] = 1.0 / (hi - lo)
            pool[g, t, t] -= 1.0
    pool = pool.reshape(POOL_G, TT, P, SEQ).transpose(2, 0, 1, 3)
    t = np.arange(SEQ)
    n = ROPE // 4
    freqs = np.float32(10000.0) ** (-np.arange(n, dtype=np.float32) / np.float32(n))
    ang = np.stack([(t // GRID_W).astype(np.float32)[:, None] * freqs, (t % GRID_W).astype(np.float32)[:, None] * freqs], 1)
    cos, sin = np.cos(ang), np.sin(ang)
    rope = np.stack([np.stack([cos, cos], 2), np.stack([-sin, sin], 2)], 1).reshape(TT, P, 2 * ROPE).transpose(1, 0, 2)
    pick = np.zeros((4, 2), np.float32)
    pick[0, 0] = pick[2, 0] = pick[1, 1] = pick[3, 1] = 1.0
    f = lambda a: np.ascontiguousarray(a, dtype=np.float32)
    return {"onehot": f(onehot), "ident": ident, "stick": f(stick), "pool": f(pool), "rope": f(rope), "pick": pick}


class NormSignals:

    NAMES = ("squared", "mean", "root", "scaled", "turned", "shifted", "hi_done", "lo_done")

    def __init__(self, sem):
        self.squared, self.mean, self.root, self.scaled, self.turned, self.shifted, self.hi_done, self.lo_done = (
            sem(f"norm_{name}") for name in self.NAMES)
        self.rows = self.means = self.scaled_rows = self.groups = self.shifts = 0


class Norm:

    def __init__(self, sig, src, xn, stats, hi, lo, nk, scale, shift=None, tmp=None, own_means=False):
        self.src, self.xn, self.hi, self.lo, self.nk, self.scale, self.shift, self.tmp = src, xn, hi, lo, nk, scale, shift, tmp
        self.nt = len(src)
        self.per = 4 // self.nt if self.nt <= 4 else 1
        self.groups = nk // self.per
        self.ss, self.ms, self.rstd = stats
        self.squared, self.mean, self.root, self.scaled = sig.squared, sig.mean, sig.root, sig.scaled
        self.turned, self.shifted, self.hi_done, self.lo_done = sig.turned, sig.shifted, sig.hi_done, sig.lo_done
        self.rows0, self.means0, self.scaled0, self.groups0, self.groups_shifted0 = (
            sig.rows, sig.means, sig.scaled_rows, sig.groups, sig.shifts)
        self.all_groups = self.groups0 + self.groups
        if not own_means:
            sig.rows += self.nt
            sig.means += 1
        sig.scaled_rows += self.nt
        sig.groups += self.groups
        sig.shifts += self.groups if shift else 0


def two_block_kernel(nc, t, out, consts):
    ctx = ExitStack()
    with ctx:
        sem = lambda name: ctx.enter_context(nc.semaphore(name))
        base = (nc.sbuf_base + 31) // 32 * 32
        fence_bytes = nc.sbuf_bytes_remaining - 64
        ctx.enter_context(nc.sbuf_tensor("fence", [P, fence_bytes // 4], F32))
        end = base + fence_bytes

        class Place:

            def __init__(self, at):
                self.at = at

            def __call__(self, name, shape, dtype=F32):
                size = 4
                for n in shape[1:]:
                    size *= n
                got = nc.alloc_sbuf_tensor_at(name, shape, dtype, offset=self.at)
                self.at += (size + 31) // 32 * 32
                assert self.at <= end, (name, self.at, end)
                return got

        keep = Place(base)
        raw = keep("raw", [P, RING, CK_T, W])
        hi = keep("hi", [P, RING, CK_T, W], F32R)
        lo = keep("lo", [P, RING, CK_T, W], F32R)
        xres = keep("xres", [P, TT, D])
        ident2 = keep("ident2", [P, 2 * P])
        ident, negones = ident2[:, 0:P], ident2[:, P:2 * P]
        cols = keep("cols", [P, VEC_TILES * P])
        adat = keep("adat", [P, 2, 4 + 48, 2])
        c4 = keep("c4", [P, 4 * KT + P], F32R)
        ada_rows = keep("ada_rows", [4, W])
        pick = keep("pick", [4, 2])
        ss = keep("ss", [P, 16])
        ms = keep("ms", [P, 16])
        rstd = keep("rstd", [P, 16])
        halves = keep("halves", [P, 2 * 42])
        hscale = keep("hscale", [P, 2, KT])
        region = keep.at

        def at(kib):
            return Place(region + int(kib * KIB))

        pl = at(0)
        h_hi = pl("h_hi", [P, KT, SEQ], F32R)
        h_lo = pl("h_lo", [P, KT, SEQ], F32R)
        proj = pl("proj", [P, TT, IN_W])
        bias = pl("bias", [P, N_TAB, SEQ])
        stage = pl("stage", [P, PAIR, TT, 2, HD])
        qkt = pl("qkt", [HD, PAIR, 2, SEQ])
        logits = pl("logits", [P, PAIR, 3 * P])
        probs = pl("probs", [P, PAIR, 3 * P])
        probs_t = pl("probs_t", [P, PAIR, 3 * P])
        stick = pl("stick", [P, 4 * P])
        mx = pl("mx", [P, PAIR, TT])
        nm = pl("nm", [P, PAIR, TT])
        sums = pl("sums", [P, PAIR, TT])
        esink = pl("esink", [P, PAIR, TT])
        recip = pl("recip", [P, PAIR, TT])
        sinks = pl("sinks", [P, HEADS_A])
        gqk = pl("gqk", [HD, 2])
        hss = pl("hss", [P, TT, 42])
        hrs = pl("hrs", [P, TT, 42])
        csil = pl("csil", [P, 2, KT])
        vec_rows = pl("vec_rows", [P, VEC_TILES, P])
        onehot = pl("onehot", [N_BUCKETS + 1, 2, 384])
        table = pl("table", [N_BUCKETS + 1, N_TAB])
        ext = pl("ext", [HEADS_C, 2, 384])
        squares = at(0)("squares", [P, TT, 2688])
        xn_first = at(32)("xn_first", [P, TT, D])
        xn_mix = at(74)("xn_mix", [P, TT, D])
        xn_ffn = at(32)("xn_ffn", [P, TT, D])
        pl = at(32)
        g_hi = pl("g_hi", [P, FT, SEQ], F32R)
        g_lo = pl("g_lo", [P, FT, SEQ], F32R)
        ustage = pl("ustage", [P, 2, TT, W])
        product = pl("product", [P, 4, SEQ])
        conv = [ustage[:, w, :, :].rearrange("p a (b n) -> p (a b) n", n=SEQ) for w in range(2)]
        pl = at(0)
        h4_hi = pl("h4_hi", [P, KT, NT * P], F32R)
        h4_lo = pl("h4_lo", [P, KT, NT * P], F32R)
        y = pl("y", [P, KT, NT * P])
        u = pl("u", [P, NT, W])
        pt_hi = pl("pt_hi", [P, 4, NT * P], F32R)
        pt_lo = pl("pt_lo", [P, 4, NT * P], F32R)
        poolm = pl("poolm", [P, POOL_G, TT, SEQ])
        gsilu = pl("gsilu", [P, 2, NT * P])
        xn4 = at(64)("xn4", [P, NT, D])
        ctx_in = at(96)("ctx_in", [P, TT, D])
        shift_tmp = at(128)("shift_tmp", [P, PAIR, NT * P])
        y_hi = at(0)("y_hi", [P, KT, NT * P], F32R)
        y_lo = at(32)("y_lo", [P, KT, NT * P], F32R)
        ctx_res = at(64)("ctx_res", [P, TT, D])
        gate_rows = at(80)("gate_rows", [P, 2, D])
        yout = at(96)("yout", [P, NT, D])
        pl = at(64)
        proj_l = pl("proj_l", [P, TT, MLA_W])
        proj_c = pl("proj_c", [P, TT, 2 * W_IN])
        k4_hi = at(0)("k4_hi", [P, KT, NT * P], F32R)
        k4_lo = at(32)("k4_lo", [P, KT, NT * P], F32R)
        xn4b = at(96)("xn4b", [P, NT, D])
        shift_tmpb = at(128)("shift_tmpb", [P, PAIR, NT * P])
        pl = at(96)
        cq_hi = pl("cq_hi", [P, RT, SEQ], F32R)
        cq_lo = pl("cq_lo", [P, RT, SEQ], F32R)
        ckv_hi = pl("ckv_hi", [P, RT, NT * P], F32R)
        ckv_lo = pl("ckv_lo", [P, RT, NT * P], F32R)
        rope = pl("rope", [P, TT, 2, ROPE])
        kr = pl("kr", [P, NT, P])
        krt = pl("krt", [ROPE, NT * P])
        kr_t = pl("kr_t", [P, TT, 2, 2, ROPE // 4])
        pl = at(0)
        om_hi = pl("om_hi", [P, MLA_H, SEQ], F32R)
        om_lo = pl("om_lo", [P, MLA_H, SEQ], F32R)
        q_nope = pl("q_nope", [P, TT, 2, NOPE])
        q_rope = pl("q_rope", [P, TT, 2, ROPE])
        q_swap = pl("q_swap", [P, TT, 2, ROPE])
        qn_t = pl("qn_t", [P, 2, SEQ])
        qr_t = pl("qr_t", [ROPE, 2, SEQ])
        kn_t = pl("kn_t", [P, 2, NT * P])
        v_sb = pl("v_sb", [P, NT, 2 * VD])
        mprobs = pl("mprobs", [P, 4, NT * P])
        mprobs_t = pl("mprobs_t", [P, 2, NT, P])
        om = pl("om", [P, 4, VD])
        mmx = pl("mmx", [P, 4])
        mnm = pl("mnm", [P, 4])
        msum = pl("msum", [P, 4])
        mrec = pl("mrec", [P, 4])
        assert pl.at <= region + 64 * KIB
        yout2 = at(64)("yout2", [P, TT, D])
        gate_rows2 = at(96)("gate_rows2", [P, D])

        ps = ctx.enter_context(nc.psum_tensor("ps", [P, 8, W], F32))
        bias_rows = nc.dram_tensor("bias_rows", (N_TAB, P, 3 * P), F32).ap()

        def turned_u(m):
            return ps[:, 6 + m // 2, (m % 2) * SEQ:(m % 2 + 1) * SEQ]

        def col(vec, k):
            return cols[:, vec[0] * P + vec[1] + k:vec[0] * P + vec[1] + k + 1]

        def cols_of(vec, n):
            return cols[:, vec[0] * P + vec[1]:vec[0] * P + vec[1] + n]

        raw_loaded = [sem(f"raw_loaded{s}") for s in range(RING)]
        hi_split = sem("hi_split")
        lo_split = sem("lo_split")
        chunks_used = sem("chunks_used")
        x_loaded, consts_loaded, vecs_loaded = sem("x_loaded"), sem("consts_loaded"), sem("vecs_loaded")
        vecs_cleared, vecs_turned, cols_ready = sem("vecs_cleared"), sem("vecs_turned"), sem("cols_ready")
        consts_set, table_loaded = sem("consts_set"), sem("table_loaded")
        c_silu, c_hi, c_lo = sem("c_silu"), sem("c_hi"), sem("c_lo")
        ext_done, ext_ready, bias_stored, bias_loaded = sem("ext_done"), sem("ext_ready"), sem("bias_stored"), sem("bias_loaded")
        proj_taken = sem("proj_taken")
        ada_rows_ready, ada_turned, ada_taken = sem("ada_rows_ready"), sem("ada_turned"), sem("ada_taken")
        heads_squared, heads_summed, heads_mean, heads_root, heads_scaled = (
            sem(n) for n in ("heads_squared", "heads_summed", "heads_mean", "heads_root", "heads_scaled"))
        staged = sem("staged")
        qk_turned, qk_ready, scored, logits_ready, exp_done, p_turned, pt_ready, pv_done, out_taken = (
            sem(n) for n in ("qk_turned", "qk_ready", "scored", "logits_ready", "exp_done", "p_turned", "pt_ready", "pv_done", "out_taken"))
        max_ready, negmax_ready, den_ready, recip_ready = (sem(n) for n in ("max_ready", "negmax_ready", "den_ready", "recip_ready"))
        b_abs, b_exp, b_ln, b_soft, b_summed, b_exponent = (
            sem(n) for n in ("b_abs", "b_exp", "b_ln", "b_soft", "b_summed", "b_exponent"))
        attn_added, ffn_added = sem("attn_added"), sem("ffn_added")
        u_staged = [sem("gate_staged"), sem("up_staged")]
        u_turned = [sem("gate_turned"), sem("up_turned")]
        taps = [sem("gate_taps"), sem("up_taps")]
        tap2 = [sem("gate_tap2"), sem("up_tap2")]
        gate_silu, gated, g_hi_done, g_lo_done = sem("gate_silu"), sem("gated"), sem("g_hi_done"), sem("g_lo_done")

        stats = lambda a, n: (ss[:, a:a + n], ms[:, a:a + n], rstd[:, a:a + n])
        norm_signals = NormSignals(sem)
        n_first = Norm(norm_signals, [xres[:, i, :] for i in range(TT)], xn_first, stats(0, TT), h_hi, h_lo, KT,
                       lambda k, s: col(V_ATTN, k))
        MIX = [(AQ, HEADS_A * HD, 0), (BQ, HEADS_B * HD, 512), (CQ, HEADS_C * HD, 1024)]

        def load_chunk(sp, c, slot, src, width):
            sp.wait_ge(lo_split, c + 1)
            sp.dma_start(raw[:, slot, :, 0:width], src.rearrange("(k p) n -> p k n", p=P)).then_inc(raw_loaded[slot], 16)

        def load_panel(sp, c, slot0, w, col0, width, nk=KT):
            for j in range(nk // CK_T):
                load_chunk(sp, c + j, (slot0 + j) % RING, w[j * CK_T * P:(j + 1) * CK_T * P, bass.ds(col0, width)], width)

        def split_hi(act, c, slot, turn):
            act.wait_ge(raw_loaded[slot], 16 * (turn + 1))
            act.wait_ge(chunks_used, c + 1)
            act.activation(hi[:, slot, :, :], raw[:, slot, :, :], ACT.Copy).then_inc(hi_split, 1)

        def split_lo(dve, c, slot):
            dve.wait_ge(hi_split, c + 1)
            dve.tensor_tensor(lo[:, slot, :, :], raw[:, slot, :, :], hi[:, slot, :, :].bitcast(F32),
                              ALU.subtract).then_inc(lo_split, 1)

        def his(act, first, i, step, a, b):
            for j in range(a, b):
                c = first + j
                if isinstance(i, int) and c + i * step >= N_CHUNKS:
                    continue
                split_hi(act, i * step + c, c % RING, i * (step // RING) + c // RING)

        def los(dve, first, i, step, a, b):
            for j in range(a, b):
                c = first + j
                if isinstance(i, int) and c + i * step >= N_CHUNKS:
                    continue
                split_lo(dve, i * step + c, c % RING)

        def by_tokens(pe, c, slot, a_hi, a_lo, kt0, outs, width, first, last):
            pe.wait_ge(lo_split, c + RING + 1)
            for k in range(CK_T):
                for tok, bank in outs:
                    for s, (a, w) in enumerate(((a_hi, hi), (a_hi, lo), (a_lo, hi))):
                        mm = pe.matmul(ps[:, bank, 0:width], a[:, kt0 + k, tok * P:(tok + 1) * P], w[:, slot, k, 0:width],
                                       start=first and k == 0 and s == 0, stop=last and k == CK_T - 1 and s == 2)
            mm.then_inc(chunks_used, 1)

        def by_channels(pe, c, slot, a_hi, a_lo, kt0, bank0, first, last):
            pe.wait_ge(lo_split, c + RING + 1)
            for k in range(CK_T):
                for n in range(W // P):
                    for s, (w, a) in enumerate(((hi, a_hi), (hi, a_lo), (lo, a_hi))):
                        mm = pe.matmul(ps[:, bank0 + n, :], w[:, slot, k, n * P:(n + 1) * P], a[:, kt0 + k, :],
                                       start=first and k == 0 and s == 0, stop=last and k == CK_T - 1 and s == 2)
            mm.then_inc(chunks_used, 1)

        def panel_by_tokens(pe, c, slot0, a_hi, a_lo, outs, width, nk=KT, after=None):
            n = nk // CK_T
            for j in range(n):
                by_tokens(pe, c + j, (slot0 + j) % RING, a_hi, a_lo, CK_T * j, outs, width, j == 0, j == n - 1)
                if after is not None and j == 1:
                    after()

        def pair(half):
            return [(i, PAIR * half + i) for i in range(TT)]

        def used(n):
            return RING + n

        def norm_squares(act, n, wait):
            for i in range(n.nt):
                wait(act, i)
                if i:
                    act.wait_ge(n.squared, n.rows0 + i)
                w = P * n.nk
                act.activation(ps[:, 4:4 + (w + W - 1) // W, :].rearrange("p a b -> p (a b)")[:, 0:w], n.src[i], ACT.Square,
                               accum_out=n.ss[:, i:i + 1]).then_inc(n.squared, 1)

        def norm_mean(dve, n):
            dve.wait_ge(n.squared, n.rows0 + n.nt)
            dve.tensor_scalar(n.ms, n.ss, 1.0 / (P * n.nk), EPS, ALU.mult, ALU.add).then_inc(n.mean, 1)

        def norm_root(pool, n):
            pool.wait_ge(n.mean, n.means0 + 1)
            pool.tensor_tensor(n.rstd, n.ms, halves[:, 0:n.nt], ALU.pow).then_inc(n.root, 1)

        def norm_apply(dve, n):
            dve.wait_ge(n.root, n.means0 + 1)
            for i in range(n.nt):
                dve.tensor_scalar(n.xn(i) if callable(n.xn) else n.xn[:, i, :], n.src[i], n.rstd[:, i:i + 1], None,
                                  ALU.mult).then_inc(n.scaled, 1)

        TURN_BANKS = 4

        def norm_turn(pe, n):
            for g in range(n.groups):
                if g >= TURN_BANKS:
                    pe.wait_ge(n.lo_done, n.groups0 + g - TURN_BANKS + 1)
                for m in range(n.per):
                    for i in range(n.nt):
                        if g == 0 and m == 0:
                            pe.wait_ge(n.scaled, n.scaled0 + i + 1)
                        src = n.xn(i) if callable(n.xn) else n.xn[:, i, :]
                        k = g * n.per + m
                        mm = pe.transpose(ps[:, 4 + g % TURN_BANKS, (m * n.nt + i) * P:(m * n.nt + i + 1) * P],
                                          src[:, k * P:(k + 1) * P], ident)
                mm.then_inc(n.turned, 1)

        def norm_parts(n, g):
            w = n.nt * P
            for m in range(n.per):
                yield g * n.per + m, ps[:, 4 + g % TURN_BANKS, m * w:(m + 1) * w]

        def norm_hi(act, n):
            for g in range(n.groups):
                if n.shift:
                    act.wait_ge(n.shifted, n.groups_shifted0 + g + 1)
                    act.activation(n.hi[:, g, :], n.tmp[:, g % 2, :], ACT.Copy).then_inc(n.hi_done, 1)
                else:
                    act.wait_ge(n.turned, n.groups0 + g + 1)
                    for k, src in norm_parts(n, g):
                        ins = act.activation(n.hi[:, k, :], src, ACT.Identity, scale=n.scale(k, 0))
                    ins.then_inc(n.hi_done, 1)

        def norm_lo(dve, n):
            for g in range(n.groups):
                dve.wait_ge(n.turned, n.groups0 + g + 1)
                dve.wait_ge(n.hi_done, n.groups0 + g + 1)
                for k, src in norm_parts(n, g):
                    ins = dve.scalar_tensor_tensor(n.lo[:, k, :], src, n.scale(k, 0), n.hi[:, k, :].bitcast(F32),
                                                   ALU.mult, ALU.subtract)
                ins.then_inc(n.lo_done, 1)

        def norm_shift_lo(dve, n):
            def shift(g):
                dve.wait_ge(n.turned, n.groups0 + g + 1)
                if g >= PAIR:
                    dve.wait_ge(n.lo_done, n.groups0 + g - PAIR + 1)
                for s in range(n.nt // TT):
                    sl = slice(s * SEQ, (s + 1) * SEQ)
                    ins = dve.tensor_scalar(n.tmp[:, g % 2, sl], ps[:, 4 + g % TURN_BANKS, sl], n.scale(g, s), n.shift(g, s),
                                            ALU.mult, ALU.add)
                ins.then_inc(n.shifted, 1)

            shift(0)
            for g in range(n.groups):
                if g + 1 < n.groups:
                    shift(g + 1)
                dve.wait_ge(n.hi_done, n.groups0 + g + 1)
                dve.wait_ge(n.shifted, n.groups_shifted0 + g + 1)
                dve.tensor_tensor(n.lo[:, g, :], n.tmp[:, g % 2, :], n.hi[:, g, :].bitcast(F32), ALU.subtract).then_inc(n.lo_done, 1)

        m_squared, m_mean, m_root = sem("mix_groups_squared"), sem("mix_groups_mean"), sem("mix_groups_root")
        n_mix = Norm(norm_signals, [xn_mix[:, i, :] for i in range(TT)], xn_mix, stats(2, 6), h_hi, h_lo, KT,
                     lambda k, s: col(V_MIX, k), own_means=True)
        n_ffn = Norm(norm_signals, [xres[:, i, :] for i in range(TT)], xn_ffn, stats(8, TT), h_hi, h_lo, KT,
                     lambda k, s: col(V_FFN, k))

        HEAD_SETS = [
            (0, HEADS_A // 4, AQ, AK, HD, 0, AV, HD, 0),
            (HEADS_A, HEADS_C // 4, CQ, CK, 4 * HD, HD, CV, 4 * HD, HD),
            (HEADS_A + HEADS_C, HEADS_B // 4, BQ, BK, 4 * HD, HD, BV, 4 * HD, HD),
        ]
        N_SOFT = HEADS_A + HEADS_C

        ctx_loaded, poolm_loaded, ctx_again, rope_loaded = (
            sem(n) for n in ("ctx_loaded", "poolm_loaded", "ctx_again", "rope_loaded"))
        ada_biased, scales_ready, gains_ready = sem("ada_biased"), sem("scales_ready"), sem("gains_ready")
        u_ready, pooled, pt_hi_done, pt_lo_done, grouped, gate_silu4, y_gated = (
            sem(n) for n in ("u_ready", "pooled", "pt_hi_done", "pt_lo_done", "grouped", "gate_silu4", "y_gated"))
        y_hi_done, y_lo_done = sem("y_hi_done"), sem("y_lo_done")
        yout_taken = [sem("yout_taken"), sem("yout2_taken")]
        diag_ready = [sem("diag_ready"), sem("diag2_ready")]
        rows_spread = [sem("rows_spread"), sem("rows2_spread")]
        gate_rows_ready = [sem("gate_rows_ready"), sem("gate_rows2_ready")]
        yout_squared, yout_mean, yout_root, yout_scaled, yout_added = (
            [sem(f"{n}{m}") for m in range(2)] for n in ("yout_squared", "yout_mean", "yout_root", "yout_scaled", "yout_added"))
        mla_taken, mla_ctx_taken = sem("mla_taken"), sem("mla_ctx_taken")
        gate_silu5 = sem("gate_silu5")
        kr_cleared, kr_swapped, kr_staged, kr_turned, kr_ready = (
            sem(n) for n in ("kr_cleared", "kr_swapped", "kr_staged", "kr_turned", "kr_ready"))
        q_nope_ready, q_swapped, q_cos, q_rope_ready, kn_ready, v_ready = (
            sem(n) for n in ("q_nope_ready", "q_swapped", "q_cos", "q_rope_ready", "kn_ready", "v_ready"))
        q_turned, qt_ready, mscored, mmax_ready, mneg_ready, mexp_done, mrec_ready = (
            sem(n) for n in ("q_turned", "qt_ready", "mscored", "mmax_ready", "mneg_ready", "mexp_done", "mrec_ready"))
        mp_turned, mpt_ready, mout_done, om_ready, om_turned, om_hi_done, om_lo_done = (
            sem(n) for n in ("mp_turned", "mpt_ready", "mout_done", "om_ready", "om_turned", "om_hi_done", "om_lo_done"))
        out_stored = sem("out_stored")

        def modulated(layer, ctx_tile, xn, k_hi, k_lo, tmp):
            return Norm(norm_signals, [xres[:, i, :] for i in range(TT)] + [ctx_tile[:, i, :] for i in range(TT)], xn, stats(0, NT),
                        k_hi, k_lo, KT, lambda k, s: hscale[:, s, k:k + 1], lambda k, s: adat[:, layer, 4 + k, s:s + 1], tmp)

        n_pool = modulated(0, ctx_in, xn4, h4_hi, h4_lo, shift_tmp)
        n_mla = modulated(1, ctx_res, xn4b, k4_hi, k4_lo, shift_tmpb)
        KVC = Q_RANK + KV_RANK - W_IN
        cq_rows = [proj_l[:, i, 0:Q_RANK] for i in range(TT)]
        ckv_rows = ([proj_l[:, i, Q_RANK:Q_RANK + KV_RANK] for i in range(TT)]
                    + [proj_c[:, i, Q_RANK - W_IN:KVC] for i in range(TT)])
        n_cq = Norm(norm_signals, cq_rows, lambda i: cq_rows[i], stats(4, TT), cq_hi, cq_lo, RT, lambda k, s: col(V_QN, k))
        n_ckv = Norm(norm_signals, ckv_rows, lambda i: ckv_rows[i], stats(8, NT), ckv_hi, ckv_lo, RT, lambda k, s: col(V_KVN, k))
        YOUT = [[yout[:, i, :] for i in range(NT)], [yout2[:, i, :] for i in range(TT)]]
        SPREAD = [[gate_rows[:, s, :] for s in range(2)], [gate_rows2[:, :]]]
        y_stats = [stats(0, NT), stats(4, TT)]
        GATE0 = Q_RANK + KV_RANK + ROPE

        VECS = vectors(t)
        block = ctx.enter_context(nc.Block())

        @block.sync
        def _(sp):
            sp.dma_start(xres[:, :, :], t["x"][0].rearrange("(t p) d -> p t d", p=P)).then_inc(x_loaded, 16)
            w_in, ada0, ada1 = t["w_in"][0], t["ada_w_2"][0], t["ada_w_2"][1]

            def first_panel(i):
                load_panel(sp, C_IN + i * 2 * CH, 0, ada0, i * W, W)
                load_panel(sp, C_IN + i * 2 * CH + CH, 0, w_in, i * W_IN, W_IN)

            first_panel(0)
            first_panel(1)
            sp.wait_ge(bias_stored, 2 * 16)
            sp.dma_start(bias[:, :, :], bass.AP(bias_rows.tensor, P - 1, [[3 * P - 1, P], [3 * P * P, N_TAB], [1, SEQ]]))\
              .then_inc(bias_loaded, 16)
            with sp.Fori(2, IN_W // W_IN) as i:
                first_panel(i)
            with sp.Fori(0, D // W) as i:
                load_panel(sp, C_OUT + i * CH, 0, t["w_out"][0], i * W, W)
            with sp.Fori(0, D_FF // W) as i:
                c = C_UP + i * 3 * CH
                load_panel(sp, c, 0, t["w_up"][0], i * W, W)
                load_panel(sp, c + CH, 0, t["w_up"][0], i * W + D_FF, W)
                load_panel(sp, c + 2 * CH, 0, ada1, i * W, W)
            load_panel(sp, C_ADA_LAST, 0, ada1, D_FF, W)
            n = FT // CK_T
            with sp.Fori(0, D // W // 2) as i:
                for e in range(2):
                    load_panel(sp, C_DOWN + i * 2 * n + e * n, e * n, t["w_down"][0], i * 2 * W + e * W, W, D_FF // P)
            with sp.Fori(0, POOL_G // 2) as i:
                for e in range(2):
                    c, s0 = i * 2 * POOL_CH + C_POOL + e * POOL_CH, e * POOL_CH
                    w, col0 = t["pool_w_in_2"][0], i * 2 * W + e * W
                    load_panel(sp, c, s0, w, col0, W)
                    for j in range(POOL_CH - CH):
                        m = CH + j
                        if j in (4, 5):
                            src = t["pool_w_grp_2"][0, bass.ds(i * 2 + e, 1), (j - 4) * CK_T * P:(j - 3) * CK_T * P, :]\
                                .rearrange("g c d -> (g c) d")
                        else:
                            r = j if j < 4 else j - 2
                            src = w[r * CK_T * P:(r + 1) * CK_T * P, bass.ds(col0 + D, W)]
                        load_chunk(sp, c + m, (s0 + m) % RING, src, W)
            with sp.Fori(0, D // W) as i:
                load_panel(sp, i * CH + C_POOL_OUT, 0, t["pool_w_out_2"][0], i * W, W)
            with sp.Fori(0, MLA_W // W_IN) as i:
                load_panel(sp, i * CH + C_MLA, 0, t["mla_w_in_2"][0], i * W_IN, W_IN)
            with sp.Fori(0, MLA_H // 2) as i:
                load_panel(sp, i * 4 + C_HEADS, 0, t["mla_w_uq_2"][0], i * 2 * QH, 2 * QH, RT)
                load_panel(sp, i * 4 + C_HEADS + 2, 2, t["mla_w_ukv_2"][0], i * W, W, RT)
            with sp.Fori(0, D // W) as i:
                load_panel(sp, i * CH + C_MLA_OUT, 0, t["mla_w_out_2"][0], i * W, W)
            sp.wait_ge(yout_added[1], TT)
            sp.dma_start(out[0].rearrange("(t p) d -> p t d", p=P), xres[:, :, :]).then_inc(out_stored, 16)
            sp.wait_ge(out_stored, 16)

        @block.gpsimd
        def _(pool):
            pool.memset(vec_rows[:, :, :], 0.0).then_inc(vecs_cleared, 1)
            pool.wait_ge(consts_set, 3)
            norm_root(pool, n_first)
            pool.wait_ge(heads_mean, 1)
            pool.tensor_tensor(hrs[:, :, :].rearrange("p a b -> p (a b)"), hss[:, :, :].rearrange("p a b -> p (a b)"),
                               halves[:, :], ALU.pow).then_inc(heads_root, 1)
            pool.wait_ge(heads_scaled, 4)

            def stage_head(n, slot, q0, k0):
                pool.wait_ge(qk_turned, n + 1)
                for m, c0 in enumerate((q0, k0)):
                    pool.tensor_copy(stage[:, slot, :, m, :], proj[:, :, bass.ds(c0, HD)]).then_inc(staged, 1)

            for n0, iters, q0, k0, kstep, kj, v0, vstep, vj in HEAD_SETS:
                with pool.Fori(0, iters) as i:
                    for j in range(4):
                        stage_head(i * 4 + n0 + j, j % PAIR, i * 4 * HD + q0 + j * HD, i * kstep + k0 + j * kj)
            pool.wait_ge(m_mean, 1)
            pool.tensor_tensor(n_mix.rstd, n_mix.ms, halves[:, 0:6], ALU.pow).then_inc(m_root, 1)
            norm_root(pool, n_ffn)
            norm_root(pool, n_pool)

            def yout_roots(m):
                pool.wait_ge(yout_mean[m], 1)
                _, mean, root = y_stats[m]
                pool.tensor_tensor(root, mean, halves[:, 0:len(YOUT[m])], ALU.pow).then_inc(yout_root[m], 1)

            yout_roots(0)
            norm_root(pool, n_mla)
            norm_root(pool, n_cq)
            norm_root(pool, n_ckv)
            yout_roots(1)

        @block.scalar
        def _(act):
            for dst, src in ((ident2, "ident"), (stick, "stick"), (onehot, "onehot"), (pick, "pick")):
                act.dma_start(dst[:], consts[src]).then_inc(consts_loaded, 16)
            act.dma_start(table[0:N_BUCKETS, :], t["rel_bias_table"]).then_inc(table_loaded, 16)
            act.dma_start(sinks[:, :], bass.AP(t["a_sinks"].tensor, 0, [[0, P], [1, HEADS_A]])).then_inc(table_loaded, 16)
            act.wait_ge(vecs_cleared, 1)
            for (tile, row), n, src in VECS:
                act.dma_start(vec_rows[row:row + n, tile, :], src.rearrange("(r p) -> r p", p=P)).then_inc(vecs_loaded, 16)
            for m, name in enumerate(GAINS):
                r = V_GAINS[1] + m
                act.dma_start(vec_rows[r:r + 1, V_GAINS[0], 0:HD], t[name]).then_inc(vecs_loaded, 16)
            act.sem_inc(proj_taken, PAIR)
            act.sem_inc(qk_ready, PAIR)
            act.sem_inc(exp_done, PAIR)
            for s in (u_staged[0], u_staged[1], g_hi_done):
                act.sem_inc(s, FREE)
            norm_squares(act, n_first, lambda e, i: e.wait_ge(x_loaded, 16))
            act.wait_ge(cols_ready, 3)
            act.activation(csil[:, :, :].rearrange("p a b -> p (a b)"), cols_of(V_C, 2 * KT), ACT.Silu).then_inc(c_silu, 1)
            act.wait_ge(c_silu, 1)
            act.activation(c4[:, 0:4 * KT].rearrange("p (k v) -> p v k", v=4)[:, 0:2, :], csil[:, :, :], ACT.Copy).then_inc(c_hi, 1)
            his(act, C_IN, 0, 2 * CH, 0, RING)
            act.wait_ge(ext_ready, 2)
            for to, e, n in ((0, 0, HEADS_A), (HEADS_A, 1, HEADS_C)):
                act.dma_start(bias_rows[to:to + n, :, :], ext[0:n, e, :].unsqueeze(1).to_broadcast([n, P, 3 * P]))\
                   .then_inc(bias_stored, 16)
            norm_hi(act, n_first)

            def take_proj(i, half):
                act.wait_ge(chunks_used, i * 4 * CH + used(C_IN + (half + 1) * 2 * CH))
                act.activation(proj[:, :, bass.ds(i * 2 * W_IN + half * W_IN, W_IN)], ps[:, 2 * half:2 * half + 2, 0:W_IN],
                               ACT.Copy).then_inc(proj_taken, 1)

            with act.Fori(0, IN_W // W_IN // 2) as i:
                for half in range(2):
                    his(act, C_IN + half * 2 * CH, i, 4 * CH, RING, RING + 2 * CH)
                    take_proj(i, half)
            act.wait_ge(proj_taken, PAIR + IN_W // W_IN)
            for i in range(TT):
                act.activation(squares[:, i, 0:640], proj[:, i, AQ:AQ + 640], ACT.Square).then_inc(heads_squared, 1)
                act.activation(squares[:, i, 640:2688], proj[:, i, CQ:CQ + 2048], ACT.Square).then_inc(heads_squared, 1)

            def head_ready(n, slot, soft):
                act.wait_ge(qk_turned, n + PAIR + 1)
                act.wait_ge(scored, n + 1)
                act.activation(qkt[:, slot, 0, :], ps[0:HD, slot, 0:SEQ], ACT.Identity,
                               scale=gqk[:, soft:soft + 1] if soft is not None else HD ** -0.5)
                act.activation(qkt[:, slot, 1, :], ps[HD:2 * HD, slot, 0:SEQ], ACT.Identity).then_inc(qk_ready, 1)

            def soft_exp(n, slot, sink):
                act.wait_ge(negmax_ready, n + 1)
                act.wait_ge(p_turned, n + 1)
                for i, sl in enumerate((slice(0, P), slice(P, 3 * P))):
                    ins = act.activation(probs[:, slot, sl], logits[:, slot, sl], ACT.Exp, bias=nm[:, slot, i:i + 1],
                                         accum_out=sums[:, slot, i:i + 1])
                    if sink is not None:
                        ins = act.activation(esink[:, slot, i:i + 1], sink, ACT.Exp, bias=nm[:, slot, i:i + 1])
                ins.then_inc(exp_done, 1)

            def stick_logs(m, slot):
                act.wait_ge(logits_ready, m + N_SOFT + PAIR + 1)
                act.wait_ge(b_summed, m + 1)
                act.activation(probs[:, slot, :], logits[:, slot, :], ACT.Abs).then_inc(b_abs, 1)
                act.wait_ge(b_abs, m + 1)
                act.activation(probs[:, slot, :], probs[:, slot, :], ACT.Exp, scale=-1.0).then_inc(b_exp, 1)
                act.wait_ge(b_exp, m + 1)
                act.activation(probs[:, slot, :], probs[:, slot, :], ACT.Ln, bias=1.0).then_inc(b_ln, 1)

            def stick_weights(m, slot):
                act.wait_ge(b_exponent, m + PAIR + 1)
                act.wait_ge(pv_done, m + N_SOFT + 1)
                act.activation(probs_t[:, slot, :], logits[:, slot, :], ACT.Exp).then_inc(pt_ready, 1)

            act.wait_ge(cols_ready, 4)
            for s, (n0, iters, *_) in enumerate(HEAD_SETS):
                with act.Fori(0, iters) as i:
                    n = i * 4 + n0
                    head_ready(n, 0, s if s < 2 else None)
                    for j in range(4):
                        if j < 3:
                            head_ready(n + j + 1, (j + 1) % PAIR, s if s < 2 else None)
                        if s < 2:
                            soft_exp(n + j, j % PAIR, sinks[:, bass.ds(i * 4 + j, 1)] if s == 0 else None)
                        else:
                            stick_logs(i * 4 + j, j % PAIR)
                            stick_weights(i * 4 + j, j % PAIR)
            act.wait_ge(out_taken, PAIR + HEADS_A + HEADS_B + HEADS_C)
            for i in range(TT):
                for g, (c0, w, _) in enumerate(MIX):
                    if i + g:
                        act.wait_ge(m_squared, 3 * i + g)
                    act.activation(ps[:, 0:2, :].rearrange("p a b -> p (a b)")[:, 0:w], proj[:, i, c0:c0 + w], ACT.Square,
                                   accum_out=n_mix.ss[:, 3 * i + g:3 * i + g + 1]).then_inc(m_squared, 1)
            norm_hi(act, n_mix)
            with act.Fori(0, D // W // 2) as i:
                his(act, C_OUT, i, 2 * CH, RING, RING + 2 * CH)
            norm_squares(act, n_ffn, lambda e, i: e.wait_ge(attn_added, PAIR + D // W))
            norm_hi(act, n_ffn)

            def stage_u(i, which, c):
                act.wait_ge(chunks_used, i * 3 * CH + used(c))
                act.wait_ge(gated, FREE + i)
                act.activation(ustage[:, which, :, :], ps[:, 2 * which:2 * which + 2, :], ACT.Copy).then_inc(u_staged[which], 1)

            def tap_two(i, which):
                act.wait_ge(u_turned[which], i + 1)
                for m in range(4):
                    ch = i * 4 + which * FT + m
                    ins = act.activation(conv[which][:, m, :], turned_u(m), ACT.Identity,
                                         scale=cols[:, bass.ds(ch + V_CONV[2][0] * P + V_CONV[2][1], 1)],
                                         bias=cols[:, bass.ds(ch + V_CONV_B[0] * P + V_CONV_B[1], 1)])
                ins.then_inc(tap2[which], 1)

            with act.Fori(0, D_FF // W) as i:
                his(act, C_UP, i, 3 * CH, RING, CH + RING)
                stage_u(i, 0, C_UP + CH)
                his(act, C_UP, i, 3 * CH, CH + RING, CH + RING + 2)
                tap_two(i, 0)
                his(act, C_UP, i, 3 * CH, CH + RING + 2, 2 * CH + RING)
                act.wait_ge(taps[0], FREE + i * 2 + 2)
                act.activation(conv[0], conv[0], ACT.Silu).then_inc(gate_silu, 1)
                stage_u(i, 1, C_UP + 2 * CH)
                his(act, C_UP, i, 3 * CH, 2 * CH + RING, 2 * CH + RING + 2)
                tap_two(i, 1)
                his(act, C_UP, i, 3 * CH, 2 * CH + RING + 2, 3 * CH + RING)
                act.wait_ge(gated, FREE + i + 1)
                act.activation(g_hi[:, bass.ds(i * 4, 4), :], product[:, :, :], ACT.Copy).then_inc(g_hi_done, 1)
            his(act, C_ADA_LAST, 0, CH, RING, RING + CH)
            n = FT // CK_T
            with act.Fori(0, D // W // 2) as i:
                his(act, C_DOWN, i, 2 * n, RING, RING + 2 * n)
            act.wait_ge(ffn_added, PAIR + D // W)
            act.dma_start(ctx_in[:, :, :], t["ctx_2"][0].rearrange("(t p) d -> p t d", p=P)).then_inc(ctx_loaded, 16)
            act.dma_start(poolm[:, :, :, :], consts["pool"]).then_inc(poolm_loaded, 16)
            act.wait_ge(scales_ready, 2)
            norm_squares(act, n_pool, lambda e, i: e.wait_ge(ctx_loaded, 16) if i >= TT else None)
            norm_hi(act, n_pool)

            def pool_group(i, e):
                first = C_POOL + e * POOL_CH
                step, n = 2 * POOL_CH, i * 2 + e
                c = i * step + first
                his(act, first, i, step, RING, CH + RING)
                act.wait_ge(chunks_used, c + RING + CH)
                act.activation(u[:, :, :], ps[:, 0:4, :], ACT.Copy).then_inc(u_ready, 1)
                his(act, first, i, step, CH + RING, CH + RING + 2)
                act.wait_ge(pt_lo_done, FREE + n)
                for m in range(4):
                    act.wait_ge(pooled, n * 4 + m + 1)
                    act.activation(pt_hi[:, m, :], ps[:, m, :], ACT.Copy).then_inc(pt_hi_done, 1)
                his(act, first, i, step, CH + RING + 2, POOL_CH + RING)
                act.wait_ge(chunks_used, c + RING + POOL_CH)
                for m in range(4):
                    act.wait_ge(y_gated, FREE + n * 4 + m - 1) if m >= 1 else act.wait_ge(y_gated, FREE + n * 4)
                    act.activation(gsilu[:, m % 2, :], ps[:, 4 + m, :], ACT.Silu).then_inc(gate_silu4, 1)

            with act.Fori(0, POOL_G // 2) as i:
                for e in range(2):
                    pool_group(i, e)
            for k in range(KT):
                act.wait_ge(y_gated, FREE + k + 1)
                act.activation(y_hi[:, k, :], y[:, k, :], ACT.Copy).then_inc(y_hi_done, 1)
            act.wait_ge(y_lo_done, KT)
            act.dma_start(ctx_res[:, :, :], t["ctx_2"][0].rearrange("(t p) d -> p t d", p=P)).then_inc(ctx_again, 16)
            act.sem_inc(yout_taken[0], PAIR)
            act.sem_inc(yout_taken[1], PAIR)
            with act.Fori(0, D // W // 2) as i:
                for half in range(2):
                    his(act, C_POOL_OUT + half * CH, i, 2 * CH, RING, RING + CH)
                    act.wait_ge(chunks_used, i * 2 * CH + used(C_POOL_OUT + (half + 1) * CH))
                    act.activation(yout[:, :, bass.ds(i * 2 * W + half * W, W)], ps[:, 4 * half:4 * half + 4, :], ACT.Copy)\
                       .then_inc(yout_taken[0], 1)

            def yout_squares(m):
                act.wait_ge(yout_taken[m], PAIR + D // W)
                for i, v in enumerate(YOUT[m]):
                    if i:
                        act.wait_ge(yout_squared[m], i)
                    act.activation(ps[:, 4:8, :].rearrange("p a b -> p (a b)"), v, ACT.Square,
                                   accum_out=y_stats[m][0][:, i:i + 1]).then_inc(yout_squared[m], 1)
                for s, v in enumerate(SPREAD[m]):
                    act.wait_ge(rows_spread[m], s + 1)
                    act.activation(v, ps[:, 0:4, :].rearrange("p a b -> p (a b)"), ACT.Copy).then_inc(gate_rows_ready[m], 1)

            yout_squares(0)
            act.wait_ge(scales_ready, 4)
            act.wait_ge(yout_added[0], NT)
            norm_squares(act, n_mla, lambda e, i: None)
            norm_hi(act, n_mla)
            act.dma_start(rope[:, :, :, :].rearrange("p t a e -> p t (a e)"), consts["rope"]).then_inc(rope_loaded, 16)

            def take_mla(n, first, half, i=0, step=0):
                act.wait_ge(chunks_used, i * step + used(C_MLA + (first + 1) * CH))
                act.activation(proj_l[:, :, bass.ds(n * W_IN, W_IN)], ps[:, 2 * half:2 * half + 2, 0:W_IN], ACT.Copy)\
                   .then_inc(mla_taken, 1)

            act.sem_inc(mla_taken, PAIR)
            for n in range(3):
                his(act, C_MLA + n * CH, 0, 0, RING, RING + CH)
                take_mla(n, n, n % 2)
            with act.Fori(0, 2) as i:
                for e in range(2):
                    his(act, C_MLA + (3 + e) * CH, i, 2 * CH, RING, RING + CH)
                    take_mla(i * 2 + 3 + e, 3 + e, (3 + e) % 2, i, 2 * CH)
            norm_squares(act, n_cq, lambda e, i: e.wait_ge(mla_ctx_taken, 2))
            act.wait_ge(n_cq.squared, n_cq.rows0 + TT)
            norm_squares(act, n_ckv, lambda e, i: None)
            norm_hi(act, n_cq)
            norm_hi(act, n_ckv)
            for i in range(TT):
                act.activation(proj_l[:, i, GATE0:], proj_l[:, i, GATE0:], ACT.Silu).then_inc(gate_silu5, 1)
            act.wait_ge(kr_turned, 1)
            act.activation(krt[:, :], ps[0:ROPE, 0, :], ACT.Copy).then_inc(kr_ready, 1)
            with act.Fori(0, MLA_H // 2) as i:
                his(act, C_HEADS, i, 4, RING, RING + 2)
                act.activation(q_nope[:, :, :, :], ps[:, 0:2, 0:2 * QH].rearrange("p t (h e) -> p t h e", h=2)[:, :, :, 0:NOPE],
                               ACT.Copy).then_inc(q_nope_ready, 1)
                his(act, C_HEADS, i, 4, RING + 2, RING + 4)
                act.activation(kn_t[:, :, :], ps[:, 2:4, :], ACT.Copy).then_inc(kn_ready, 1)
                act.wait_ge(q_turned, i + 1)
                act.activation(qn_t[:, :, :].rearrange("p a b -> p (a b)"), ps[:, 6, :], ACT.Copy)
                act.activation(qr_t[:, 0, :], ps[0:ROPE, 7, 0:SEQ], ACT.Copy)
                act.activation(qr_t[:, 1, :], ps[ROPE:2 * ROPE, 7, 0:SEQ], ACT.Copy).then_inc(qt_ready, 1)
                for m in range(4):
                    act.wait_ge(mneg_ready, i * 4 + m + 1)
                    act.activation(mprobs[:, m, :], ps[:, 2 + m, :], ACT.Exp, scale=MLA_SCALE, bias=mnm[:, m:m + 1],
                                   accum_out=msum[:, m:m + 1]).then_inc(mexp_done, 1)
                act.wait_ge(om_turned, i + 1)
                act.activation(om_hi[:, bass.ds(i * 2, 2), :].rearrange("p a b -> p (a b)"), ps[:, 1, :], ACT.Copy)\
                   .then_inc(om_hi_done, 1)
            for n in range(D // W):
                his(act, C_MLA_OUT + n * CH, 0, 0, RING, RING + CH)
                act.wait_ge(chunks_used, used(C_MLA_OUT + (n + 1) * CH))
                act.activation(yout2[:, :, n * W:(n + 1) * W], ps[:, 2 * (n % 2):2 * (n % 2) + 2, :], ACT.Copy)\
                   .then_inc(yout_taken[1], 1)
            yout_squares(1)

        @block.vector
        def _(dve):
            dve.sem_inc(lo_split, RING)
            for s in (logits_ready, pt_ready, out_taken, b_exponent, attn_added, ffn_added):
                dve.sem_inc(s, PAIR)
            for s in (ada_rows_ready, ada_taken, taps[0], taps[1], gated, pt_lo_done, grouped, y_gated, mpt_ready, om_lo_done):
                dve.sem_inc(s, FREE)
            dve.memset(halves[:, :], -0.5).then_inc(consts_set, 1)
            dve.memset(table[N_BUCKETS:N_BUCKETS + 1, :], 1.0).then_inc(consts_set, 1)
            dve.memset(c4[:, 4 * KT:].bitcast(F32), 0.0).then_inc(consts_set, 1)
            dve.wait_ge(vecs_turned, 1)
            dve.tensor_copy(cols[:, 4 * P:6 * P], ps[:, 1, 0:2 * P]).then_inc(cols_ready, 2)
            dve.tensor_copy(cols[:, 0:4 * P], ps[:, 0, :]).then_inc(cols_ready, 1)
            dve.wait_ge(cols_ready, 3)
            for m in range(2):
                g0 = V_GAINS[0] * P + V_GAINS[1] + 2 * m
                ins = dve.tensor_tensor(gqk[:, m:m + 1], cols[0:HD, g0:g0 + 1], cols[0:HD, g0 + 1:g0 + 2], ALU.mult)
            ins.then_inc(cols_ready, 1)
            dve.wait_ge(ext_done, 1)
            dve.tensor_copy(ext[0:HEADS_A, 0, :], ps[0:HEADS_A, 2, 0:384]).then_inc(ext_ready, 1)
            dve.tensor_copy(ext[:, 1, :], ps[0:HEADS_C, 3, 0:384]).then_inc(ext_ready, 1)
            norm_mean(dve, n_first)
            norm_apply(dve, n_first)
            dve.wait_ge(c_hi, 1)
            for v in range(2):
                ck = c4[:, 0:4 * KT].rearrange("p (k v) -> p v k", v=4)
                ins = dve.tensor_tensor(ck[:, 2 + v, :], csil[:, v, :], ck[:, v, :].bitcast(F32), ALU.subtract)
            ins.then_inc(c_lo, 1)
            los(dve, C_IN, 0, 2 * CH, 0, RING)
            norm_lo(dve, n_first)

            def take_ada_rows(c, n):
                dve.wait_ge(chunks_used, c)
                dve.wait_ge(ada_turned, FREE + n)
                dve.tensor_copy(ada_rows[:, :], ps[0:4, 4, :]).then_inc(ada_rows_ready, 1)

            def take_ada_cols(layer, n, at):
                dve.wait_ge(ada_turned, FREE + n + 1)
                dve.tensor_copy(adat[:, layer, bass.ds(at, 4), :], ps[:, 5, 0:8].rearrange("p (a b) -> p a b", b=2))\
                   .then_inc(ada_taken, 1)

            with dve.Fori(0, IN_W // W_IN // 2) as i:
                for half in range(2):
                    c0, n = C_IN + half * 2 * CH, i * 2 + half
                    los(dve, c0, i, 4 * CH, RING, CH + RING)
                    take_ada_rows(i * 4 * CH + used(c0 + CH), n)
                    los(dve, c0, i, 4 * CH, CH + RING, CH + RING + 2)
                    take_ada_cols(0, n, i * 8 + 4 + 4 * half)
                    los(dve, c0, i, 4 * CH, CH + RING + 2, 2 * CH + RING)
            HD_A, HD_C = HEADS_A + KV_A, 2 * HEADS_C
            for i in range(TT):
                dve.wait_ge(heads_squared, 2 * i + 2)
                dve.reduce_sum(hss[:, i, :], squares[:, i, :].rearrange("p (h e) -> p h e", e=HD), AX_X).then_inc(heads_summed, 1)
            dve.wait_ge(heads_summed, TT)
            dve.tensor_scalar(hss[:, :, :], hss[:, :, :], 1.0 / HD, EPS, ALU.mult, ALU.add).then_inc(heads_mean, 1)
            dve.wait_ge(heads_root, 1)
            for h0, n, c0 in ((0, HD_A, AQ), (HD_A, HD_C, CQ)):
                for i in range(TT):
                    v = proj[:, i, c0:c0 + n * HD].rearrange("p (h e) -> p h e", e=HD)
                    dve.tensor_tensor(v, v, hrs[:, i, h0:h0 + n].unsqueeze(2).to_broadcast([P, n, HD]), ALU.mult)\
                       .then_inc(heads_scaled, 1)
            dve.wait_ge(bias_loaded, 16)

            def soft_logits(n, slot, h, sink):
                dve.wait_ge(scored, n + PAIR + 1)
                dve.wait_ge(exp_done, n + 1)
                dve.scalar_tensor_tensor(logits[:, slot, 0:P], ps[:, 2 + slot, 0:P], HD ** -0.5,
                                         bias[:, bass.ds(h, 1), P:2 * P].rearrange("p a b -> p (a b)"), ALU.mult, ALU.add)
                dve.scalar_tensor_tensor(logits[:, slot, P:3 * P], ps[:, 2 + slot, P:3 * P], HD ** -0.5,
                                         bias[:, bass.ds(h, 1), :].rearrange("p a b -> p (a b)"), ALU.mult, ALU.add)\
                   .then_inc(logits_ready, 1)
                dve.wait_ge(logits_ready, n + PAIR + 1)
                dve.reduce_max(mx[:, slot, 0:1], logits[:, slot, 0:P], AX_X)
                dve.reduce_max(mx[:, slot, 1:2], logits[:, slot, P:3 * P], AX_X).then_inc(max_ready, 1)
                dve.wait_ge(max_ready, n + 1)
                if sink is None:
                    dve.tensor_scalar(nm[:, slot, :], mx[:, slot, :], -1.0, None, ALU.mult).then_inc(negmax_ready, 1)
                else:
                    dve.tensor_scalar(nm[:, slot, :], mx[:, slot, :], sink, -1.0, ALU.max, ALU.mult).then_inc(negmax_ready, 1)

            def soft_finish(n, slot, q0, sink_n):
                dve.wait_ge(exp_done, n + PAIR + 1)
                den = sums
                if sink_n is not None:
                    dve.tensor_tensor(sums[:, slot, :], sums[:, slot, :], esink[:, slot, :], ALU.add).then_inc(den_ready, 1)
                    dve.wait_ge(den_ready, sink_n + 1)
                dve.reciprocal(recip[:, slot, :], den[:, slot, :]).then_inc(recip_ready, 1)
                dve.wait_ge(p_turned, n + PAIR + 1)
                dve.wait_ge(pv_done, n + 1)
                dve.tensor_copy(probs_t[:, slot, :], ps[:, 4 + slot, 0:3 * P]).then_inc(pt_ready, 1)
                dve.wait_ge(pv_done, n + PAIR + 1)
                dve.wait_ge(recip_ready, n + 1)
                dve.tensor_tensor(proj[:, :, bass.ds(q0, HD)], ps[:, 6 + slot, 0:2 * HD].rearrange("p (a b) -> p a b", a=2),
                                  recip[:, slot, :].unsqueeze(2).to_broadcast([P, TT, HD]), ALU.mult).then_inc(out_taken, 1)

            def stick_z(m, slot):
                dve.wait_ge(scored, m + N_SOFT + PAIR + 1)
                dve.wait_ge(exp_done, PAIR + N_SOFT)
                dve.wait_ge(pt_ready, m + N_SOFT + 1)
                dve.tensor_tensor(logits[:, slot, :], ps[:, 2 + slot, 0:3 * P], stick[:, 0:3 * P], ALU.add).then_inc(logits_ready, 1)

            def stick_soft(m, slot):
                dve.wait_ge(b_ln, m + 1)
                dve.scalar_tensor_tensor(probs[:, slot, :], logits[:, slot, :], 0.0, probs[:, slot, :], ALU.max, ALU.add)\
                   .then_inc(b_soft, 1)

            def stick_finish(m, slot, q0):
                dve.wait_ge(b_summed, m + PAIR + 1)
                dve.tensor_tensor(logits[:, slot, :], logits[:, slot, :], ps[:, 4 + slot, 0:3 * P], ALU.add).then_inc(b_exponent, 1)
                dve.wait_ge(pv_done, m + N_SOFT + PAIR + 1)
                dve.tensor_copy(proj[:, :, bass.ds(q0, HD)], ps[:, 6 + slot, 0:2 * HD].rearrange("p (a b) -> p a b", a=2))\
                   .then_inc(out_taken, 1)

            for s, (n0, iters, q0, *_) in enumerate(HEAD_SETS):
                with dve.Fori(0, iters) as i:
                    n = i * 4 + n0
                    if s < 2:
                        sink = lambda j: sinks[:, bass.ds(i * 4 + j, 1)] if s == 0 else None
                        soft_logits(n, 0, n, sink(0))
                        for j in range(4):
                            if j < 3:
                                soft_logits(n + j + 1, (j + 1) % PAIR, n + j + 1, sink(j + 1))
                            soft_finish(n + j, j % PAIR, i * 4 * HD + q0 + j * HD, i * 4 + j if s == 0 else None)
                    else:
                        m = i * 4
                        stick_z(m, 0)
                        for j in range(4):
                            stick_soft(m + j, j % PAIR)
                            if j < 3:
                                stick_z(m + j + 1, (j + 1) % PAIR)
                            stick_finish(m + j, j % PAIR, i * 4 * HD + q0 + j * HD)
            dve.wait_ge(m_squared, 3 * TT)
            for g, (_, w, _) in enumerate(MIX):
                sl = slice(g, 3 * TT, 3)
                ins = dve.tensor_scalar(n_mix.ms[:, sl], n_mix.ss[:, sl], 1.0 / w, EPS, ALU.mult, ALU.add)
            ins.then_inc(m_mean, 1)
            dve.wait_ge(m_root, 1)
            for i in range(TT):
                for g, (c0, w, to) in enumerate(MIX):
                    ins = dve.tensor_scalar(xn_mix[:, i, to:to + w], proj[:, i, c0:c0 + w], n_mix.rstd[:, 3 * i + g:3 * i + g + 1],
                                            None, ALU.mult)
                ins.then_inc(n_mix.scaled, 1)
            norm_lo(dve, n_mix)

            def add_panel(done, c, half, col0):
                dve.wait_ge(chunks_used, c)
                v = xres[:, :, bass.ds(col0, W)]
                dve.tensor_tensor(v, ps[:, 2 * half:2 * half + 2, :], v, ALU.add).then_inc(done, 1)

            with dve.Fori(0, D // W // 2) as i:
                for half in range(2):
                    los(dve, C_OUT + half * CH, i, 2 * CH, RING, RING + CH)
                    add_panel(attn_added, i * 2 * CH + used(C_OUT + (half + 1) * CH), half, i * 2 * W + half * W)
            norm_mean(dve, n_ffn)
            norm_apply(dve, n_ffn)
            norm_lo(dve, n_ffn)
            n_in = IN_W // W_IN

            def older_taps(i, which):
                dve.wait_ge(tap2[which], i + 1)
                for back in (1, 2):
                    vec = V_CONV[2 - back]
                    for m in range(4):
                        ch = i * 4 + which * FT + m
                        ins = dve.scalar_tensor_tensor(conv[which][:, m, back:SEQ], turned_u(m)[:, 0:SEQ - back],
                                                       cols[:, bass.ds(ch + vec[0] * P + vec[1], 1)], conv[which][:, m, back:SEQ],
                                                       ALU.mult, ALU.add)
                    ins.then_inc(taps[which], 1)
                    dve.wait_ge(taps[which], FREE + i * 2 + back)

            with dve.Fori(0, D_FF // W) as i:
                los(dve, C_UP, i, 3 * CH, RING, RING + 2)
                take_ada_cols(1, i + n_in, i * 4)
                los(dve, C_UP, i, 3 * CH, RING + 2, CH + RING + 2)
                older_taps(i, 0)
                los(dve, C_UP, i, 3 * CH, CH + RING + 2, 2 * CH + RING + 2)
                older_taps(i, 1)
                dve.wait_ge(gate_silu, i + 1)
                dve.wait_ge(g_hi_done, FREE + i)
                dve.tensor_tensor(product[:, :, :], conv[0], conv[1], ALU.mult).then_inc(gated, 1)
                los(dve, C_UP, i, 3 * CH, 2 * CH + RING + 2, 3 * CH + RING)
                take_ada_rows(i * 3 * CH + used(C_UP + 3 * CH), i + n_in + 1)
                dve.wait_ge(g_hi_done, FREE + i + 1)
                dve.tensor_tensor(g_lo[:, bass.ds(i * 4, 4), :], product[:, :, :], g_hi[:, bass.ds(i * 4, 4), :].bitcast(F32),
                                  ALU.subtract).then_inc(g_lo_done, 1)
            n_up = D_FF // W
            los(dve, C_ADA_LAST, 0, CH, RING, RING + 2)
            take_ada_cols(1, n_in + n_up, 4 * n_up)
            los(dve, C_ADA_LAST, 0, CH, RING + 2, RING + CH)
            take_ada_rows(used(C_ADA_LAST + CH), n_in + n_up + 1)
            take_ada_cols(1, n_in + n_up + 1, 4 * n_up + 4)
            n = FT // CK_T
            with dve.Fori(0, D // W // 2) as i:
                for half in range(2):
                    los(dve, C_DOWN + half * n, i, 2 * n, RING, RING + n)
                    add_panel(ffn_added, i * 2 * n + used(C_DOWN + (half + 1) * n), half, i * 2 * W + half * W)
            def scales(layer, pre):
                v = adat[:, layer, 4:, :]
                dve.tensor_tensor(v, v, cols_of(V_ADA_B[layer], 3 * KT).unsqueeze(2).to_broadcast([P, 3 * KT, 2]), ALU.add)\
                   .then_inc(ada_biased, 1)
                dve.wait_ge(ada_biased, layer + 1)
                for s in range(2):
                    dve.scalar_tensor_tensor(hscale[:, s, :], adat[:, layer, 4 + KT:4 + 2 * KT, s], 1.0, cols_of(pre, KT),
                                             ALU.add, ALU.mult).then_inc(scales_ready, 1)

            def gate_diagonals(m, layer, post, n):
                for s in range(len(SPREAD[m])):
                    dve.tensor_tensor(hscale[:, s, :], adat[:, layer, 4 + 2 * KT:, s], cols_of(post, KT), ALU.mult)\
                       .then_inc(gains_ready, 1)
                dve.wait_ge(gains_ready, n)
                for s, v in enumerate(SPREAD[m]):
                    for k in range(KT):
                        ins = dve.tensor_scalar(v[:, k * P:(k + 1) * P], ident, hscale[:, s, k:k + 1], -1.0, ALU.mult, ALU.mult)
                    ins.then_inc(diag_ready[m], 1)

            def yout_join(m, targets):
                total, mean, root = y_stats[m]
                dve.wait_ge(yout_squared[m], len(YOUT[m]))
                dve.tensor_scalar(mean, total, 1.0 / D, EPS, ALU.mult, ALU.add).then_inc(yout_mean[m], 1)
                dve.wait_ge(yout_root[m], 1)
                for i, v in enumerate(YOUT[m]):
                    dve.wait_ge(gate_rows_ready[m], i // TT + 1)
                    dve.scalar_tensor_tensor(v, v, root[:, i:i + 1], SPREAD[m][i // TT], ALU.mult, ALU.mult)\
                       .then_inc(yout_scaled[m], 1)
                    dve.wait_ge(yout_scaled[m], i + 1)
                    dve.tensor_tensor(targets[i], targets[i], v, ALU.add).then_inc(yout_added[m], 1)

            scales(0, V_PRE0)
            dve.wait_ge(scales_ready, 2)
            norm_mean(dve, n_pool)
            norm_apply(dve, n_pool)
            norm_shift_lo(dve, n_pool)

            def pool_group(i, e):
                first = C_POOL + e * POOL_CH
                step, n = 2 * POOL_CH, i * 2 + e
                los(dve, first, i, step, RING, CH + RING + 2)
                for m in range(4):
                    dve.wait_ge(pt_hi_done, n * 4 + m + 1)
                    ins = dve.tensor_tensor(pt_lo[:, m, :], ps[:, m, :], pt_hi[:, m, :].bitcast(F32), ALU.subtract)
                ins.then_inc(pt_lo_done, 1)
                los(dve, first, i, step, CH + RING + 2, CH + RING + 6)
                dve.wait_ge(chunks_used, i * step + used(first + CH + 6))
                for m in range(4):
                    ch = n * 4 + m
                    ins = dve.tensor_scalar(y[:, bass.ds(ch, 1), :].rearrange("p a b -> p (a b)"), ps[:, m, :],
                                            cols[:, bass.ds(ch + V_POOL_B[0] * P + V_POOL_B[1], 1)],
                                            cols[:, bass.ds(ch + V_POOL_S[0] * P + V_POOL_S[1], 1)], ALU.add, ALU.mult)
                ins.then_inc(grouped, 1)
                los(dve, first, i, step, CH + RING + 6, POOL_CH + RING)
                dve.wait_ge(grouped, FREE + n + 1)
                for m in range(4):
                    v = y[:, bass.ds(n * 4 + m, 1), :].rearrange("p a b -> p (a b)")
                    dve.wait_ge(gate_silu4, n * 4 + m + 1)
                    dve.tensor_tensor(v, v, gsilu[:, m % 2, :], ALU.mult).then_inc(y_gated, 1)

            with dve.Fori(0, POOL_G // 2) as i:
                for e in range(2):
                    pool_group(i, e)
            for k in range(KT):
                dve.wait_ge(y_hi_done, k + 1)
                dve.tensor_tensor(y_lo[:, k, :], y[:, k, :], y_hi[:, k, :].bitcast(F32), ALU.subtract).then_inc(y_lo_done, 1)
            gate_diagonals(0, 0, V_POST0, 2)
            with dve.Fori(0, D // W // 2) as i:
                los(dve, C_POOL_OUT, i, 2 * CH, RING, RING + 2 * CH)
            dve.wait_ge(ctx_again, 16)
            yout_join(0, [xres[:, i, :] for i in range(TT)] + [ctx_res[:, i, :] for i in range(TT)])
            scales(1, V_PRE1)
            dve.wait_ge(scales_ready, 4)
            norm_mean(dve, n_mla)
            norm_apply(dve, n_mla)
            norm_shift_lo(dve, n_mla)
            dve.memset(kr[:, :, ROPE:], 0.0).then_inc(kr_cleared, 1)
            for n in range(3):
                los(dve, C_MLA + n * CH, 0, 0, RING, RING + CH)
                if n:
                    dve.wait_ge(chunks_used, used(C_MLA + (n + 1) * CH))
                    dve.tensor_copy(proj_c[:, :, (n - 1) * W_IN:n * W_IN], ps[:, 2 + 2 * n:4 + 2 * n, 0:W_IN])\
                       .then_inc(mla_ctx_taken, 1)
            with dve.Fori(0, 2) as i:
                los(dve, C_MLA + 3 * CH, i, 2 * CH, RING, RING + 2 * CH)
            dve.wait_ge(mla_taken, PAIR + MLA_W // W_IN)
            dve.wait_ge(rope_loaded, 16)
            dve.wait_ge(mla_ctx_taken, 2)
            for i in range(TT):
                x4 = proj_l[:, i, GATE0 - ROPE:GATE0].rearrange("p (r h n) -> p r h n", r=2, h=2)
                sin4 = rope[:, i, 1, :].rearrange("p (r h n) -> p r h n", r=2, h=2)
                for h in range(2):
                    dve.tensor_tensor(kr_t[:, i, :, h, :], x4[:, :, 1 - h, :], sin4[:, :, h, :], ALU.mult).then_inc(kr_swapped, 1)
                dve.tensor_tensor(kr[:, i, 0:ROPE], proj_l[:, i, GATE0 - ROPE:GATE0], rope[:, i, 0, :], ALU.mult).then_inc(kr_swapped, 1)
                dve.wait_ge(kr_swapped, 3 * i + 3)
                dve.tensor_tensor(kr[:, i, 0:ROPE], kr[:, i, 0:ROPE], kr_t[:, i, :, :, :].rearrange("p r h n -> p (r h n)"), ALU.add)\
                   .then_inc(kr_staged, 1)
                dve.tensor_copy(kr[:, TT + i, 0:ROPE], proj_c[:, i, KVC:KVC + ROPE]).then_inc(kr_staged, 1)
            norm_mean(dve, n_cq)
            norm_mean(dve, n_ckv)
            norm_apply(dve, n_cq)
            norm_apply(dve, n_ckv)
            norm_lo(dve, n_cq)
            norm_lo(dve, n_ckv)
            dve.wait_ge(gate_silu5, TT)
            with dve.Fori(0, MLA_H // 2) as i:
                los(dve, C_HEADS, i, 4, RING, RING + 2)
                dve.wait_ge(q_nope_ready, i + 1)
                for tt in range(TT):
                    x3 = ps[:, tt, 0:2 * QH].rearrange("p (h e) -> p h e", h=2)[:, :, NOPE:]
                    x5 = x3.rearrange("p h (r a n) -> p h r a n", r=2, a=2)
                    o5 = q_swap[:, tt, :, :].rearrange("p h (r a n) -> p h r a n", r=2, a=2)
                    sin5 = rope[:, tt, 1, :].rearrange("p (r a n) -> p r a n", r=2, a=2)
                    for a in range(2):
                        dve.tensor_tensor(o5[:, :, :, a, :], x5[:, :, :, 1 - a, :],
                                          sin5[:, :, a, :].unsqueeze(1).to_broadcast([P, 2, 2, ROPE // 4]), ALU.mult)
                    dve.tensor_tensor(q_rope[:, tt, :, :], x3, rope[:, tt, 0, :].unsqueeze(1).to_broadcast([P, 2, ROPE]), ALU.mult)\
                       .then_inc(q_swapped, 1)
                dve.wait_ge(q_swapped, i * 2 + 2)
                dve.tensor_tensor(q_rope[:, :, :, :], q_rope[:, :, :, :], q_swap[:, :, :, :], ALU.add).then_inc(q_rope_ready, 1)
                los(dve, C_HEADS, i, 4, RING + 2, RING + 4)
                dve.tensor_copy(v_sb[:, :, :].rearrange("p a b -> p (a b)"), ps[:, 4:6, :].rearrange("p a b -> p (a b)"))\
                   .then_inc(v_ready, 1)
                for m in range(4):
                    dve.wait_ge(mscored, i * 4 + m + 1)
                    dve.reduce_max(mmx[:, m:m + 1], ps[:, 2 + m, :], AX_X).then_inc(mmax_ready, 1)
                    dve.wait_ge(mmax_ready, i * 4 + m + 1)
                    dve.tensor_scalar(mnm[:, m:m + 1], mmx[:, m:m + 1], -MLA_SCALE, None, ALU.mult).then_inc(mneg_ready, 1)
                for m in range(4):
                    dve.wait_ge(mexp_done, i * 4 + m + 1)
                    dve.reciprocal(mrec[:, m:m + 1], msum[:, m:m + 1]).then_inc(mrec_ready, 1)
                    dve.wait_ge(mp_turned, i * 4 + m + 1)
                    dve.wait_ge(mout_done, FREE + i * 4 + m - 1) if m else dve.wait_ge(mout_done, FREE + i * 4)
                    dve.tensor_copy(mprobs_t[:, m % 2, :, :].rearrange("p a b -> p (a b)"), ps[:, 6 + m % 2, :]).then_inc(mpt_ready, 1)
                for m in range(4):
                    h, tt = m // TT, m % TT
                    dve.wait_ge(mout_done, FREE + i * 4 + m + 1)
                    dve.wait_ge(mrec_ready, i * 4 + m + 1)
                    dve.scalar_tensor_tensor(om[:, m, :], ps[:, 2 + m, 0:VD], mrec[:, m:m + 1],
                                             proj_l[:, tt, bass.ds(i * 2 * VD + GATE0 + h * VD, VD)], ALU.mult, ALU.mult)\
                       .then_inc(om_ready, 1)
                dve.wait_ge(om_hi_done, i + 1)
                v = om_hi[:, bass.ds(i * 2, 2), :].rearrange("p a b -> p (a b)")
                dve.tensor_tensor(om_lo[:, bass.ds(i * 2, 2), :].rearrange("p a b -> p (a b)"), ps[:, 1, :], v.bitcast(F32),
                                  ALU.subtract).then_inc(om_lo_done, 1)
            gate_diagonals(1, 1, V_POST1, 3)
            for n in range(D // W):
                los(dve, C_MLA_OUT + n * CH, 0, 0, RING, RING + CH)
            yout_join(1, [xres[:, i, :] for i in range(TT)])

        @block.tensor
        def _(pe):
            pe.sem_inc(chunks_used, RING)
            for s in (ada_turned, mout_done):
                pe.sem_inc(s, FREE)
            for s in (qk_turned, scored, p_turned, pv_done, b_summed):
                pe.sem_inc(s, PAIR)
            pe.wait_ge(consts_loaded, 16 * 4)
            pe.wait_ge(vecs_loaded, 16 * (len(VECS) + len(GAINS)))
            for v in range(VEC_TILES):
                mm = pe.transpose(ps[:, v // 4, (v % 4) * P:(v % 4 + 1) * P], vec_rows[:, v, :], ident)
            mm.then_inc(vecs_turned, 1)
            pe.wait_ge(table_loaded, 32)
            pe.wait_ge(consts_set, 3)
            pe.matmul(ps[0:HEADS_A, 2, 0:384], table[:, 0:HEADS_A], onehot[:, 0, :], start=True, stop=True)
            pe.matmul(ps[0:HEADS_C, 3, 0:384], table[:, HEADS_A:N_TAB], onehot[:, 1, :], start=True, stop=True).then_inc(ext_done, 1)
            norm_turn(pe, n_first)

            def ada_panel(c, n, after=None):
                pe.wait_ge(ada_rows_ready, FREE + n)
                for j in range(CH):
                    pe.wait_ge(lo_split, c + RING + j + 1)
                    for k in range(CK_T):
                        kt = CK_T * j + k
                        for s, w in enumerate((hi, lo)):
                            mm = pe.matmul(ps[:, 4, :], c4[:, 4 * kt:4 * kt + P], w[:, j % RING, k, :],
                                           start=kt == 0 and s == 0, stop=kt == KT - 1 and s == 1)
                    mm.then_inc(chunks_used, 1)
                    if after is not None and j == 1:
                        after()

            def turn_ada(rows, n):
                pe.wait_ge(ada_rows_ready, FREE + rows)
                pe.wait_ge(ada_taken, FREE + n)
                for q in range(4):
                    mm = pe.matmul(ps[:, 5, 2 * q:2 * q + 2], ada_rows[:, q * P:(q + 1) * P], pick[:, :], start=True, stop=True)
                mm.then_inc(ada_turned, 1)

            pe.wait_ge(c_lo, 1)
            pe.wait_ge(ext_ready, 2)
            pe.wait_ge(n_first.lo_done, n_first.all_groups)
            with pe.Fori(0, IN_W // W_IN // 2) as i:
                for half in range(2):
                    c, n = i * 4 * CH + C_IN + half * 2 * CH, i * 2 + half
                    ada_panel(c, n)
                    pe.wait_ge(proj_taken, n + 1)
                    panel_by_tokens(pe, c + CH, 0, h_hi, h_lo, pair(half), W_IN, after=lambda: turn_ada(n + 1, n))

            def head_scores(n, slot, stick_layout):
                pe.wait_ge(staged, n * 2 + 2)
                pe.wait_ge(qk_ready, n + 1)
                for i in range(TT):
                    mm = pe.transpose(ps[:, slot, i * P:(i + 1) * P], stage[:, slot, i, :, :].rearrange("p a b -> p (a b)"), ident)
                mm.then_inc(qk_turned, 1)
                pe.wait_ge(qk_ready, n + PAIR + 1)
                pe.wait_ge(logits_ready, n + 1)
                q, k = qkt[:, slot, 0, :], qkt[:, slot, 1, :]
                if stick_layout:
                    pe.matmul(ps[:, 2 + slot, 0:2 * P], k[:, 0:P], q, start=True, stop=True)
                    pe.matmul(ps[:, 2 + slot, 2 * P:3 * P], k[:, P:2 * P], q[:, P:2 * P], start=True, stop=True).then_inc(scored, 1)
                else:
                    pe.matmul(ps[:, 2 + slot, 0:P], q[:, 0:P], k[:, 0:P], start=True, stop=True)
                    pe.matmul(ps[:, 2 + slot, P:3 * P], q[:, P:2 * P], k, start=True, stop=True).then_inc(scored, 1)

            def soft_turn(n, slot):
                pe.wait_ge(exp_done, n + PAIR + 1)
                pe.wait_ge(pt_ready, n + 1)
                for b in range(3):
                    mm = pe.transpose(ps[:, 4 + slot, b * P:(b + 1) * P], probs[:, slot, b * P:(b + 1) * P], ident)
                mm.then_inc(p_turned, 1)

            def stick_sum(m, slot):
                pe.wait_ge(b_soft, m + 1)
                pe.wait_ge(b_exponent, m + 1)
                pe.matmul(ps[:, 4 + slot, 0:3 * P], stick[:, 3 * P:4 * P], probs[:, slot, :], start=True, stop=False)
                pe.matmul(ps[:, 4 + slot, P:2 * P], negones, probs[:, slot, 2 * P:3 * P], start=False, stop=True).then_inc(b_summed, 1)

            def head_out(n, slot, v0):
                pe.wait_ge(pt_ready, n + PAIR + 1)
                pe.wait_ge(out_taken, n + 1)
                v = [proj[:, i, bass.ds(v0, HD)] for i in range(TT)]
                pe.matmul(ps[:, 6 + slot, 0:HD], probs_t[:, slot, 0:P], v[0], start=True, stop=True)
                pe.matmul(ps[:, 6 + slot, HD:2 * HD], probs_t[:, slot, P:2 * P], v[0], start=True, stop=False)
                pe.matmul(ps[:, 6 + slot, HD:2 * HD], probs_t[:, slot, 2 * P:3 * P], v[1], start=False, stop=True).then_inc(pv_done, 1)

            for s, (n0, iters, q0, k0, ks, kj, v0, vs, vj) in enumerate(HEAD_SETS):
                with pe.Fori(0, iters) as i:
                    n = i * 4 + n0
                    head_scores(n, 0, s == 2)
                    for j in range(4):
                        if j < 3:
                            head_scores(n + j + 1, (j + 1) % PAIR, s == 2)
                        if s < 2:
                            soft_turn(n + j, j % PAIR)
                        else:
                            stick_sum(i * 4 + j, j % PAIR)
                        head_out(n + j, j % PAIR, i * vs + v0 + j * vj)
            norm_turn(pe, n_mix)

            def residual_product(c0, a_hi, a_lo, added, n_norm):
                pe.wait_ge(n_norm.lo_done, n_norm.all_groups)
                with pe.Fori(0, D // W // 2) as i:
                    for half in range(2):
                        pe.wait_ge(added, i * 2 + half + 1)
                        panel_by_tokens(pe, i * 2 * CH + c0 + half * CH, 0, a_hi, a_lo, pair(half), W)

            residual_product(C_OUT, h_hi, h_lo, attn_added, n_mix)
            norm_turn(pe, n_ffn)
            pe.wait_ge(n_ffn.lo_done, n_ffn.all_groups)
            n_in, n_up = IN_W // W_IN, D_FF // W

            def turn_u(i, which):
                pe.wait_ge(u_staged[which], FREE + i + 1)
                pe.wait_ge(taps[1 - which], FREE + i * 2 + 2 * which)
                for m in range(4):
                    for tok in range(TT):
                        mm = pe.transpose(turned_u(m)[:, tok * P:(tok + 1) * P], ustage[:, which, tok, m * P:(m + 1) * P], ident)
                mm.then_inc(u_turned[which], 1)

            with pe.Fori(0, n_up) as i:
                c = i * 3 * CH + C_UP
                pe.wait_ge(u_staged[0], FREE + i)
                panel_by_tokens(pe, c, 0, h_hi, h_lo, pair(0), W, after=lambda: turn_ada(i + n_in, i + n_in))
                pe.wait_ge(u_staged[1], FREE + i)
                panel_by_tokens(pe, c + CH, 0, h_hi, h_lo, pair(1), W, after=lambda: turn_u(i, 0))
                ada_panel(c + 2 * CH, i + n_in, after=lambda: turn_u(i, 1))
            ada_panel(C_ADA_LAST, n_in + n_up, after=lambda: turn_ada(n_in + n_up, n_in + n_up))
            turn_ada(n_in + n_up + 1, n_in + n_up + 1)
            pe.wait_ge(g_lo_done, n_up)
            n = FT // CK_T
            with pe.Fori(0, D // W // 2) as i:
                for half in range(2):
                    pe.wait_ge(ffn_added, i * 2 + half + 1)
                    panel_by_tokens(pe, i * 2 * n + C_DOWN + half * n, half * n, g_hi, g_lo, pair(half), W, FT)
            norm_turn(pe, n_pool)
            pe.wait_ge(n_pool.lo_done, n_pool.all_groups)
            pe.wait_ge(poolm_loaded, 16)
            streams = [(i, i) for i in range(NT)]

            def pool_group(i, e):
                c, s0, n = i * 2 * POOL_CH + C_POOL + e * POOL_CH, e * POOL_CH, i * 2 + e
                pe.wait_ge(grouped, FREE + n)
                panel_by_tokens(pe, c, s0, h4_hi, h4_lo, streams, W)
                pe.wait_ge(y_gated, FREE + n * 4)
                chunk = lambda j, *a: by_channels(pe, c + CH + j, (s0 + CH + j) % RING, *a)
                for j in range(2):
                    chunk(j, h4_hi, h4_lo, CK_T * j, 4, j == 0, False)
                pe.wait_ge(u_ready, n + 1)
                for m in range(4):
                    for s in range(2):
                        for k in range(TT):
                            mm = pe.matmul(ps[:, m, s * SEQ:(s + 1) * SEQ], u[:, TT * s + k, m * P:(m + 1) * P],
                                           poolm[:, bass.ds(n, 1), k, :].rearrange("p a b -> p (a b)"),
                                           start=k == 0, stop=k == TT - 1)
                    mm.then_inc(pooled, 1)
                for j in range(2, 4):
                    chunk(j, h4_hi, h4_lo, CK_T * j, 4, False, False)
                pe.wait_ge(pt_lo_done, FREE + n + 1)
                for j in range(4, 6):
                    chunk(j, pt_hi, pt_lo, CK_T * (j - 4), 0, j == 4, j == 5)
                for j in range(6, 10):
                    chunk(j, h4_hi, h4_lo, CK_T * (j - 2), 4, False, j == 9)

            with pe.Fori(0, POOL_G // 2) as i:
                for e in range(2):
                    pool_group(i, e)
            pe.wait_ge(y_lo_done, KT)
            with pe.Fori(0, D // W // 2) as i:
                for half in range(2):
                    pe.wait_ge(yout_taken[0], i * 2 + half + 1)
                    panel_by_tokens(pe, i * 2 * CH + C_POOL_OUT + half * CH, 0, y_hi, y_lo, [(n, 4 * half + n) for n in range(NT)], W)

            def spread_rows(m):
                pe.wait_ge(yout_taken[m], PAIR + D // W)
                for s, v in enumerate(SPREAD[m]):
                    pe.wait_ge(diag_ready[m], s + 1)
                    if s:
                        pe.wait_ge(gate_rows_ready[m], s)
                    for q in range(4):
                        mm = pe.matmul(ps[:, q, :], negones, v[:, q * W:(q + 1) * W], start=True, stop=True)
                    mm.then_inc(rows_spread[m], 1)

            spread_rows(0)
            norm_turn(pe, n_mla)
            pe.wait_ge(n_mla.lo_done, n_mla.all_groups)
            for n in range(3):
                pe.wait_ge(mla_taken, n + 1)
                ctx_too = [(TT + i, 2 + 2 * n + i) for i in range(TT)] if n else []
                panel_by_tokens(pe, C_MLA + n * CH, 0, k4_hi, k4_lo, pair(n % 2) + ctx_too, W_IN)
            with pe.Fori(0, 2) as i:
                for e in range(2):
                    pe.wait_ge(mla_taken, i * 2 + 4 + e)
                    panel_by_tokens(pe, i * 2 * CH + C_MLA + (3 + e) * CH, 0, k4_hi, k4_lo, pair((3 + e) % 2), W_IN)
            pe.wait_ge(kr_cleared, 1)
            pe.wait_ge(kr_staged, NT)
            pe.wait_ge(mla_taken, PAIR + MLA_W // W_IN)
            for i in range(NT):
                mm = pe.transpose(ps[:, 0, i * P:(i + 1) * P], kr[:, i, :], ident)
            mm.then_inc(kr_turned, 1)
            norm_turn(pe, n_cq)
            pe.wait_ge(n_cq.lo_done, n_cq.all_groups)
            norm_turn(pe, n_ckv)
            pe.wait_ge(n_ckv.lo_done, n_ckv.all_groups)
            pe.wait_ge(kr_ready, 1)
            with pe.Fori(0, MLA_H // 2) as i:
                c = i * 4 + C_HEADS
                pe.wait_ge(om_lo_done, FREE + i)
                panel_by_tokens(pe, c, 0, cq_hi, cq_lo, pair(0), 2 * QH, RT)
                pe.wait_ge(lo_split, c + RING + 4)
                for h in range(2):
                    for k in range(RT):
                        for s, (w, a) in enumerate(((hi, ckv_hi), (hi, ckv_lo), (lo, ckv_hi))):
                            pe.matmul(ps[:, 2 + h, :], w[:, 2 + k // CK_T, k % CK_T, h * 2 * P:h * 2 * P + P], a[:, k, :],
                                      start=k == 0 and s == 0, stop=k == RT - 1 and s == 2)
                for n in range(NT):
                    for k in range(RT):
                        for s, (a, w) in enumerate(((ckv_hi, hi), (ckv_hi, lo), (ckv_lo, hi))):
                            v = w[:, 2 + k // CK_T, k % CK_T, :].rearrange("p (h e) -> p h e", h=2)[:, :, NOPE:]
                            mm = pe.matmul(ps[:, 4 + n // 2, (n % 2) * 2 * VD:(n % 2 + 1) * 2 * VD].rearrange("p (h e) -> p h e", h=2),
                                           a[:, k, n * P:(n + 1) * P], v, start=k == 0 and s == 0, stop=k == RT - 1 and s == 2)
                mm.then_inc(chunks_used, 2)
                pe.wait_ge(q_nope_ready, i + 1)
                for h in range(2):
                    for tt in range(TT):
                        pe.transpose(ps[:, 6, h * SEQ + tt * P:h * SEQ + (tt + 1) * P], q_nope[:, tt, h, :], ident)
                pe.wait_ge(q_rope_ready, i + 1)
                for tt in range(TT):
                    mm = pe.transpose(ps[:, 7, tt * P:(tt + 1) * P], q_rope[:, tt, :, :].rearrange("p h e -> p (h e)"), ident)
                mm.then_inc(q_turned, 1)
                pe.wait_ge(qt_ready, i + 1)
                pe.wait_ge(kn_ready, i + 1)
                pe.wait_ge(v_ready, i + 1)
                for m in range(4):
                    h, q = m // TT, slice(m % TT * P, m % TT * P + P)
                    pe.matmul(ps[:, 2 + m, :], qn_t[:, h, q], kn_t[:, h, :], start=True, stop=False)
                    pe.matmul(ps[:, 2 + m, :], qr_t[:, h, q], krt[:, :], start=False, stop=True).then_inc(mscored, 1)
                for m in range(4):
                    pe.wait_ge(mexp_done, i * 4 + m + 1)
                    pe.wait_ge(mpt_ready, FREE + i * 4 + m - 1) if m else pe.wait_ge(mpt_ready, FREE + i * 4)
                    for k in range(NT):
                        mm = pe.transpose(ps[:, 6 + m % 2, k * P:(k + 1) * P], mprobs[:, m, k * P:(k + 1) * P], ident)
                    mm.then_inc(mp_turned, 1)
                    pe.wait_ge(mpt_ready, FREE + i * 4 + m + 1)
                    for k in range(NT):
                        mm = pe.matmul(ps[:, 2 + m, 0:VD], mprobs_t[:, m % 2, k, :], v_sb[:, k, m // TT * VD:(m // TT + 1) * VD],
                                       start=k == 0, stop=k == NT - 1)
                    mm.then_inc(mout_done, 1)
                for m in range(4):
                    pe.wait_ge(om_ready, i * 4 + m + 1)
                    mm = pe.transpose(ps[:, 1, m * P:(m + 1) * P], om[:, m, :], ident)
                mm.then_inc(om_turned, 1)
            pe.wait_ge(om_lo_done, FREE + MLA_H // 2)
            for n in range(D // W):
                pe.wait_ge(yout_taken[1], n + 1)
                panel_by_tokens(pe, C_MLA_OUT + n * CH, 0, om_hi, om_lo, pair(n % 2), W)
            spread_rows(1)


_OUTS = [((1, SEQ, D), "float32")]


def kernel(**inputs):
    import concourse.bacc as bacc
    from concourse.bass_utils import run_bass_kernel_spmd

    nc = bacc.Bacc("TRN2", target_bir_lowering=False, num_devices=1)
    arrays, t = {}, {}
    for name, a in inputs.items():
        a = np.ascontiguousarray(a)
        arrays[f"in_{name}"] = a
        t[name] = nc.dram_tensor(f"in_{name}", a.shape, mybir.dt.from_np(a.dtype), kind="ExternalInput").ap()
    consts = {name: nc.inline_tensor(a, name=f"const_{name}").ap() for name, a in shape_constants().items()}
    out = nc.dram_tensor("out", (1, SEQ, D), F32, kind="ExternalOutput").ap()
    two_block_kernel(nc, t, out, consts)
    r = run_bass_kernel_spmd(nc, [arrays], core_ids=[0])
    return r.results[0]["out"]
```

```python
import math
from contextlib import ExitStack

import numpy as np

import concourse.bass as bass
from concourse import mybir

F32 = mybir.dt.float32
F32R = mybir.dt.float32r
ALU = mybir.AluOpType
ACT = mybir.ActivationFunctionType
AX_X = mybir.AxisListType.X

P = 128
KIB = 1024
D = 2048
KT = D // P
SEQ = 256
TT = SEQ // P
NT = 2 * TT
HD = 64
HEADS_A, KV_A, HEADS_B, HEADS_C = 8, 2, 8, 16
IN_W = 5376
IN_HEADS = IN_W // HD
PANEL_HEADS = 448 // HD
AQ, AK, AV = 0, 512, 640
BQ, BK, BV = 768, 1280, 1792
CQ, CK, CV = 2304, 3328, 4352
D_FF = 5632
FT = D_FF // P
N_UP = D_FF // 512
N_BUCKETS, T5_MAX = 32, 2048
N_TAB = HEADS_A + HEADS_C
EPS = 1e-6
NEG = -1e30
W = 512
W_IN = 448
RING = 4
CK_T = 2
CH = KT // CK_T
PAIR = 2
FREE = 1
Q_RANK, KV_RANK, NOPE, ROPE, VD, MLA_H = 512, 512, 128, 64, 128, 16
RT = Q_RANK // P
MLA_W = Q_RANK + KV_RANK + ROPE + D
QH = NOPE + ROPE
PAIRS = MLA_H // 2
POOL_G, POOL_WINDOWS = 4, (2, 4, 8, 16)
GRID_W = 64
MLA_SCALE = (NOPE + ROPE) ** -0.5
LAT, CTX = 0, 1

def turn_order(n_weights, ada_after):
    return [c for j in range(n_weights)
            for c in [(False, j)] + [(True, m) for m, after in enumerate(ada_after) if after == j]]


def evenly(n_weights, n_ada):
    return [RING + m * (n_weights - RING - 2) // (n_ada - 1) for m in range(n_ada)]


IN_PANELS = 4
POOL_W = 2 * CH + RT // CK_T
POOL_ADA = [4, 4, 5, 5, 5, 6, 6, 6] + [j for j in range(7, 15) for _ in range(2)]
IN_ORDER = turn_order(IN_PANELS * CH, evenly(IN_PANELS * CH, 2 * CH))
OUT_ORDER = turn_order(2 * CH, evenly(2 * CH, CH))
UP_ORDER = turn_order(2 * CH, [])
DOWN_ORDER = turn_order(2 * FT // CK_T, evenly(2 * FT // CK_T, 2 * CH))
POOL_ORDER = turn_order(2 * POOL_W, POOL_ADA + [POOL_W + j for j in POOL_ADA])
PLAIN_ORDER = turn_order(2 * CH, [])
HEADS_ORDER = turn_order(2 * RT // CK_T, [])
C_IN = 0
C_OUT = C_IN + IN_W // W_IN // IN_PANELS * len(IN_ORDER)
C_UP = C_OUT + D // W // 2 * len(OUT_ORDER)
C_DOWN = C_UP + D_FF // W * len(UP_ORDER)
C_POOL = C_DOWN + D // W // 2 * len(DOWN_ORDER)
C_POOL_OUT = C_POOL + POOL_G // 2 * len(POOL_ORDER)
C_MLA = C_POOL_OUT + (D // W) * CH
C_HEADS = C_MLA + (MLA_W // W_IN) * CH
C_MLA_OUT = C_HEADS + (MLA_H // 2) * 4
N_CHUNKS = C_MLA_OUT + (D // W) * CH
ADA_PANELS = 3 * D // W
ADA_OUT = 2 * IN_W // W_IN // IN_PANELS
ADA_DOWN = ADA_OUT + D // W // 2
ADA_POOL = 2 * ADA_PANELS - 3 * POOL_G
assert ADA_DOWN + D // W == ADA_POOL == ADA_PANELS
STREAM = ((IN_ORDER * (IN_W // W_IN // IN_PANELS)) + OUT_ORDER * (D // W // 2) + UP_ORDER * (D_FF // W)
          + DOWN_ORDER * (D // W // 2) + POOL_ORDER * (POOL_G // 2))


IN_TURN, OUT_TURN, DOWN_TURN = 19, 2 * CH - 1, 25


def is_ada(c):
    return c < len(STREAM) and STREAM[c][0]


def ada_behind(c):
    n = 0
    while is_ada(c + n + 1):
        n += 1
    return n


def place(order, j):
    return order.index((False, j)) if (False, j) in order else len(order)


VEC_TILES = 6
V_CONV = [(0, 0), (1, 0), (2, 0)]
V_CONV_B = (3, 0)
V_ATTN, V_FFN, V_QN, V_KVN = (0, 88), (0, 104), (0, 120), (0, 124)
V_MIX, V_PRE0 = (1, 88), (1, 104)
V_PRE1, V_POST0 = (2, 88), (2, 104)
V_POST1, V_POOL_B = (3, 88), (3, 104)
V_ADA_B, V_POOL_S = [(4, 0), (4, 48)], (4, 96)
V_GAINS = (4, 112)
V_C, V_CCTX = (5, 0), (5, 16)


def vectors(t):
    return ([(V_CONV[m], D_FF * 2 // P, t["conv_w"][0, m]) for m in range(3)]
            + [(V_CONV_B, D_FF * 2 // P, t["conv_b"][0]), (V_ATTN, KT, t["attn_norm"][0]), (V_FFN, KT, t["ffn_norm"][0]),
               (V_QN, RT, t["mla_q_norm_2"][0]), (V_KVN, RT, t["mla_kv_norm_2"][0]), (V_MIX, KT, t["mix_out_gain"][0]),
               (V_PRE0, KT, t["pre_norm_2"][0]), (V_PRE1, KT, t["pre_norm_2"][1]),
               (V_POST0, KT, t["post_norm_2"][0]), (V_POST1, KT, t["post_norm_2"][1]),
               (V_POOL_B, KT, t["pool_b_grp_2"][0].rearrange("g c -> (g c)")), (V_POOL_S, KT, t["pool_scale_2"][0]),
               (V_ADA_B[0], 3 * KT, t["ada_b_2"][0]), (V_ADA_B[1], 3 * KT, t["ada_b_2"][1]),
               (V_C, KT, t["c_2"][0]), (V_CCTX, KT, t["c_ctx_2"])])


GAINS = ["a_q_gain", "a_k_gain", "c_q_gain", "c_k_gain"]


def shape_constants():
    dist = 255 - np.arange(384)
    max_exact = N_BUCKETS // 2
    large = max_exact + (np.log(np.maximum(dist, 1).astype(np.float32) / np.float32(max_exact))
                         / np.float32(math.log(T5_MAX / max_exact)) * np.float32(N_BUCKETS - max_exact)).astype(np.int32)
    bucket = np.where(dist < max_exact, np.maximum(dist, 0), np.minimum(large, N_BUCKETS - 1))
    onehot = np.zeros((N_BUCKETS + 1, 2, 384), np.float32)
    seen_a = (dist >= 0) & (dist <= 127)
    times_c = np.where(dist >= 0, (dist <= 128).astype(int) + (dist % 4 == 0) + (dist % 16 == 0), 0)
    for n, seen in enumerate((seen_a, times_c > 0)):
        onehot[bucket[seen], n, np.nonzero(seen)[0]] = 1.0
    onehot[N_BUCKETS, 0] = np.where(seen_a, 0.0, NEG)
    onehot[N_BUCKETS, 1] = np.where(times_c > 0, np.log(np.maximum(times_c, 1)), NEG)
    i = np.arange(P)
    ident = np.concatenate([np.eye(P), -np.ones((P, P))], 1).astype(np.float32)
    before = np.where(i[:, None] < i[None, :], 0.0, NEG)
    stick = np.concatenate([before, np.zeros((P, P)), before, np.where(i[:, None] >= i[None, :], -1.0, 0.0)], 1)
    pool = np.zeros((POOL_G, SEQ, SEQ), np.float64)
    for g, win in enumerate(POOL_WINDOWS):
        left = win // 2
        right = win - 1 - left
        for t in range(SEQ):
            lo, hi = max(t - left, 0), min(t + right + 1, SEQ)
            pool[g, lo:hi, t] = 1.0 / (hi - lo)
            pool[g, t, t] -= 1.0
    pool = pool.reshape(POOL_G, TT, P, SEQ).transpose(2, 0, 1, 3)
    t = np.arange(SEQ)
    n = ROPE // 4
    freqs = np.float32(10000.0) ** (-np.arange(n, dtype=np.float32) / np.float32(n))
    ang = np.stack([(t // GRID_W).astype(np.float32)[:, None] * freqs, (t % GRID_W).astype(np.float32)[:, None] * freqs], 1)
    cos, sin = np.cos(ang), np.sin(ang)
    rope = np.stack([np.stack([cos, cos], 2), np.stack([-sin, sin], 2)], 1).reshape(TT, P, 2 * ROPE).transpose(1, 0, 2)
    f = lambda a: np.ascontiguousarray(a, dtype=np.float32)
    return {"onehot": f(onehot), "ident": ident, "stick": f(stick), "pool": f(pool), "rope": f(rope)}


class NormSignals:

    NAMES = ("squared", "mean", "root", "scaled", "turned", "shifted", "hi_done", "lo_done")

    def __init__(self, sem):
        self.squared, self.mean, self.root, self.scaled, self.turned, self.shifted, self.hi_done, self.lo_done = (
            sem(f"norm_{name}") for name in self.NAMES)
        self.rows = self.means = self.scaled_rows = self.groups = self.shifts = 0


class Norm:

    def __init__(self, sig, src, xn, stats, hi, lo, nk, scale, shift=None, tmp=None, own_means=False):
        self.src, self.xn, self.hi, self.lo, self.nk, self.scale, self.shift, self.tmp = src, xn, hi, lo, nk, scale, shift, tmp
        self.nt = len(src)
        self.per = 4 // self.nt if self.nt <= 4 else 1
        self.groups = nk // self.per
        self.ss, self.ms, self.rstd = stats
        self.squared, self.mean, self.root, self.scaled = sig.squared, sig.mean, sig.root, sig.scaled
        self.turned, self.shifted, self.hi_done, self.lo_done = sig.turned, sig.shifted, sig.hi_done, sig.lo_done
        self.rows0, self.means0, self.scaled0, self.groups0, self.groups_shifted0 = (
            sig.rows, sig.means, sig.scaled_rows, sig.groups, sig.shifts)
        self.all_groups = self.groups0 + self.groups
        if not own_means:
            sig.rows += self.nt
            sig.means += 1
        sig.scaled_rows += self.nt
        sig.groups += self.groups
        sig.shifts += self.groups if shift else 0


def two_block_kernel(nc, t, out, consts):
    ctx = ExitStack()
    with ctx:
        sem = lambda name: ctx.enter_context(nc.semaphore(name))
        base = (nc.sbuf_base + 31) // 32 * 32
        fence_bytes = nc.sbuf_bytes_remaining - 64
        ctx.enter_context(nc.sbuf_tensor("fence", [P, fence_bytes // 4], F32))
        end = base + fence_bytes

        class Place:

            def __init__(self, at):
                self.at = at

            def __call__(self, name, shape, dtype=F32):
                size = 4
                for n in shape[1:]:
                    size *= n
                got = nc.alloc_sbuf_tensor_at(name, shape, dtype, offset=self.at)
                self.at += (size + 31) // 32 * 32
                assert self.at <= end, (name, self.at, end)
                return got

        keep = Place(base)
        raw = keep("raw", [P, RING, CK_T, W])
        hi = keep("hi", [P, RING, CK_T, W], F32R)
        lo = keep("lo", [P, RING, CK_T, W], F32R)
        xres = keep("xres", [P, TT, D])
        ident2 = keep("ident2", [P, 2 * P])
        ident, negones = ident2[:, 0:P], ident2[:, P:2 * P]
        cols = keep("cols", [P, VEC_TILES * P])
        adat = keep("adat", [P, 2, 3 * KT, 2])
        csil = keep("csil", [P, 2, KT])
        ada_acc = keep("ada_acc", [P, PAIR, 2, W])
        ss = keep("ss", [P, 16])
        ms = keep("ms", [P, 16])
        rstd = keep("rstd", [P, 16])
        halves = keep("halves", [P, TT * PANEL_HEADS])
        head_eps = keep("head_eps", [P, TT * PANEL_HEADS])
        hscale = keep("hscale", [P, 2, KT])
        region = keep.at

        def at(kib):
            return Place(region + int(kib * KIB))

        pl = at(0)
        h_hi = pl("h_hi", [P, KT, SEQ], F32R)
        h_lo = pl("h_lo", [P, KT, SEQ], F32R)
        proj = pl("proj", [P, TT, IN_W])
        bias = pl("bias", [P, N_TAB, SEQ])
        stage = pl("stage", [P, PAIR, TT, 2, HD])
        qkt = pl("qkt", [HD, PAIR, 2, SEQ])
        logits = pl("logits", [P, PAIR, 3 * P])
        probs = pl("probs", [P, PAIR, 3 * P])
        probs_t = pl("probs_t", [P, PAIR, 3 * P])
        stick = pl("stick", [P, 4 * P])
        mx = pl("mx", [P, PAIR, TT])
        nm = pl("nm", [P, PAIR, TT])
        sums = pl("sums", [P, PAIR, TT])
        esink = pl("esink", [P, PAIR, TT])
        recip = pl("recip", [P, PAIR, TT])
        sinks = pl("sinks", [P, HEADS_A])
        gqk = pl("gqk", [HD, 2])
        hss = pl("hss", [P, TT, IN_HEADS])
        hrs = pl("hrs", [P, TT, IN_HEADS])
        vec_rows = pl("vec_rows", [P, VEC_TILES, P])
        onehot = pl("onehot", [N_BUCKETS + 1, 2, 384])
        table = pl("table", [N_BUCKETS + 1, N_TAB])
        ext = pl("ext", [HEADS_C, 2, 384])
        squares = pl("squares", [P, TT, W_IN])
        pb = at(0)
        b_z = pb("b_z", [P, HEADS_B, 3 * P])
        b_w = pb("b_w", [P, HEADS_B, 3 * P])
        xn_first = at(32)("xn_first", [P, TT, D])
        xn_mix = at(74)("xn_mix", [P, TT, D])
        xn_ffn = at(32)("xn_ffn", [P, TT, D])
        pl = at(32)
        g_hi = pl("g_hi", [P, FT, SEQ], F32R)
        g_lo = pl("g_lo", [P, FT, SEQ], F32R)
        ustage = pl("ustage", [P, 2, TT, W])
        conv = [ustage[:, w, :, :].rearrange("p a (b n) -> p (a b) n", n=SEQ) for w in range(2)]
        product = conv[0]
        pl = at(0)
        h4_hi = pl("h4_hi", [P, KT, NT * P], F32R)
        h4_lo = pl("h4_lo", [P, KT, NT * P], F32R)
        y = pl("y", [P, KT, NT * P])
        u = pl("u", [P, NT, W])
        pt_hi = pl("pt_hi", [P, 4, NT * P], F32R)
        pt_lo = pl("pt_lo", [P, 4, NT * P], F32R)
        poolm = pl("poolm", [P, POOL_G, TT, SEQ])
        gsilu = [u[:, m, :] for m in range(2)]
        xn4 = at(64)("xn4", [P, NT, D])
        ctx_in = at(96)("ctx_in", [P, TT, D])
        shift_tmp = at(112)("shift_tmp", [P, PAIR, NT * P])
        y_hi = at(0)("y_hi", [P, KT, NT * P], F32R)
        y_lo = at(32)("y_lo", [P, KT, NT * P], F32R)
        ctx_res = at(64)("ctx_res", [P, TT, D])
        gate_rows = at(80)("gate_rows", [P, 2, D])
        yout = at(96)("yout", [P, NT, D])
        pl = at(64)
        proj_l = pl("proj_l", [P, TT, MLA_W])
        proj_c_at = pl.at
        proj_c = pl("proj_c", [P, TT, 2 * W_IN])
        k4_hi = at(0)("k4_hi", [P, KT, NT * P], F32R)
        k4_lo = at(32)("k4_lo", [P, KT, NT * P], F32R)
        xn4b = at(96)("xn4b", [P, NT, D])
        shift_tmpb = at(80)("shift_tmpb", [P, PAIR, NT * P])
        pl = at(96)
        cq_hi = pl("cq_hi", [P, RT, SEQ], F32R)
        cq_lo = pl("cq_lo", [P, RT, SEQ], F32R)
        ckv_hi = pl("ckv_hi", [P, RT, NT * P], F32R)
        ckv_lo = pl("ckv_lo", [P, RT, NT * P], F32R)
        rope = pl("rope", [P, TT, 2, ROPE])
        rot = pl.at
        kr = pl("kr", [P, NT, 2, P])
        kr_t = pl("kr_t", [P, TT, 2, 2, ROPE // 4])
        kr_lo = pl("kr_lo", [P, 2, NT * P], F32R)
        pl = Place(rot)
        q_rope = pl("q_rope", [P, TT, 2, ROPE])
        q_swap = pl("q_swap", [P, TT, 2, ROPE])
        mmx = pl("mmx", [P, 4])
        mnm = pl("mnm", [P, 4])
        msum = pl("msum", [P, 4])
        mrec = pl("mrec", [P, 4])
        pl = Place(proj_c_at)
        kr_hi = pl("kr_hi", [P, 2, NT * P], F32R)
        om = pl("om", [P, 4, VD])
        pl = at(0)
        om_hi = pl("om_hi", [P, MLA_H, SEQ], F32R)
        om_lo = pl("om_lo", [P, MLA_H, SEQ], F32R)
        q_nope = pl("q_nope", [P, TT, 2, NOPE])
        qn_hi = pl("qn_hi", [P, 2, SEQ], F32R)
        qn_lo = pl("qn_lo", [P, 2, SEQ], F32R)
        qr_hi = pl("qr_hi", [P, SEQ], F32R)
        qr_lo = pl("qr_lo", [P, SEQ], F32R)
        kn_hi = pl("kn_hi", [P, 2, NT * P], F32R)
        kn_lo = pl("kn_lo", [P, 2, NT * P], F32R)
        v_sb = pl("v_sb", [P, NT, 2 * VD])
        mprobs = pl("mprobs", [P, 4, NT * P])
        mprobs_t = pl("mprobs_t", [P, 2, NT, P])
        assert pl.at <= region + 64 * KIB
        yout2 = at(64)("yout2", [P, TT, D])
        gate_rows2 = at(96)("gate_rows2", [P, D])

        ps = ctx.enter_context(nc.psum_tensor("ps", [P, 8, W], F32))
        bias_rows = nc.dram_tensor("bias_rows", (N_TAB, P, 3 * P), F32).ap()

        def turned_u(m):
            return ps[:, 6 + m // 2, (m % 2) * SEQ:(m % 2 + 1) * SEQ]

        def col(vec, k):
            return cols[:, vec[0] * P + vec[1] + k:vec[0] * P + vec[1] + k + 1]

        def cols_of(vec, n):
            return cols[:, vec[0] * P + vec[1]:vec[0] * P + vec[1] + n]

        raw_loaded = [sem(f"raw_loaded{s}") for s in range(RING)]
        hi_split = sem("hi_split")
        lo_split = sem("lo_split")
        chunks_used = sem("chunks_used")
        x_loaded, consts_loaded, vecs_loaded = sem("x_loaded"), sem("consts_loaded"), sem("vecs_loaded")
        vecs_cleared, vecs_turned, cols_ready = sem("vecs_cleared"), sem("vecs_turned"), sem("cols_ready")
        consts_set, table_loaded = sem("consts_set"), sem("table_loaded")
        c_silu = sem("c_silu")
        ext_done, ext_ready, bias_stored, bias_loaded = sem("ext_done"), sem("ext_ready"), sem("bias_stored"), sem("bias_loaded")
        proj_taken = sem("proj_taken")
        ada_added, ada_turned, ada_taken = sem("ada_added"), sem("ada_turned"), sem("ada_taken")
        heads_squared, heads_mean, heads_root, heads_scaled = (
            sem(n) for n in ("heads_squared", "heads_mean", "heads_root", "heads_scaled"))
        staged = sem("staged")
        qk_turned, qk_ready, scored, logits_ready, exp_done, p_turned, pt_ready, pv_done, out_taken = (
            sem(n) for n in ("qk_turned", "qk_ready", "scored", "logits_ready", "exp_done", "p_turned", "pt_ready", "pv_done", "out_taken"))
        max_ready, negmax_ready, den_ready, recip_ready = (sem(n) for n in ("max_ready", "negmax_ready", "den_ready", "recip_ready"))
        b_abs, b_exp, b_ln, b_soft, b_summed, b_exponent = (
            sem(n) for n in ("b_abs", "b_exp", "b_ln", "b_soft", "b_summed", "b_exponent"))
        b_weights = sem("b_weights")
        attn_added, ffn_added = sem("attn_added"), sem("ffn_added")
        u_staged = [sem("gate_staged"), sem("up_staged")]
        u_turned = [sem("gate_turned"), sem("up_turned")]
        taps = [sem("gate_taps"), sem("up_taps")]
        tap2 = [sem("gate_tap2"), sem("up_tap2")]
        gate_silu, gated, g_hi_done, g_lo_done = sem("gate_silu"), sem("gated"), sem("g_hi_done"), sem("g_lo_done")

        stats = lambda a, n: (ss[:, a:a + n], ms[:, a:a + n], rstd[:, a:a + n])
        norm_signals = NormSignals(sem)
        n_first = Norm(norm_signals, [xres[:, i, :] for i in range(TT)], xn_first, stats(0, TT), h_hi, h_lo, KT,
                       lambda k, s: col(V_ATTN, k))
        MIX = [(AQ, HEADS_A * HD, 0), (CQ, HEADS_C * HD, 1024), (BQ, HEADS_B * HD, 512)]

        def load_chunk(sp, c, slot, src, width):
            sp.wait_ge(lo_split, c + 1)
            sp.dma_start(raw[:, slot, :, 0:width], src.rearrange("(k p) n -> p k n", p=P)).then_inc(raw_loaded[slot], 16)

        def load_panel(sp, c, slot0, w, col0, width, nk=KT):
            for j in range(nk // CK_T):
                load_chunk(sp, c + j, (slot0 + j) % RING, w[j * CK_T * P:(j + 1) * CK_T * P, bass.ds(col0, width)], width)

        def split_hi(act, c, slot, turn, ada):
            act.wait_ge(raw_loaded[slot], 16 * (turn + 1))
            act.wait_ge(chunks_used, c + 1)
            act.activation(hi[:, slot, :, :], raw[:, slot, :, :], ACT.Copy).then_inc(hi_split, 1 + ada)

        def split_lo(dve, c, slot):
            dve.wait_ge(hi_split, c + 1)
            dve.tensor_tensor(lo[:, slot, :, :], raw[:, slot, :, :], hi[:, slot, :, :].bitcast(F32),
                              ALU.subtract).then_inc(lo_split, 1)

        def his(act, first, i, step, a, b):
            for j in range(a, b):
                c = first + j
                if isinstance(i, int) and c + i * step >= N_CHUNKS:
                    continue
                if not is_ada(c):
                    split_hi(act, i * step + c, c % RING, i * (step // RING) + c // RING, ada_behind(c))

        def ada_chunk(dve, c, slot, turn, n, j, a, turned):
            dve.wait_ge(raw_loaded[slot], 16 * (turn + 1))
            done = (n * CH + j) * 3
            for k in range(CK_T):
                for v in range(2):
                    kt = j * CK_T + k
                    acc = ada_acc[:, a, v, :]
                    if kt == 0:
                        if v == 0:
                            dve.wait_ge(ada_turned, turned)
                        ins = dve.tensor_scalar(acc, raw[:, slot, k, :], csil[:, v, kt:kt + 1], None, ALU.mult)
                    else:
                        if k == 0 and v == 1:
                            dve.wait_ge(lo_split, c + RING)
                        else:
                            dve.wait_ge(ada_added, done + k + v)
                        ins = dve.scalar_tensor_tensor(acc, raw[:, slot, k, :], csil[:, v, kt:kt + 1], acc, ALU.mult, ALU.add)
                    ins.then_inc(lo_split if (k, v) == (CK_T - 1, 1) else ada_added, 1)

        def los(dve, first, i, step, a, b, ada0=0, ada_step=0, slot=None):
            for j in range(a, b):
                c = first + j
                if isinstance(i, int) and c + i * step >= N_CHUNKS:
                    continue
                if is_ada(c):
                    m = STREAM[c][1]
                    n = i * ada_step + ada0 + m // CH
                    ada_chunk(dve, i * step + c, c % RING, i * (step // RING) + c // RING, n, m % CH,
                              m // CH % PAIR if slot is None else slot, n + 1 if slot is None else n + 2)
                else:
                    split_lo(dve, i * step + c, c % RING)

        def by_tokens(pe, c, slot, a_hi, a_lo, kt0, outs, width, first, last, ada=0):
            pe.wait_ge(lo_split, c + RING + 1)
            for k in range(CK_T):
                for tok, bank in outs:
                    for s, (a, w) in enumerate(((a_hi, hi), (a_hi, lo), (a_lo, hi))):
                        mm = pe.matmul(ps[:, bank, 0:width], a[:, kt0 + k, tok * P:(tok + 1) * P], w[:, slot, k, 0:width],
                                       start=first and k == 0 and s == 0, stop=last and k == CK_T - 1 and s == 2)
            mm.then_inc(chunks_used, 1 + ada)

        def by_channels(pe, c, slot, a_hi, a_lo, kt0, bank0, first, last, ada=0):
            pe.wait_ge(lo_split, c + RING + 1)
            for k in range(CK_T):
                for n in range(W // P):
                    for s, (w, a) in enumerate(((hi, a_hi), (hi, a_lo), (lo, a_hi))):
                        mm = pe.matmul(ps[:, bank0 + n, :], w[:, slot, k, n * P:(n + 1) * P], a[:, kt0 + k, :],
                                       start=first and k == 0 and s == 0, stop=last and k == CK_T - 1 and s == 2)
            mm.then_inc(chunks_used, 1 + ada)

        def panel_by_tokens(pe, first, i, order, j0, a_hi, a_lo, outs, width, nk=KT, before=None):
            n = nk // CK_T
            for j in range(n):
                if before is not None:
                    before(j0 + j)
                at = first + place(order, j0 + j)
                by_tokens(pe, i * len(order) + at, at % RING, a_hi, a_lo, CK_T * j, outs, width, j == 0, j == n - 1, ada_behind(at))

        def turn_ada(pe, n, a, bank, col0=0):
            pe.wait_ge(ada_taken, n + FREE)
            for q in range(W // P):
                for v in range(2):
                    acc = ada_acc[:, a, v, q * P:(q + 1) * P]
                    at = col0 + 2 * q + v
                    mm = pe.matmul(ps[:, bank, at:at + 1], acc, negones[:, 0:1], start=True, stop=True)
            mm.then_inc(ada_turned, 1)

        def take_ada(dve, n, layer, bank, col0=0):
            dve.wait_ge(ada_turned, n + PAIR + 1)
            dve.tensor_scalar(adat[:, layer, bass.ds((n - layer * ADA_PANELS) * 4, 4), :],
                              ps[:, bank, col0:col0 + 8].rearrange("p (a b) -> p a b", b=2), -1.0, None, ALU.mult)\
               .then_inc(ada_taken, 1)

        def pair(half):
            return [(i, PAIR * half + i) for i in range(TT)]

        def used(n):
            return RING + n

        def norm_squares(act, n, wait):
            for i in range(n.nt):
                wait(act, i)
                if i:
                    act.wait_ge(n.squared, n.rows0 + i)
                w = P * n.nk
                act.activation(ps[:, 4:4 + (w + W - 1) // W, :].rearrange("p a b -> p (a b)")[:, 0:w], n.src[i], ACT.Square,
                               accum_out=n.ss[:, i:i + 1]).then_inc(n.squared, 1)

        def norm_mean(dve, n):
            dve.wait_ge(n.squared, n.rows0 + n.nt)
            dve.tensor_scalar(n.ms, n.ss, 1.0 / (P * n.nk), EPS, ALU.mult, ALU.add).then_inc(n.mean, 1)

        def norm_root(pool, n):
            pool.wait_ge(n.mean, n.means0 + 1)
            pool.tensor_tensor(n.rstd, n.ms, halves[:, 0:n.nt], ALU.pow).then_inc(n.root, 1)

        def norm_apply(dve, n):
            dve.wait_ge(n.root, n.means0 + 1)
            for i in range(n.nt):
                dve.tensor_scalar(n.xn(i) if callable(n.xn) else n.xn[:, i, :], n.src[i], n.rstd[:, i:i + 1], None,
                                  ALU.mult).then_inc(n.scaled, 1)

        TURN_BANKS = 4

        def norm_turn(pe, n):
            for g in range(n.groups):
                if g >= TURN_BANKS:
                    pe.wait_ge(n.lo_done, n.groups0 + g - TURN_BANKS + 1)
                for m in range(n.per):
                    for i in range(n.nt):
                        if g == 0 and m == 0:
                            pe.wait_ge(n.scaled, n.scaled0 + i + 1)
                        src = n.xn(i) if callable(n.xn) else n.xn[:, i, :]
                        k = g * n.per + m
                        mm = pe.transpose(ps[:, 4 + g % TURN_BANKS, (m * n.nt + i) * P:(m * n.nt + i + 1) * P],
                                          src[:, k * P:(k + 1) * P], ident)
                mm.then_inc(n.turned, 1)

        def norm_parts(n, g):
            w = n.nt * P
            for m in range(n.per):
                yield g * n.per + m, ps[:, 4 + g % TURN_BANKS, m * w:(m + 1) * w]

        def norm_hi(act, n):
            for g in range(n.groups):
                if n.shift:
                    act.wait_ge(n.shifted, n.groups_shifted0 + g + 1)
                    act.activation(n.hi[:, g, :], n.tmp[:, g % 2, :], ACT.Copy).then_inc(n.hi_done, 1)
                else:
                    act.wait_ge(n.turned, n.groups0 + g + 1)
                    for k, src in norm_parts(n, g):
                        ins = act.activation(n.hi[:, k, :], src, ACT.Identity, scale=n.scale(k, 0))
                    ins.then_inc(n.hi_done, 1)

        def norm_lo(dve, n):
            for g in range(n.groups):
                dve.wait_ge(n.turned, n.groups0 + g + 1)
                dve.wait_ge(n.hi_done, n.groups0 + g + 1)
                for k, src in norm_parts(n, g):
                    ins = dve.scalar_tensor_tensor(n.lo[:, k, :], src, n.scale(k, 0), n.hi[:, k, :].bitcast(F32),
                                                   ALU.mult, ALU.subtract)
                ins.then_inc(n.lo_done, 1)

        def norm_shift_lo(dve, n):
            def shift(g):
                dve.wait_ge(n.turned, n.groups0 + g + 1)
                if g >= PAIR:
                    dve.wait_ge(n.lo_done, n.groups0 + g - PAIR + 1)
                for s in range(n.nt // TT):
                    sl = slice(s * SEQ, (s + 1) * SEQ)
                    ins = dve.tensor_scalar(n.tmp[:, g % 2, sl], ps[:, 4 + g % TURN_BANKS, sl], n.scale(g, s), n.shift(g, s),
                                            ALU.mult, ALU.add)
                ins.then_inc(n.shifted, 1)

            shift(0)
            for g in range(n.groups):
                if g + 1 < n.groups:
                    shift(g + 1)
                dve.wait_ge(n.hi_done, n.groups0 + g + 1)
                dve.wait_ge(n.shifted, n.groups_shifted0 + g + 1)
                dve.tensor_tensor(n.lo[:, g, :], n.tmp[:, g % 2, :], n.hi[:, g, :].bitcast(F32), ALU.subtract).then_inc(n.lo_done, 1)

        m_squared, m_mean, m_root = sem("mix_groups_squared"), sem("mix_groups_mean"), sem("mix_groups_root")
        n_mix = Norm(norm_signals, [xn_mix[:, i, :] for i in range(TT)], xn_mix, stats(2, 6), h_hi, h_lo, KT,
                     lambda k, s: col(V_MIX, k), own_means=True)
        n_ffn = Norm(norm_signals, [xres[:, i, :] for i in range(TT)], xn_ffn, stats(8, TT), h_hi, h_lo, KT,
                     lambda k, s: col(V_FFN, k))

        N_SOFT = HEADS_A + HEADS_C
        N_HEADS = N_SOFT + HEADS_B

        class Head:

            def __init__(self, n, slot, kind, q, k, v, member):
                self.n, self.slot, self.kind, self.q, self.k, self.v, self.member = n, slot, kind, q, k, v, member

        def head(m, i=0):
            if m < HEADS_A:
                g = m // (HEADS_A // KV_A)
                return Head(m, m % PAIR, "a", AQ + m * HD, AK + g * HD, AV + g * HD, m)
            if m < N_SOFT:
                c = m - HEADS_A
                return Head(i * 2 + m, m % PAIR, "c", i * 2 * HD + CQ + c * HD, i * 2 * HD + CK + c * HD, i * 2 * HD + CV + c * HD, c)
            b = m - N_SOFT
            return Head(m, m % PAIR, "b", BQ + b * HD, BK + b * HD, BV + b * HD, b)

        pairs = [slice(2 * p, 2 * p + 2) for p in range(HEADS_B // 2)]
        C_LOOP = (HEADS_C - 4) // 2

        def soft_steps(eng, step):
            for m in range(HEADS_A):
                step(head(m), head(m + 2), head(m + 3))
            with eng.Fori(0, C_LOOP) as i:
                for m in range(HEADS_A, HEADS_A + 2):
                    step(head(m, i), head(m + 2, i), head(m + 3, i))
            for m in range(HEADS_A + 2 * C_LOOP, N_SOFT):
                step(head(m), head(m + 2), head(m + 3))

        ctx_loaded, poolm_loaded, ctx_again, rope_loaded = (
            sem(n) for n in ("ctx_loaded", "poolm_loaded", "ctx_again", "rope_loaded"))
        ada_biased, scales_ready, gains_ready = sem("ada_biased"), sem("scales_ready"), sem("gains_ready")
        u_ready, pooled, pt_hi_done, pt_lo_done, grouped, gate_silu4, y_gated = (
            sem(n) for n in ("u_ready", "pooled", "pt_hi_done", "pt_lo_done", "grouped", "gate_silu4", "y_gated"))
        y_hi_done, y_lo_done = sem("y_hi_done"), sem("y_lo_done")
        yout_taken = [sem("yout_taken"), sem("yout2_taken")]
        diag_ready = [sem("diag_ready"), sem("diag2_ready")]
        rows_spread = [sem("rows_spread"), sem("rows2_spread")]
        gate_rows_ready = [sem("gate_rows_ready"), sem("gate_rows2_ready")]
        yout_squared, yout_mean, yout_root, yout_scaled, yout_added = (
            [sem(f"{n}{m}") for m in range(2)] for n in ("yout_squared", "yout_mean", "yout_root", "yout_scaled", "yout_added"))
        mla_taken, mla_ctx_taken = sem("mla_taken"), sem("mla_ctx_taken")
        gate_silu5 = sem("gate_silu5")
        kr_cleared, kr_swapped, kr_staged, kr_turned, kr_hi_done, kr_lo_done = (
            sem(n) for n in ("kr_cleared", "kr_swapped", "kr_staged", "kr_turned", "kr_hi_done", "kr_lo_done"))
        q_nope_ready, q_swapped, q_rope_ready, q_turned, q_hi_done, q_lo_done = (
            sem(n) for n in ("q_nope_ready", "q_swapped", "q_rope_ready", "q_turned", "q_hi_done", "q_lo_done"))
        kn_summed, kn_hi_done, kn_lo_done, v_ready = (sem(n) for n in ("kn_summed", "kn_hi_done", "kn_lo_done", "v_ready"))
        mscored, mmax_ready, mneg_ready, mexp_done, mrec_ready = (
            sem(n) for n in ("mscored", "mmax_ready", "mneg_ready", "mexp_done", "mrec_ready"))
        mp_turned, mpt_ready, mout_done, om_ready, om_turned, om_hi_done, om_lo_done = (
            sem(n) for n in ("mp_turned", "mpt_ready", "mout_done", "om_ready", "om_turned", "om_hi_done", "om_lo_done"))
        out_stored = sem("out_stored")

        def modulated(layer, ctx_tile, xn, k_hi, k_lo, tmp):
            return Norm(norm_signals, [xres[:, i, :] for i in range(TT)] + [ctx_tile[:, i, :] for i in range(TT)], xn, stats(0, NT),
                        k_hi, k_lo, KT, lambda k, s: hscale[:, s, k:k + 1], lambda k, s: adat[:, layer, k, s:s + 1], tmp)

        n_pool = modulated(0, ctx_in, xn4, h4_hi, h4_lo, shift_tmp)
        n_mla = modulated(1, ctx_res, xn4b, k4_hi, k4_lo, shift_tmpb)
        KVC = Q_RANK + KV_RANK - W_IN
        cq_rows = [proj_l[:, i, 0:Q_RANK] for i in range(TT)]
        ckv_rows = ([proj_l[:, i, Q_RANK:Q_RANK + KV_RANK] for i in range(TT)]
                    + [proj_c[:, i, Q_RANK - W_IN:KVC] for i in range(TT)])
        n_cq = Norm(norm_signals, cq_rows, lambda i: cq_rows[i], stats(4, TT), cq_hi, cq_lo, RT, lambda k, s: col(V_QN, k))
        n_ckv = Norm(norm_signals, ckv_rows, lambda i: ckv_rows[i], stats(8, NT), ckv_hi, ckv_lo, RT, lambda k, s: col(V_KVN, k))
        YOUT = [[yout[:, i, :] for i in range(NT)], [yout2[:, i, :] for i in range(TT)]]
        SPREAD = [[gate_rows[:, s, :] for s in range(2)], [gate_rows2[:, :]]]
        y_stats = [stats(0, NT), stats(4, TT)]
        GATE0 = Q_RANK + KV_RANK + ROPE

        VECS = vectors(t)
        block = ctx.enter_context(nc.Block())

        @block.sync
        def _(sp):
            sp.dma_start(xres[:, :, :], t["x"][0].rearrange("(t p) d -> p t d", p=P)).then_inc(x_loaded, 16)
            def load_turn(first, i, order, weights, ada=None):
                for at, (of_ada, m) in enumerate(order):
                    c = first + at
                    if of_ada:
                        layer, col0 = ada
                        src, width = t["ada_w_2"][layer][m % CH * CK_T * P:(m % CH + 1) * CK_T * P,
                                                         bass.ds(col0 + m // CH * W, W)], W
                    else:
                        src, width = weights(m)
                    load_chunk(sp, i * len(order) + c, c % RING, src, width)

            def rows(w, j, col0, width):
                return w[j * CK_T * P:(j + 1) * CK_T * P, bass.ds(col0, width)], width

            def first_panels(i):
                load_turn(C_IN, i, IN_ORDER, lambda j: rows(t["w_in"][0], j % CH, (i * IN_PANELS + j // CH) * W_IN, W_IN), (0, i * 2 * W))

            first_panels(0)
            sp.wait_ge(bias_stored, 2 * 16)
            sp.dma_start(bias[:, :, :], bass.AP(bias_rows.tensor, P - 1, [[3 * P - 1, P], [3 * P * P, N_TAB], [1, SEQ]]))\
              .then_inc(bias_loaded, 16)
            with sp.Fori(1, IN_W // W_IN // IN_PANELS) as i:
                first_panels(i)
            with sp.Fori(0, D // W // 2) as i:
                load_turn(C_OUT, i, OUT_ORDER, lambda j: rows(t["w_out"][0], j % CH, i * 2 * W + j // CH * W, W), (0, (i + ADA_OUT) * W))
            with sp.Fori(0, D_FF // W) as i:
                load_turn(C_UP, i, UP_ORDER, lambda j: rows(t["w_up"][0], j % CH, i * W + j // CH * D_FF, W))
            n = FT // CK_T
            with sp.Fori(0, D // W // 2) as i:
                load_turn(C_DOWN, i, DOWN_ORDER, lambda j: rows(t["w_down"][0], j % n, i * 2 * W + j // n * W, W),
                          (0, (i * 2 + ADA_DOWN) * W))
            def pool_weights(i, j):
                g, m = i * 2 + j // POOL_W, j % POOL_W
                if m < CH:
                    return rows(t["pool_w_in_2"][0], m, g * W, W)
                if m - CH in (4, 5):
                    r = (m - CH - 4) * CK_T * P
                    return t["pool_w_grp_2"][0, bass.ds(g, 1), r:r + CK_T * P, :].rearrange("g c d -> (g c) d"), W
                return rows(t["pool_w_in_2"][0], m - CH - 2 * (m - CH > 5), g * W + D, W)

            with sp.Fori(0, POOL_G // 2) as i:
                load_turn(C_POOL, i, POOL_ORDER, lambda j: pool_weights(i, j), (1, i * 6 * W))
            with sp.Fori(0, D // W) as i:
                load_panel(sp, i * CH + C_POOL_OUT, 0, t["pool_w_out_2"][0], i * W, W)
            with sp.Fori(0, MLA_W // W_IN) as i:
                load_panel(sp, i * CH + C_MLA, 0, t["mla_w_in_2"][0], i * W_IN, W_IN)
            with sp.Fori(0, MLA_H // 2) as i:
                load_panel(sp, i * 4 + C_HEADS, 0, t["mla_w_uq_2"][0], i * 2 * QH, 2 * QH, RT)
                load_panel(sp, i * 4 + C_HEADS + 2, 2, t["mla_w_ukv_2"][0], i * W, W, RT)
            with sp.Fori(0, D // W) as i:
                load_panel(sp, i * CH + C_MLA_OUT, 0, t["mla_w_out_2"][0], i * W, W)
            sp.wait_ge(yout_added[1], TT)
            sp.dma_start(out[0].rearrange("(t p) d -> p t d", p=P), xres[:, :, :]).then_inc(out_stored, 16)
            sp.wait_ge(out_stored, 16)

        @block.gpsimd
        def _(pool):
            pool.memset(vec_rows[:, :, :], 0.0).then_inc(vecs_cleared, 1)
            pool.wait_ge(consts_set, 4)
            norm_root(pool, n_first)
            by_head = lambda c: c[:, :].rearrange("p (t h) -> p t h", t=TT)
            with pool.Fori(0, IN_W // W_IN // IN_PANELS) as i:
                for q in range(IN_PANELS):
                    n = i * IN_PANELS + q
                    some = bass.ds(n * PANEL_HEADS, PANEL_HEADS)
                    pool.wait_ge(heads_squared, TT * (n + 1) + FREE)
                    pool.tensor_tensor(hss[:, :, some], hss[:, :, some], by_head(head_eps), ALU.add).then_inc(heads_mean, 1)
                    pool.wait_ge(heads_mean, n + 1)
                    pool.tensor_tensor(hrs[:, :, some], hss[:, :, some], by_head(halves), ALU.pow).then_inc(heads_root, 1)

            def stage_head(h):
                pool.wait_ge(qk_turned, h.n + 1)
                for m, c0 in enumerate((h.q, h.k)):
                    pool.tensor_copy(stage[:, h.slot, :, m, :], proj[:, :, bass.ds(c0, HD)]).then_inc(staged, 1)

            pool.wait_ge(heads_scaled, TT)
            for m in range(HEADS_A):
                stage_head(head(m))
            pool.wait_ge(heads_scaled, 2 * TT)
            with pool.Fori(0, HEADS_C // 2) as i:
                for m in range(HEADS_A, HEADS_A + 2):
                    stage_head(head(m, i))
            for m in range(N_SOFT, N_HEADS):
                stage_head(head(m))
            for m, sl in enumerate((slice(0, 2 * TT), slice(2 * TT, 3 * TT))):
                pool.wait_ge(m_mean, m + 1)
                pool.tensor_tensor(n_mix.rstd[:, sl], n_mix.ms[:, sl], halves[:, sl], ALU.pow).then_inc(m_root, 1)
            norm_root(pool, n_ffn)
            norm_root(pool, n_pool)

            def yout_roots(m):
                pool.wait_ge(yout_mean[m], 1)
                _, mean, root = y_stats[m]
                pool.tensor_tensor(root, mean, halves[:, 0:len(YOUT[m])], ALU.pow).then_inc(yout_root[m], 1)

            yout_roots(0)
            norm_root(pool, n_mla)
            norm_root(pool, n_cq)
            norm_root(pool, n_ckv)
            yout_roots(1)

        @block.scalar
        def _(act):
            for dst, src in ((ident2, "ident"), (stick, "stick"), (onehot, "onehot")):
                act.dma_start(dst[:], consts[src]).then_inc(consts_loaded, 16)
            act.dma_start(table[0:N_BUCKETS, :], t["rel_bias_table"]).then_inc(table_loaded, 16)
            act.dma_start(sinks[:, :], bass.AP(t["a_sinks"].tensor, 0, [[0, P], [1, HEADS_A]])).then_inc(table_loaded, 16)
            act.wait_ge(vecs_cleared, 1)
            for (tile, row), n, src in VECS:
                act.dma_start(vec_rows[row:row + n, tile, :], src.rearrange("(r p) -> r p", p=P)).then_inc(vecs_loaded, 16)
            for m, name in enumerate(GAINS):
                r = V_GAINS[1] + m
                act.dma_start(vec_rows[r:r + 1, V_GAINS[0], 0:HD], t[name]).then_inc(vecs_loaded, 16)
            act.sem_inc(proj_taken, PAIR)
            act.sem_inc(qk_ready, PAIR)
            act.sem_inc(exp_done, PAIR)
            for s in (heads_squared, u_staged[0], u_staged[1], g_hi_done):
                act.sem_inc(s, FREE)
            norm_squares(act, n_first, lambda e, i: e.wait_ge(x_loaded, 16))
            act.wait_ge(cols_ready, 3)
            act.activation(csil[:, :, :].rearrange("p a b -> p (a b)"), cols_of(V_C, 2 * KT), ACT.Silu).then_inc(c_silu, 1)
            act.wait_ge(consts_set, 4)
            his(act, C_IN, 0, 0, 0, RING)
            act.wait_ge(ext_ready, 2)
            for to, e, n in ((0, 0, HEADS_A), (HEADS_A, 1, HEADS_C)):
                act.dma_start(bias_rows[to:to + n, :, :], ext[0:n, e, :].unsqueeze(1).to_broadcast([n, P, 3 * P]))\
                   .then_inc(bias_stored, 16)
            norm_hi(act, n_first)

            with act.Fori(0, IN_W // W_IN // IN_PANELS) as i:
                for q in range(IN_PANELS):
                    step, at, end = len(IN_ORDER), place(IN_ORDER, q * CH), place(IN_ORDER, (q + 1) * CH)
                    his(act, C_IN, i, step, at + RING + (3 if q else 0), end + RING)
                    act.wait_ge(chunks_used, i * step + used(C_IN + end))
                    act.activation(proj[:, :, bass.ds((i * IN_PANELS + q) * W_IN, W_IN)], ps[:, 2 * (q % 2):2 * (q % 2) + 2, 0:W_IN],
                                   ACT.Copy).then_inc(proj_taken, 1)
                    n = i * IN_PANELS + q
                    act.wait_ge(proj_taken, n + PAIR + 1)
                    for tt in range(TT):
                        act.wait_ge(heads_squared, TT * n + tt + FREE)
                        for h in range(PANEL_HEADS):
                            ins = act.activation(squares[:, tt, h * HD:(h + 1) * HD], proj[:, tt, bass.ds(n * W_IN + h * HD, HD)],
                                                 ACT.Square, accum_out=hss[:, tt, bass.ds(n * PANEL_HEADS + h, 1)])
                        ins.then_inc(heads_squared, 1)
                        if tt == 0 and q < IN_PANELS - 1:
                            his(act, C_IN, i, step, end + RING, end + RING + 3)
            def turned(h):
                act.wait_ge(qk_turned, h.n + PAIR + 1)
                act.wait_ge(scored, h.n + 1)
                act.activation(qkt[:, h.slot, 0, :], ps[0:HD, h.slot, 0:SEQ], ACT.Identity,
                               scale=HD ** -0.5 if h.kind == "b" else gqk[:, int(h.kind == "c"):int(h.kind == "c") + 1])
                act.activation(qkt[:, h.slot, 1, :], ps[HD:2 * HD, h.slot, 0:SEQ], ACT.Identity).then_inc(qk_ready, 1)

            def soft_exp(h):
                act.wait_ge(negmax_ready, h.n + 1)
                act.wait_ge(p_turned, h.n + 1)
                act.wait_ge(recip_ready, h.n + 1)
                for i, sl in enumerate((slice(0, P), slice(P, 3 * P))):
                    ins = act.activation(probs[:, h.slot, sl], logits[:, h.slot, sl], ACT.Exp, bias=nm[:, h.slot, i:i + 1],
                                         accum_out=sums[:, h.slot, i:i + 1])
                    if h.kind == "a":
                        ins = act.activation(esink[:, h.slot, i:i + 1], sinks[:, h.member:h.member + 1], ACT.Exp,
                                             bias=nm[:, h.slot, i:i + 1])
                ins.then_inc(exp_done, 1)

            def step(h, two, three):
                turned(three)
                if two.kind != "b":
                    soft_exp(two)

            act.wait_ge(cols_ready, 4)
            turned(head(0))
            turned(head(1))
            soft_exp(head(0))
            turned(head(2))
            soft_exp(head(1))
            soft_steps(act, step)
            for m in range(N_SOFT + 3, N_HEADS):
                turned(head(m))
            for p, sl in enumerate(pairs):
                act.wait_ge(logits_ready, PAIR + N_SOFT + 2 * p + 2)
                act.activation(b_w[:, sl, :], b_z[:, sl, :], ACT.Abs).then_inc(b_abs, 1)
                act.wait_ge(b_abs, p + 1)
                act.activation(b_w[:, sl, :], b_w[:, sl, :], ACT.Exp, scale=-1.0).then_inc(b_exp, 1)
            for p, sl in enumerate(pairs):
                act.wait_ge(b_exp, p + 1)
                act.activation(b_w[:, sl, :], b_w[:, sl, :], ACT.Ln, bias=1.0).then_inc(b_ln, 1)

            def mix_squares(g, n):
                c0, w, _ = MIX[g]
                act.wait_ge(out_taken, PAIR + n)
                for i in range(TT):
                    at = TT * g + i
                    if at:
                        act.wait_ge(m_squared, at)
                    act.activation(ps[:, 0:2, :].rearrange("p a b -> p (a b)")[:, 0:w], proj[:, i, c0:c0 + w], ACT.Square,
                                   accum_out=n_mix.ss[:, at:at + 1]).then_inc(m_squared, 1)

            for m in range(HEADS_B):
                act.wait_ge(b_exponent, m + PAIR + 1)
                act.activation(b_w[:, m, :], b_z[:, m, :], ACT.Exp).then_inc(b_weights, 1)
                if m == 1:
                    mix_squares(0, HEADS_A)
                    mix_squares(1, N_SOFT)
            mix_squares(2, N_HEADS)
            norm_hi(act, n_mix)
            with act.Fori(0, D // W // 2) as i:
                his(act, C_OUT, i, len(OUT_ORDER), RING, RING + len(OUT_ORDER))
            norm_squares(act, n_ffn, lambda e, i: e.wait_ge(attn_added, PAIR + D // W))
            norm_hi(act, n_ffn)

            def stage_u(i, which):
                act.wait_ge(chunks_used, i * 2 * CH + used(C_UP + (1 + which) * CH))
                act.wait_ge(g_lo_done, FREE + i) if which == 0 else act.wait_ge(gated, FREE + i)
                act.activation(ustage[:, which, :, :], ps[:, 2 * which:2 * which + 2, :], ACT.Copy).then_inc(u_staged[which], 1)

            def tap_two(i, which):
                act.wait_ge(u_turned[which], i + 1)
                for m in range(4):
                    ch = i * 4 + which * FT + m
                    ins = act.activation(conv[which][:, m, :], turned_u(m), ACT.Identity,
                                         scale=cols[:, bass.ds(ch + V_CONV[2][0] * P + V_CONV[2][1], 1)],
                                         bias=cols[:, bass.ds(ch + V_CONV_B[0] * P + V_CONV_B[1], 1)])
                ins.then_inc(tap2[which], 1)

            def up_and_gate(i, first, last):
                step = 2 * CH
                his(act, first, i, step, RING, RING + 2)
                tap_two(i, 0)
                his(act, first, i, step, RING + 2, CH + RING)
                act.wait_ge(taps[0], FREE + i * 2 + 2)
                act.activation(conv[0], conv[0], ACT.Silu).then_inc(gate_silu, 1)
                stage_u(i, 1)
                if not last:
                    his(act, first, i, step, CH + RING, CH + RING + 2)
                tap_two(i, 1)
                if not last:
                    his(act, first, i, step, CH + RING + 2, CH + RING + 5)
                act.wait_ge(gated, FREE + i + 1)
                act.activation(g_hi[:, bass.ds(i * 4, 4), :], product[:, :, :], ACT.Copy).then_inc(g_hi_done, 1)
                if not last:
                    his(act, first, i, step, CH + RING + 5, 2 * CH + RING)
                    stage_u(i + 1, 0)

            his(act, C_UP, 0, 0, RING, CH + RING)
            stage_u(0, 0)
            with act.Fori(0, N_UP - 1) as i:
                up_and_gate(i, C_UP + CH, False)
            up_and_gate(N_UP - 1, C_UP + CH, True)
            with act.Fori(0, D // W // 2) as i:
                his(act, C_DOWN, i, len(DOWN_ORDER), RING, RING + len(DOWN_ORDER))
            act.wait_ge(ffn_added, PAIR + D // W)
            act.dma_start(ctx_in[:, :, :], t["ctx_2"][0].rearrange("(t p) d -> p t d", p=P)).then_inc(ctx_loaded, 16)
            act.dma_start(poolm[:, :, :, :], consts["pool"]).then_inc(poolm_loaded, 16)
            act.wait_ge(scales_ready, 2)
            norm_squares(act, n_pool, lambda e, i: e.wait_ge(ctx_loaded, 16) if i >= TT else None)
            norm_hi(act, n_pool)

            def pool_group(i, e):
                step, n = len(POOL_ORDER), i * 2 + e
                ahead = lambda j: place(POOL_ORDER, e * POOL_W + j) + RING
                done = lambda j: i * step + used(C_POOL + place(POOL_ORDER, e * POOL_W + j) + 1)
                his(act, C_POOL, i, step, ahead(0), ahead(CH))
                act.wait_ge(chunks_used, done(CH - 1))
                act.wait_ge(y_gated, FREE + n * 4)
                act.activation(u[:, :, :], ps[:, 0:4, :], ACT.Copy).then_inc(u_ready, 1)
                his(act, C_POOL, i, step, ahead(CH), ahead(CH + 2))
                act.wait_ge(pt_lo_done, FREE + n)
                for m in range(4):
                    act.wait_ge(pooled, n * 4 + m + 1)
                    act.activation(pt_hi[:, m, :], ps[:, m, :], ACT.Copy).then_inc(pt_hi_done, 1)
                his(act, C_POOL, i, step, ahead(CH + 2), ahead(POOL_W))
                act.wait_ge(chunks_used, done(POOL_W - 1))
                for m in range(4):
                    act.wait_ge(y_gated, FREE + n * 4 + m - 1) if m >= 1 else act.wait_ge(y_gated, FREE + n * 4)
                    act.activation(gsilu[m % 2], ps[:, 4 + m, :], ACT.Silu).then_inc(gate_silu4, 1)

            with act.Fori(0, POOL_G // 2) as i:
                for e in range(2):
                    pool_group(i, e)
            for k in range(KT):
                act.wait_ge(y_gated, FREE + k + 1)
                act.activation(y_hi[:, k, :], y[:, k, :], ACT.Copy).then_inc(y_hi_done, 1)
            act.wait_ge(y_lo_done, KT)
            act.dma_start(ctx_res[:, :, :], t["ctx_2"][0].rearrange("(t p) d -> p t d", p=P)).then_inc(ctx_again, 16)
            act.sem_inc(yout_taken[0], PAIR)
            act.sem_inc(yout_taken[1], PAIR)
            with act.Fori(0, D // W // 2) as i:
                for half in range(2):
                    his(act, C_POOL_OUT + half * CH, i, 2 * CH, RING, RING + CH)
                    act.wait_ge(chunks_used, i * 2 * CH + used(C_POOL_OUT + (half + 1) * CH))
                    act.activation(yout[:, :, bass.ds(i * 2 * W + half * W, W)], ps[:, 4 * half:4 * half + 4, :], ACT.Copy)\
                       .then_inc(yout_taken[0], 1)

            def yout_squares(m):
                act.wait_ge(yout_taken[m], PAIR + D // W)
                for i, v in enumerate(YOUT[m]):
                    if i:
                        act.wait_ge(yout_squared[m], i)
                    act.activation(ps[:, 4:8, :].rearrange("p a b -> p (a b)"), v, ACT.Square,
                                   accum_out=y_stats[m][0][:, i:i + 1]).then_inc(yout_squared[m], 1)
                for s, v in enumerate(SPREAD[m]):
                    act.wait_ge(rows_spread[m], s + 1)
                    act.activation(v, ps[:, 0:4, :].rearrange("p a b -> p (a b)"), ACT.Copy).then_inc(gate_rows_ready[m], 1)

            yout_squares(0)
            act.wait_ge(scales_ready, 4)
            act.wait_ge(yout_added[0], NT)
            norm_squares(act, n_mla, lambda e, i: None)
            norm_hi(act, n_mla)
            act.dma_start(rope[:, :, :, :].rearrange("p t a e -> p t (a e)"), consts["rope"]).then_inc(rope_loaded, 16)

            def take_mla(n, first, half, i=0, step=0):
                act.wait_ge(chunks_used, i * step + used(C_MLA + (first + 1) * CH))
                act.activation(proj_l[:, :, bass.ds(n * W_IN, W_IN)], ps[:, 2 * half:2 * half + 2, 0:W_IN], ACT.Copy)\
                   .then_inc(mla_taken, 1)

            act.sem_inc(mla_taken, PAIR)
            for n in range(3):
                his(act, C_MLA + n * CH, 0, 0, RING, RING + CH)
                take_mla(n, n, n % 2)
            with act.Fori(0, 2) as i:
                for e in range(2):
                    his(act, C_MLA + (3 + e) * CH, i, 2 * CH, RING, RING + CH)
                    take_mla(i * 2 + 3 + e, 3 + e, (3 + e) % 2, i, 2 * CH)
            norm_squares(act, n_cq, lambda e, i: e.wait_ge(mla_ctx_taken, 2))
            act.wait_ge(n_cq.squared, n_cq.rows0 + TT)
            norm_squares(act, n_ckv, lambda e, i: None)
            norm_hi(act, n_cq)
            norm_hi(act, n_ckv)

            def pair_values(p, ahead, i=0):
                act.wait_ge(chunks_used, p * 4 + used(C_HEADS + 2))
                act.activation(q_nope[:, :, :, :], ps[:, 0:2, 0:2 * QH].rearrange("p t (h e) -> p t h e", h=2)[:, :, :, 0:NOPE],
                               ACT.Copy).then_inc(q_nope_ready, 1)
                his(act, C_HEADS, i, 4, ahead, ahead + 2)
                act.wait_ge(kn_summed, p + 1)
                act.activation(kn_hi[:, :, :], ps[:, 2:4, :], ACT.Copy).then_inc(kn_hi_done, 1)
                act.wait_ge(q_turned, p + 1)
                act.activation(qn_hi[:, :, :].rearrange("p a b -> p (a b)"), ps[:, 0, :], ACT.Copy)
                act.activation(qr_hi[:, :], ps[:, 1, 0:SEQ], ACT.Copy).then_inc(q_hi_done, 1)
                his(act, C_HEADS, i, 4, ahead + 2, ahead + 4)

            def pair_exps(p):
                for m in range(4):
                    act.wait_ge(mneg_ready, p * 4 + m + 1)
                    act.activation(mprobs[:, m, :], ps[:, 4 + m, :], ACT.Exp, scale=MLA_SCALE, bias=mnm[:, m:m + 1],
                                   accum_out=msum[:, m:m + 1]).then_inc(mexp_done, 1)

            def pair_out(p):
                act.wait_ge(om_turned, p + 1)
                act.activation(om_hi[:, bass.ds(p * 2, 2), :].rearrange("p a b -> p (a b)"), ps[:, 7, :], ACT.Copy)\
                   .then_inc(om_hi_done, 1)

            pair_values(0, RING)
            act.wait_ge(kr_turned, 1)
            act.activation(kr_hi[:, :, :], ps[:, 4:6, :], ACT.Copy).then_inc(kr_hi_done, 1)
            for i in range(TT):
                act.activation(proj_l[:, i, GATE0:], proj_l[:, i, GATE0:], ACT.Silu).then_inc(gate_silu5, 1)
            with act.Fori(0, PAIRS - 1) as i:
                pair_exps(i)
                pair_values(i + 1, 2 * RING, i)
                pair_out(i)
            pair_exps(PAIRS - 1)
            pair_out(PAIRS - 1)
            for n in range(D // W):
                his(act, C_MLA_OUT + n * CH, 0, 0, RING, RING + CH)
                act.wait_ge(chunks_used, used(C_MLA_OUT + (n + 1) * CH))
                act.activation(yout2[:, :, n * W:(n + 1) * W], ps[:, 2 * (n % 2):2 * (n % 2) + 2, :], ACT.Copy)\
                   .then_inc(yout_taken[1], 1)
            yout_squares(1)

        @block.vector
        def _(dve):
            dve.sem_inc(lo_split, RING)
            for s in (logits_ready, pt_ready, out_taken, recip_ready, b_exponent, attn_added, ffn_added):
                dve.sem_inc(s, PAIR)
            for s in (ada_taken, taps[0], taps[1], gated, g_lo_done, pt_lo_done, grouped, y_gated, q_lo_done, v_ready, om_lo_done):
                dve.sem_inc(s, FREE)
            dve.memset(halves[:, :], -0.5).then_inc(consts_set, 1)
            dve.memset(head_eps[:, :], HD * EPS).then_inc(consts_set, 1)
            dve.memset(raw[:, :, :, W_IN:], 0.0).then_inc(consts_set, 1)
            dve.memset(table[N_BUCKETS:N_BUCKETS + 1, :], 1.0).then_inc(consts_set, 1)
            dve.wait_ge(vecs_turned, 1)
            dve.tensor_copy(cols[:, 4 * P:6 * P], ps[:, 1, 0:2 * P]).then_inc(cols_ready, 2)
            dve.tensor_copy(cols[:, 0:4 * P], ps[:, 0, :]).then_inc(cols_ready, 1)
            dve.wait_ge(cols_ready, 3)
            for m in range(2):
                g0 = V_GAINS[0] * P + V_GAINS[1] + 2 * m
                ins = dve.tensor_tensor(gqk[:, m:m + 1], cols[0:HD, g0:g0 + 1], cols[0:HD, g0 + 1:g0 + 2], ALU.mult)
            ins.then_inc(cols_ready, 1)
            dve.wait_ge(ext_done, 1)
            dve.tensor_copy(ext[0:HEADS_A, 0, :], ps[0:HEADS_A, 2, 0:384]).then_inc(ext_ready, 1)
            dve.tensor_copy(ext[:, 1, :], ps[0:HEADS_C, 3, 0:384]).then_inc(ext_ready, 1)
            norm_mean(dve, n_first)
            norm_apply(dve, n_first)
            los(dve, C_IN, 0, 0, 0, RING)
            norm_lo(dve, n_first)

            dve.wait_ge(c_silu, 1)
            with dve.Fori(0, IN_W // W_IN // IN_PANELS) as i:
                order = IN_ORDER
                mid = place(order, IN_TURN) + 1 + RING
                los(dve, C_IN, i, len(order), RING, mid, 0, 2)
                take_ada(dve, i * 2, 0, 5)
                los(dve, C_IN, i, len(order), mid, len(order) + RING, 0, 2)
                take_ada(dve, i * 2 + 1, 0, 5)
            dve.wait_ge(heads_root, IN_W // W_IN)
            for c0, n in ((AQ, HEADS_A + KV_A), (CQ, 2 * HEADS_C)):
                for i in range(TT):
                    v = proj[:, i, c0:c0 + n * HD].rearrange("p (h e) -> p h e", e=HD)
                    dve.tensor_tensor(v, v, hrs[:, i, c0 // HD:c0 // HD + n].unsqueeze(2).to_broadcast([P, n, HD]), ALU.mult)\
                       .then_inc(heads_scaled, 1)
            dve.wait_ge(bias_loaded, 16)

            def soft_logits(h):
                slot, n = h.slot, h.n
                table = bias[:, bass.ds(n, 1), :].rearrange("p a b -> p (a b)")
                dve.wait_ge(scored, n + PAIR + 1)
                dve.wait_ge(exp_done, n + 1)
                dve.scalar_tensor_tensor(logits[:, slot, 0:P], ps[:, 2 + slot, 0:P], HD ** 0.5, table[:, P:2 * P], ALU.mult, ALU.add)
                dve.scalar_tensor_tensor(logits[:, slot, P:3 * P], ps[:, 2 + slot, P:3 * P], HD ** 0.5, table, ALU.mult, ALU.add)\
                   .then_inc(logits_ready, 1)
                dve.wait_ge(logits_ready, n + PAIR + 1)
                dve.reduce_max(mx[:, slot, 0:1], logits[:, slot, 0:P], AX_X)
                dve.reduce_max(mx[:, slot, 1:2], logits[:, slot, P:3 * P], AX_X).then_inc(max_ready, 1)
                dve.wait_ge(max_ready, n + 1)
                if h.kind == "a":
                    dve.tensor_scalar(nm[:, slot, :], mx[:, slot, :], sinks[:, h.member:h.member + 1], -1.0, ALU.max, ALU.mult)\
                       .then_inc(negmax_ready, 1)
                else:
                    dve.tensor_scalar(nm[:, slot, :], mx[:, slot, :], -1.0, None, ALU.mult).then_inc(negmax_ready, 1)

            def stick_z(h):
                dve.wait_ge(scored, h.n + PAIR + 1)
                dve.tensor_tensor(b_z[:, h.member, :], ps[:, 2 + h.slot, 0:3 * P], stick[:, 0:3 * P], ALU.add).then_inc(logits_ready, 1)

            def soft_turned(h):
                dve.wait_ge(p_turned, h.n + PAIR + 1)
                dve.wait_ge(pv_done, h.n + 1)
                dve.tensor_copy(probs_t[:, h.slot, :], ps[:, 4 + h.slot, 0:3 * P]).then_inc(pt_ready, 1)

            def soft_recip(h):
                dve.wait_ge(exp_done, h.n + PAIR + 1)
                if h.kind == "a":
                    dve.tensor_tensor(sums[:, h.slot, :], sums[:, h.slot, :], esink[:, h.slot, :], ALU.add).then_inc(den_ready, 1)
                    dve.wait_ge(den_ready, h.n + 1)
                dve.reciprocal(recip[:, h.slot, :], sums[:, h.slot, :]).then_inc(recip_ready, 1)

            def soft_out(h):
                dve.wait_ge(pv_done, h.n + PAIR + 1)
                dve.wait_ge(recip_ready, h.n + PAIR + 1)
                dve.tensor_tensor(proj[:, :, bass.ds(h.q, HD)], ps[:, 6 + h.slot, 0:2 * HD].rearrange("p (a b) -> p a b", a=2),
                                  recip[:, h.slot, :].unsqueeze(2).to_broadcast([P, TT, HD]), ALU.mult).then_inc(out_taken, 1)

            def step(h, two, three):
                soft_recip(h)
                soft_turned(h)
                soft_logits(two) if two.kind != "b" else stick_z(two)
                soft_out(h)

            soft_logits(head(0))
            soft_logits(head(1))
            soft_steps(dve, step)
            for m in range(N_SOFT + 2, N_HEADS):
                stick_z(head(m))

            def mix_scale(g):
                c0, w, to = MIX[g]
                for i in range(TT):
                    ins = dve.tensor_scalar(xn_mix[:, i, to:to + w], proj[:, i, c0:c0 + w], n_mix.rstd[:, TT * g + i:TT * g + i + 1],
                                            None, ALU.mult)
                    if g == 2:
                        ins.then_inc(n_mix.scaled, 1)

            def mix_mean(groups):
                dve.wait_ge(m_squared, TT * (groups[-1] + 1))
                for g in groups:
                    sl = slice(TT * g, TT * (g + 1))
                    ins = dve.tensor_scalar(n_mix.ms[:, sl], n_mix.ss[:, sl], 1.0 / MIX[g][1], EPS, ALU.mult, ALU.add)
                ins.then_inc(m_mean, 1)

            for p, sl in enumerate(pairs):
                dve.wait_ge(b_ln, p + 1)
                dve.scalar_tensor_tensor(b_w[:, sl, :], b_z[:, sl, :], 0.0, b_w[:, sl, :], ALU.max, ALU.add).then_inc(b_soft, 1)
                for m in (2 * p, 2 * p + 1):
                    dve.wait_ge(b_summed, m + PAIR + 1)
                    dve.tensor_tensor(b_z[:, m, :], b_z[:, m, :], ps[:, 4 + m % PAIR, 0:3 * P], ALU.add).then_inc(b_exponent, 1)
            mix_mean((0, 1))
            for m in range(HEADS_B):
                h = head(N_SOFT + m)
                dve.wait_ge(pv_done, h.n + PAIR + 1)
                dve.tensor_copy(proj[:, :, h.q:h.q + HD], ps[:, 6 + h.slot, 0:2 * HD].rearrange("p (a b) -> p a b", a=2))\
                   .then_inc(out_taken, 1)
            dve.wait_ge(m_root, 1)
            mix_scale(0)
            mix_scale(1)
            mix_mean((2,))
            dve.wait_ge(m_root, 2)
            mix_scale(2)
            norm_lo(dve, n_mix)

            def add_panel(done, c, half, col0):
                dve.wait_ge(chunks_used, c)
                v = xres[:, :, bass.ds(col0, W)]
                dve.tensor_tensor(v, ps[:, 2 * half:2 * half + 2, :], v, ALU.add).then_inc(done, 1)

            with dve.Fori(0, D // W // 2) as i:
                order = OUT_ORDER
                for half in range(2):
                    at, end = place(order, half * CH), place(order, (half + 1) * CH)
                    los(dve, C_OUT, i, len(order), at + RING, end + RING, ADA_OUT, 1, 1)
                    if half:
                        take_ada(dve, i + ADA_OUT, 0, 5)
                    add_panel(attn_added, i * len(order) + used(C_OUT + end), half, i * 2 * W + half * W)
            norm_mean(dve, n_ffn)
            norm_apply(dve, n_ffn)
            norm_lo(dve, n_ffn)
            def older_taps(i, which):
                dve.wait_ge(tap2[which], i + 1)
                for back in (1, 2):
                    vec = V_CONV[2 - back]
                    for m in range(4):
                        ch = i * 4 + which * FT + m
                        ins = dve.scalar_tensor_tensor(conv[which][:, m, back:SEQ], turned_u(m)[:, 0:SEQ - back],
                                                       cols[:, bass.ds(ch + vec[0] * P + vec[1], 1)], conv[which][:, m, back:SEQ],
                                                       ALU.mult, ALU.add)
                    ins.then_inc(taps[which], 1)
                    dve.wait_ge(taps[which], FREE + i * 2 + back)

            def up_and_gate(i, first, last):
                step = 2 * CH
                los(dve, first, i, step, RING, RING + 2)
                older_taps(i, 0)
                los(dve, first, i, step, RING + 2, CH + RING + (0 if last else 2))
                older_taps(i, 1)
                dve.wait_ge(gate_silu, i + 1)
                dve.tensor_tensor(product[:, :, :], conv[0], conv[1], ALU.mult).then_inc(gated, 1)
                if not last:
                    los(dve, first, i, step, CH + RING + 2, CH + RING + 4)
                dve.wait_ge(g_hi_done, FREE + i + 1)
                dve.tensor_tensor(g_lo[:, bass.ds(i * 4, 4), :], product[:, :, :], g_hi[:, bass.ds(i * 4, 4), :].bitcast(F32),
                                  ALU.subtract).then_inc(g_lo_done, 1)
                if not last:
                    los(dve, first, i, step, CH + RING + 4, 2 * CH + RING)

            los(dve, C_UP, 0, 0, RING, CH + RING)
            with dve.Fori(0, N_UP - 1) as i:
                up_and_gate(i, C_UP + CH, False)
            up_and_gate(N_UP - 1, C_UP + CH, True)
            n = FT // CK_T
            with dve.Fori(0, D // W // 2) as i:
                order = DOWN_ORDER
                mid = place(order, DOWN_TURN) + 1 + RING
                end = place(order, n) + RING
                los(dve, C_DOWN, i, len(order), RING, end, ADA_DOWN, 2)
                add_panel(ffn_added, i * len(order) + used(C_DOWN + end - RING), 0, i * 2 * W)
                los(dve, C_DOWN, i, len(order), end, mid, ADA_DOWN, 2)
                take_ada(dve, i * 2 + ADA_DOWN, 0, 5)
                los(dve, C_DOWN, i, len(order), mid, len(order) + RING, ADA_DOWN, 2)
                take_ada(dve, i * 2 + ADA_DOWN + 1, 0, 5)
                add_panel(ffn_added, i * len(order) + used(C_DOWN + len(order)), 1, i * 2 * W + W)
            def scales(layer, pre):
                v = adat[:, layer, :, :]
                dve.wait_ge(ada_taken, FREE + (layer + 1) * ADA_PANELS)
                dve.tensor_tensor(v, v, cols_of(V_ADA_B[layer], 3 * KT).unsqueeze(2).to_broadcast([P, 3 * KT, 2]), ALU.add)\
                   .then_inc(ada_biased, 1)
                dve.wait_ge(ada_biased, layer + 1)
                for s in range(2):
                    dve.scalar_tensor_tensor(hscale[:, s, :], adat[:, layer, KT:2 * KT, s], 1.0, cols_of(pre, KT),
                                             ALU.add, ALU.mult).then_inc(scales_ready, 1)

            def gate_diagonals(m, layer, post, n):
                for s in range(len(SPREAD[m])):
                    dve.tensor_tensor(hscale[:, s, :], adat[:, layer, 2 * KT:, s], cols_of(post, KT), ALU.mult)\
                       .then_inc(gains_ready, 1)
                dve.wait_ge(gains_ready, n)
                for s, v in enumerate(SPREAD[m]):
                    for k in range(KT):
                        ins = dve.tensor_scalar(v[:, k * P:(k + 1) * P], ident, hscale[:, s, k:k + 1], -1.0, ALU.mult, ALU.mult)
                    ins.then_inc(diag_ready[m], 1)

            def yout_join(m, targets):
                total, mean, root = y_stats[m]
                dve.wait_ge(yout_squared[m], len(YOUT[m]))
                dve.tensor_scalar(mean, total, 1.0 / D, EPS, ALU.mult, ALU.add).then_inc(yout_mean[m], 1)
                dve.wait_ge(yout_root[m], 1)
                for i, v in enumerate(YOUT[m]):
                    dve.wait_ge(gate_rows_ready[m], i // TT + 1)
                    dve.scalar_tensor_tensor(v, v, root[:, i:i + 1], SPREAD[m][i // TT], ALU.mult, ALU.mult)\
                       .then_inc(yout_scaled[m], 1)
                    dve.wait_ge(yout_scaled[m], i + 1)
                    dve.tensor_tensor(targets[i], targets[i], v, ALU.add).then_inc(yout_added[m], 1)

            scales(0, V_PRE0)
            dve.wait_ge(scales_ready, 2)
            norm_mean(dve, n_pool)
            norm_apply(dve, n_pool)
            norm_shift_lo(dve, n_pool)

            def pool_group(i, e):
                step, n = len(POOL_ORDER), i * 2 + e
                place_of = lambda j: place(POOL_ORDER, e * POOL_W + j)
                split = lambda a, b: los(dve, C_POOL, i, step, a, b, ADA_POOL, 6)
                ada0 = i * 6 + ADA_POOL + 3 * e
                split(place_of(0) + RING, place_of(CH) + 1)
                take_ada(dve, ada0, 1, 4)
                split(place_of(CH) + 1, place_of(CH + 2) + RING)
                for m in range(4):
                    dve.wait_ge(pt_hi_done, n * 4 + m + 1)
                    ins = dve.tensor_tensor(pt_lo[:, m, :], ps[:, m, :], pt_hi[:, m, :].bitcast(F32), ALU.subtract)
                ins.then_inc(pt_lo_done, 1)
                split(place_of(CH + 2) + RING, place_of(CH + 6) + RING)
                dve.wait_ge(chunks_used, i * step + used(C_POOL + place_of(CH + 5) + 1))
                for m in range(4):
                    ch = n * 4 + m
                    ins = dve.tensor_scalar(y[:, bass.ds(ch, 1), :].rearrange("p a b -> p (a b)"), ps[:, m, :],
                                            cols[:, bass.ds(ch + V_POOL_B[0] * P + V_POOL_B[1], 1)],
                                            cols[:, bass.ds(ch + V_POOL_S[0] * P + V_POOL_S[1], 1)], ALU.add, ALU.mult)
                ins.then_inc(grouped, 1)
                split(place_of(CH + 6) + RING, place_of(POOL_W) + 2)
                take_ada(dve, ada0 + 1, 1, 0, 0)
                take_ada(dve, ada0 + 2, 1, 0, 8)
                split(place_of(POOL_W) + 2, place_of(POOL_W) + RING)
                dve.wait_ge(grouped, FREE + n + 1)
                for m in range(4):
                    v = y[:, bass.ds(n * 4 + m, 1), :].rearrange("p a b -> p (a b)")
                    dve.wait_ge(gate_silu4, n * 4 + m + 1)
                    dve.tensor_tensor(v, v, gsilu[m % 2], ALU.mult).then_inc(y_gated, 1)

            with dve.Fori(0, POOL_G // 2) as i:
                for e in range(2):
                    pool_group(i, e)
            for k in range(KT):
                dve.wait_ge(y_hi_done, k + 1)
                dve.tensor_tensor(y_lo[:, k, :], y[:, k, :], y_hi[:, k, :].bitcast(F32), ALU.subtract).then_inc(y_lo_done, 1)
            gate_diagonals(0, 0, V_POST0, 2)
            with dve.Fori(0, D // W // 2) as i:
                los(dve, C_POOL_OUT, i, 2 * CH, RING, RING + 2 * CH)
            dve.wait_ge(ctx_again, 16)
            yout_join(0, [xres[:, i, :] for i in range(TT)] + [ctx_res[:, i, :] for i in range(TT)])
            scales(1, V_PRE1)
            dve.wait_ge(scales_ready, 4)
            norm_mean(dve, n_mla)
            norm_apply(dve, n_mla)
            norm_shift_lo(dve, n_mla)
            for n in range(3):
                los(dve, C_MLA + n * CH, 0, 0, RING, RING + CH)
                if n:
                    dve.wait_ge(chunks_used, used(C_MLA + (n + 1) * CH))
                    dve.tensor_copy(proj_c[:, :, (n - 1) * W_IN:n * W_IN], ps[:, 2 + 2 * n:4 + 2 * n, 0:W_IN])\
                       .then_inc(mla_ctx_taken, 1)
            with dve.Fori(0, 2) as i:
                los(dve, C_MLA + 3 * CH, i, 2 * CH, RING, RING + 2 * CH)
            dve.memset(kr[:, :, :, :], 0.0).then_inc(kr_cleared, 1)
            norm_mean(dve, n_cq)
            norm_mean(dve, n_ckv)
            norm_apply(dve, n_cq)
            norm_apply(dve, n_ckv)
            dve.wait_ge(mla_taken, PAIR + MLA_W // W_IN)
            dve.wait_ge(rope_loaded, 16)
            dve.wait_ge(mla_ctx_taken, 2)
            dve.wait_ge(kr_cleared, 1)
            for i in range(TT):
                x4 = proj_l[:, i, GATE0 - ROPE:GATE0].rearrange("p (r h n) -> p r h n", r=2, h=2)
                sin4 = rope[:, i, 1, :].rearrange("p (r h n) -> p r h n", r=2, h=2)
                for h in range(2):
                    dve.tensor_tensor(kr_t[:, i, :, h, :], x4[:, :, 1 - h, :], sin4[:, :, h, :], ALU.mult).then_inc(kr_swapped, 1)
                dve.tensor_tensor(kr[:, i, 0, 0:ROPE], proj_l[:, i, GATE0 - ROPE:GATE0], rope[:, i, 0, :], ALU.mult).then_inc(kr_swapped, 1)
                dve.wait_ge(kr_swapped, 3 * i + 3)
                for h in (1, 0):
                    dve.tensor_tensor(kr[:, i, h, h * ROPE:(h + 1) * ROPE], kr[:, i, 0, 0:ROPE],
                                      kr_t[:, i, :, :, :].rearrange("p r h n -> p (r h n)"), ALU.add).then_inc(kr_staged, 1)
                for h in range(2):
                    dve.tensor_copy(kr[:, TT + i, h, h * ROPE:(h + 1) * ROPE], proj_c[:, i, KVC:KVC + ROPE]).then_inc(kr_staged, 1)
            norm_lo(dve, n_cq)
            norm_lo(dve, n_ckv)

            def pair_rope(p):
                dve.wait_ge(q_nope_ready, p + 1)
                for tt in range(TT):
                    x3 = ps[:, tt, 0:2 * QH].rearrange("p (h e) -> p h e", h=2)[:, :, NOPE:]
                    x5 = x3.rearrange("p h (r a n) -> p h r a n", r=2, a=2)
                    o5 = q_swap[:, tt, :, :].rearrange("p h (r a n) -> p h r a n", r=2, a=2)
                    sin5 = rope[:, tt, 1, :].rearrange("p (r a n) -> p r a n", r=2, a=2)
                    for a in range(2):
                        dve.tensor_tensor(o5[:, :, :, a, :], x5[:, :, :, 1 - a, :],
                                          sin5[:, :, a, :].unsqueeze(1).to_broadcast([P, 2, 2, ROPE // 4]), ALU.mult)
                    dve.tensor_tensor(q_rope[:, tt, :, :], x3, rope[:, tt, 0, :].unsqueeze(1).to_broadcast([P, 2, ROPE]), ALU.mult)\
                       .then_inc(q_swapped, 1)
                dve.wait_ge(q_swapped, p * 2 + 2)
                dve.tensor_tensor(q_rope[:, :, :, :], q_rope[:, :, :, :], q_swap[:, :, :, :], ALU.add).then_inc(q_rope_ready, 1)

            def pair_kn_lo(p):
                dve.wait_ge(kn_hi_done, p + 1)
                dve.tensor_tensor(kn_lo[:, :, :], ps[:, 2:4, :], kn_hi[:, :, :].bitcast(F32), ALU.subtract).then_inc(kn_lo_done, 1)

            def pair_q_lo(p):
                dve.wait_ge(q_hi_done, p + 1)
                dve.tensor_tensor(qn_lo[:, :, :].rearrange("p a b -> p (a b)"), ps[:, 0, :],
                                  qn_hi[:, :, :].rearrange("p a b -> p (a b)").bitcast(F32), ALU.subtract)
                dve.tensor_tensor(qr_lo[:, :], ps[:, 1, 0:SEQ], qr_hi[:, :].bitcast(F32), ALU.subtract).then_inc(q_lo_done, 1)

            def pair_v(p):
                dve.wait_ge(chunks_used, p * 4 + used(C_HEADS + 4))
                dve.tensor_copy(v_sb[:, :, :].rearrange("p a b -> p (a b)"), ps[:, 2:4, :].rearrange("p a b -> p (a b)"))\
                   .then_inc(v_ready, 1)

            def pair_max(p):
                for m in range(4):
                    dve.wait_ge(mscored, p * 4 + m + 1)
                    dve.reduce_max(mmx[:, m:m + 1], ps[:, 4 + m, :], AX_X).then_inc(mmax_ready, 1)
                    dve.wait_ge(mmax_ready, p * 4 + m + 1)
                    dve.tensor_scalar(mnm[:, m:m + 1], mmx[:, m:m + 1], -MLA_SCALE, None, ALU.mult).then_inc(mneg_ready, 1)

            def pair_turned(p, ms):
                for m in ms:
                    dve.wait_ge(mexp_done, p * 4 + m + 1)
                    dve.reciprocal(mrec[:, m:m + 1], msum[:, m:m + 1]).then_inc(mrec_ready, 1)
                    dve.wait_ge(mp_turned, p * 4 + m + 1)
                    dve.tensor_copy(mprobs_t[:, m % 2, :, :].rearrange("p a b -> p (a b)"), ps[:, 4 + m, :]).then_inc(mpt_ready, 1)

            def pair_gate(p, ms):
                for m in ms:
                    h, tt = m // TT, m % TT
                    dve.wait_ge(mout_done, p * 4 + m + 1)
                    dve.wait_ge(mrec_ready, p * 4 + m + 1)
                    dve.scalar_tensor_tensor(om[:, m, :], ps[:, 4 + m, 0:VD], mrec[:, m:m + 1],
                                             proj_l[:, tt, bass.ds(p * 2 * VD + GATE0 + h * VD, VD)], ALU.mult, ALU.mult)\
                       .then_inc(om_ready, 1)

            def pair_out_lo(p):
                dve.wait_ge(om_hi_done, p + 1)
                v = om_hi[:, bass.ds(p * 2, 2), :].rearrange("p a b -> p (a b)")
                dve.tensor_tensor(om_lo[:, bass.ds(p * 2, 2), :].rearrange("p a b -> p (a b)"), ps[:, 7, :], v.bitcast(F32),
                                  ALU.subtract).then_inc(om_lo_done, 1)

            dve.wait_ge(kr_turned, 1)
            pair_rope(0)
            los(dve, C_HEADS, 0, 4, RING, RING + 2)
            pair_kn_lo(0)
            pair_q_lo(0)
            pair_v(0)
            los(dve, C_HEADS, 0, 4, RING + 2, RING + 4)
            dve.wait_ge(kr_hi_done, 1)
            dve.tensor_tensor(kr_lo[:, :, :], ps[:, 4:6, :], kr_hi[:, :, :].bitcast(F32), ALU.subtract).then_inc(kr_lo_done, 1)
            dve.wait_ge(gate_silu5, TT)
            with dve.Fori(0, PAIRS - 1) as i:
                pair_max(i)
                pair_turned(i, (0, 1))
                pair_rope(i + 1)
                los(dve, C_HEADS, i, 4, 2 * RING, 2 * RING + 2)
                pair_gate(i, (0, 1))
                pair_turned(i, (2, 3))
                pair_kn_lo(i + 1)
                pair_gate(i, (2, 3))
                pair_q_lo(i + 1)
                pair_v(i + 1)
                los(dve, C_HEADS, i, 4, 2 * RING + 2, 2 * RING + 4)
                pair_out_lo(i)
            pair_max(PAIRS - 1)
            for ms in ((0, 1), (2, 3)):
                pair_turned(PAIRS - 1, ms)
                pair_gate(PAIRS - 1, ms)
            pair_out_lo(PAIRS - 1)
            gate_diagonals(1, 1, V_POST1, 3)
            for n in range(D // W):
                los(dve, C_MLA_OUT + n * CH, 0, 0, RING, RING + CH)
            yout_join(1, [xres[:, i, :] for i in range(TT)])

        @block.tensor
        def _(pe):
            pe.sem_inc(chunks_used, RING)
            for s in (ada_turned, qk_turned, scored, p_turned, pv_done, b_summed):
                pe.sem_inc(s, PAIR)
            pe.wait_ge(consts_loaded, 16 * 3)
            pe.wait_ge(vecs_loaded, 16 * (len(VECS) + len(GAINS)))
            for v in range(VEC_TILES):
                mm = pe.transpose(ps[:, v // 4, (v % 4) * P:(v % 4 + 1) * P], vec_rows[:, v, :], ident)
            mm.then_inc(vecs_turned, 1)
            pe.wait_ge(table_loaded, 32)
            pe.wait_ge(consts_set, 4)
            pe.matmul(ps[0:HEADS_A, 2, 0:384], table[:, 0:HEADS_A], onehot[:, 0, :], start=True, stop=True)
            pe.matmul(ps[0:HEADS_C, 3, 0:384], table[:, HEADS_A:N_TAB], onehot[:, 1, :], start=True, stop=True).then_inc(ext_done, 1)
            norm_turn(pe, n_first)

            pe.wait_ge(ext_ready, 2)
            pe.wait_ge(n_first.lo_done, n_first.all_groups)
            with pe.Fori(0, IN_W // W_IN // IN_PANELS) as i:
                def ada_before(j):
                    for m, at in enumerate((IN_TURN, IN_PANELS * CH - 1)):
                        if j == at:
                            pe.wait_ge(lo_split, i * len(IN_ORDER) + C_IN + IN_ORDER.index((True, m * CH + CH - 1)) + RING + 1)
                            turn_ada(pe, i * 2 + m, m, 5)

                for q in range(IN_PANELS):
                    pe.wait_ge(proj_taken, i * IN_PANELS + q + 1)
                    panel_by_tokens(pe, C_IN, i, IN_ORDER, q * CH, h_hi, h_lo, pair(q % 2), W_IN, before=ada_before)

            def turn_qk(h):
                pe.wait_ge(staged, h.n * 2 + 2)
                pe.wait_ge(qk_ready, h.n + 1)
                for i in range(TT):
                    mm = pe.transpose(ps[:, h.slot, i * P:(i + 1) * P], stage[:, h.slot, i, :, :].rearrange("p a b -> p (a b)"), ident)
                mm.then_inc(qk_turned, 1)

            def scores(h):
                pe.wait_ge(qk_ready, h.n + PAIR + 1)
                pe.wait_ge(logits_ready, h.n + 1)
                q, k, bank = qkt[:, h.slot, 0, :], qkt[:, h.slot, 1, :], 2 + h.slot
                if h.kind == "b":
                    pe.matmul(ps[:, bank, 0:2 * P], k[:, 0:P], q, start=True, stop=True)
                    pe.matmul(ps[:, bank, 2 * P:3 * P], k[:, P:2 * P], q[:, P:2 * P], start=True, stop=True).then_inc(scored, 1)
                else:
                    pe.matmul(ps[:, bank, 0:P], q[:, 0:P], k[:, 0:P], start=True, stop=True)
                    pe.matmul(ps[:, bank, P:3 * P], q[:, P:2 * P], k, start=True, stop=True).then_inc(scored, 1)

            def soft_turn(h):
                pe.wait_ge(exp_done, h.n + PAIR + 1)
                pe.wait_ge(pt_ready, h.n + 1)
                for b in range(3):
                    mm = pe.transpose(ps[:, 4 + h.slot, b * P:(b + 1) * P], probs[:, h.slot, b * P:(b + 1) * P], ident)
                mm.then_inc(p_turned, 1)

            def head_out(h, weights):
                pe.wait_ge(out_taken, h.n + 1)
                v = [proj[:, i, bass.ds(h.v, HD)] for i in range(TT)]
                bank = 6 + h.slot
                pe.matmul(ps[:, bank, 0:HD], weights[:, 0:P], v[0], start=True, stop=True)
                pe.matmul(ps[:, bank, HD:2 * HD], weights[:, P:2 * P], v[0], start=True, stop=False)
                pe.matmul(ps[:, bank, HD:2 * HD], weights[:, 2 * P:3 * P], v[1], start=False, stop=True).then_inc(pv_done, 1)

            def step(h, two, three):
                soft_turn(h)
                scores(two)
                turn_qk(three)
                pe.wait_ge(pt_ready, h.n + PAIR + 1)
                head_out(h, probs_t[:, h.slot, :])

            turn_qk(head(0))
            turn_qk(head(1))
            scores(head(0))
            turn_qk(head(2))
            scores(head(1))
            soft_steps(pe, step)
            for m in range(N_SOFT + 2, N_HEADS):
                if m + 1 < N_HEADS:
                    turn_qk(head(m + 1))
                scores(head(m))

            def stick_sum(m):
                pe.wait_ge(b_soft, m // 2 + 1)
                pe.wait_ge(b_exponent, m + 1)
                bank = 4 + m % PAIR
                pe.matmul(ps[:, bank, 0:3 * P], stick[:, 3 * P:4 * P], b_w[:, m, :], start=True, stop=False)
                pe.matmul(ps[:, bank, P:2 * P], negones, b_w[:, m, 2 * P:3 * P], start=False, stop=True).then_inc(b_summed, 1)

            pe.wait_ge(pt_ready, PAIR + N_SOFT)
            for m in range(HEADS_B):
                stick_sum(m)
            for m in range(HEADS_B):
                pe.wait_ge(b_weights, m + 1)
                head_out(head(N_SOFT + m), b_w[:, m, :])
            norm_turn(pe, n_mix)

            pe.wait_ge(n_mix.lo_done, n_mix.all_groups)
            with pe.Fori(0, D // W // 2) as i:
                def ada_before(j):
                    if j == OUT_TURN:
                        pe.wait_ge(lo_split, i * len(OUT_ORDER) + C_OUT + OUT_ORDER.index((True, CH - 1)) + RING + 1)
                        turn_ada(pe, i + ADA_OUT, 1, 5)

                for half in range(2):
                    pe.wait_ge(attn_added, i * 2 + half + 1)
                    panel_by_tokens(pe, C_OUT, i, OUT_ORDER, half * CH, h_hi, h_lo, pair(half), W, before=ada_before)
            norm_turn(pe, n_ffn)
            pe.wait_ge(n_ffn.lo_done, n_ffn.all_groups)
            def turn_u(i, which):
                pe.wait_ge(u_staged[which], FREE + i + 1)
                pe.wait_ge(taps[1 - which], FREE + i * 2 + 2 * which)
                for m in range(4):
                    for tok in range(TT):
                        mm = pe.transpose(turned_u(m)[:, tok * P:(tok + 1) * P], ustage[:, which, tok, m * P:(m + 1) * P], ident)
                mm.then_inc(u_turned[which], 1)

            def gate_panel(i, first, j0, before=None):
                pe.wait_ge(u_staged[0], FREE + i)
                panel_by_tokens(pe, first, i - j0 // CH, UP_ORDER, j0, h_hi, h_lo, pair(0), W, before=before)

            def up_panel(i):
                pe.wait_ge(u_staged[1], FREE + i)
                panel_by_tokens(pe, C_UP + CH, i, UP_ORDER, 0, h_hi, h_lo, pair(1), W,
                                before=lambda j: turn_u(i, 0) if j == 2 else None)

            gate_panel(0, C_UP, 0)
            with pe.Fori(0, N_UP - 1) as i:
                up_panel(i)
                gate_panel(i + 1, C_UP + CH, CH, lambda j: turn_u(i, 1) if j == CH + 2 else None)
            up_panel(N_UP - 1)
            turn_u(N_UP - 1, 1)
            n = FT // CK_T
            with pe.Fori(0, D // W // 2) as i:
                def ada_before(j):
                    if j < n and j * CK_T % 4 == 0:
                        pe.wait_ge(g_lo_done, FREE + j * CK_T // 4 + 1)
                    for m, at in enumerate((DOWN_TURN, 2 * n - 1)):
                        if j == at:
                            pe.wait_ge(lo_split, i * len(DOWN_ORDER) + C_DOWN + DOWN_ORDER.index((True, m * CH + CH - 1)) + RING + 1)
                            turn_ada(pe, i * 2 + ADA_DOWN + m, m, 5)

                for half in range(2):
                    pe.wait_ge(ffn_added, i * 2 + half + 1)
                    panel_by_tokens(pe, C_DOWN, i, DOWN_ORDER, half * n, g_hi, g_lo, pair(half), W, FT, before=ada_before)
            norm_turn(pe, n_pool)
            pe.wait_ge(n_pool.lo_done, n_pool.all_groups)
            pe.wait_ge(poolm_loaded, 16)
            streams = [(i, i) for i in range(NT)]

            def pool_group(i, e):
                n, step = i * 2 + e, len(POOL_ORDER)
                ada0 = i * 6 + ADA_POOL + 3 * e

                def ada_done(m):
                    pe.wait_ge(lo_split, i * step + C_POOL + POOL_ORDER.index((True, (3 * e + m) * CH + CH - 1)) + RING + 1)

                def before(j):
                    if j == e * POOL_W + CH - 1:
                        ada_done(0)
                        pe.wait_ge(y_gated, FREE + n * 4)
                        turn_ada(pe, ada0, 3 * e % PAIR, 4)

                pe.wait_ge(grouped, FREE + n)
                pe.wait_ge(ada_taken, FREE + ada0)
                panel_by_tokens(pe, C_POOL, i, POOL_ORDER, e * POOL_W, h4_hi, h4_lo, streams, W, before=before)

                def chunk(j, *a):
                    at = C_POOL + place(POOL_ORDER, e * POOL_W + CH + j)
                    by_channels(pe, i * step + at, at % RING, *a, ada_behind(at))

                pe.wait_ge(ada_taken, FREE + ada0 + 1)
                for j in range(2):
                    chunk(j, h4_hi, h4_lo, CK_T * j, 4, j == 0, False)
                pe.wait_ge(u_ready, n + 1)
                for m in range(4):
                    for s in range(2):
                        for k in range(TT):
                            mm = pe.matmul(ps[:, m, s * SEQ:(s + 1) * SEQ], u[:, TT * s + k, m * P:(m + 1) * P],
                                           poolm[:, bass.ds(n, 1), k, :].rearrange("p a b -> p (a b)"),
                                           start=k == 0, stop=k == TT - 1)
                    mm.then_inc(pooled, 1)
                for j in range(2, 4):
                    chunk(j, h4_hi, h4_lo, CK_T * j, 4, False, False)
                pe.wait_ge(pt_lo_done, FREE + n + 1)
                for j in range(4, 6):
                    chunk(j, pt_hi, pt_lo, CK_T * (j - 4), 0, j == 4, j == 5)
                for j in range(6, 10):
                    if j == 9:
                        pe.wait_ge(grouped, FREE + n + 1)
                        for m in (1, 2):
                            ada_done(m)
                            turn_ada(pe, ada0 + m, (3 * e + m) % PAIR, 0, 8 * (m - 1))
                    chunk(j, h4_hi, h4_lo, CK_T * (j - 2), 4, False, j == 9)

            with pe.Fori(0, POOL_G // 2) as i:
                for e in range(2):
                    pool_group(i, e)
            pe.wait_ge(y_lo_done, KT)
            with pe.Fori(0, D // W // 2) as i:
                for half in range(2):
                    pe.wait_ge(yout_taken[0], i * 2 + half + 1)
                    panel_by_tokens(pe, C_POOL_OUT, i, PLAIN_ORDER, half * CH, y_hi, y_lo, [(n, 4 * half + n) for n in range(NT)], W)

            def spread_rows(m):
                pe.wait_ge(yout_taken[m], PAIR + D // W)
                for s, v in enumerate(SPREAD[m]):
                    pe.wait_ge(diag_ready[m], s + 1)
                    if s:
                        pe.wait_ge(gate_rows_ready[m], s)
                    for q in range(4):
                        mm = pe.matmul(ps[:, q, :], negones, v[:, q * W:(q + 1) * W], start=True, stop=True)
                    mm.then_inc(rows_spread[m], 1)

            spread_rows(0)
            norm_turn(pe, n_mla)
            pe.wait_ge(n_mla.lo_done, n_mla.all_groups)
            for n in range(3):
                pe.wait_ge(mla_taken, n + 1)
                ctx_too = [(TT + i, 2 + 2 * n + i) for i in range(TT)] if n else []
                panel_by_tokens(pe, C_MLA + n * CH, 0, PLAIN_ORDER, 0, k4_hi, k4_lo, pair(n % 2) + ctx_too, W_IN)
            with pe.Fori(0, 2) as i:
                for e in range(2):
                    pe.wait_ge(mla_taken, i * 2 + 4 + e)
                    panel_by_tokens(pe, C_MLA + 3 * CH, i, PLAIN_ORDER, e * CH, k4_hi, k4_lo, pair((3 + e) % 2), W_IN)
            norm_turn(pe, n_cq)
            pe.wait_ge(n_cq.lo_done, n_cq.all_groups)
            norm_turn(pe, n_ckv)

            def pair_queries(p, first, i):
                pe.wait_ge(q_lo_done, FREE + p)
                panel_by_tokens(pe, first, i, HEADS_ORDER, 0, cq_hi, cq_lo, pair(0), 2 * QH, RT)

            def pair_keys(p, h):
                if h == 0:
                    pe.wait_ge(lo_split, p * 4 + C_HEADS + RING + 4)
                    pe.wait_ge(v_ready, FREE + p)
                for k in range(RT):
                    for s, (w, a) in enumerate(((hi, ckv_hi), (hi, ckv_lo), (lo, ckv_hi))):
                        mm = pe.matmul(ps[:, 2 + h, :], w[:, 2 + k // CK_T, k % CK_T, h * 2 * P:h * 2 * P + P], a[:, k, :],
                                       start=k == 0 and s == 0, stop=k == RT - 1 and s == 2)
                if h == 1:
                    mm.then_inc(kn_summed, 1)

            def pair_turn(p):
                pe.wait_ge(q_nope_ready, p + 1)
                pe.wait_ge(q_rope_ready, p + 1)
                for h in range(2):
                    for tt in range(TT):
                        pe.transpose(ps[:, 0, h * SEQ + tt * P:h * SEQ + (tt + 1) * P], q_nope[:, tt, h, :], ident)
                for tt in range(TT):
                    mm = pe.transpose(ps[:, 1, tt * P:(tt + 1) * P], q_rope[:, tt, :, :].rearrange("p h e -> p (h e)"), ident)
                mm.then_inc(q_turned, 1)

            def pair_values(p):
                pe.wait_ge(kn_lo_done, p + 1)
                for n in range(NT):
                    for k in range(RT):
                        for s, (a, w) in enumerate(((ckv_hi, hi), (ckv_hi, lo), (ckv_lo, hi))):
                            v = w[:, 2 + k // CK_T, k % CK_T, :].rearrange("p (h e) -> p h e", h=2)[:, :, NOPE:]
                            mm = pe.matmul(ps[:, 2 + n // 2, (n % 2) * 2 * VD:(n % 2 + 1) * 2 * VD].rearrange("p (h e) -> p h e", h=2),
                                           a[:, k, n * P:(n + 1) * P], v, start=k == 0 and s == 0, stop=k == RT - 1 and s == 2)
                mm.then_inc(chunks_used, 2)

            def pair_scores(p):
                pe.wait_ge(q_lo_done, FREE + p + 1)
                pe.wait_ge(om_lo_done, FREE + p)
                for m in range(4):
                    h, q = m // TT, slice(m % TT * P, m % TT * P + P)
                    for s, (a, k) in enumerate(((qn_hi, kn_hi), (qn_hi, kn_lo), (qn_lo, kn_hi))):
                        pe.matmul(ps[:, 4 + m, :], a[:, h, q], k[:, h, :], start=s == 0, stop=False)
                    for s, (a, k) in enumerate(((qr_hi, kr_hi), (qr_hi, kr_lo), (qr_lo, kr_hi))):
                        mm = pe.matmul(ps[:, 4 + m, :], a[:, q], k[:, h, :], start=False, stop=s == 2)
                    mm.then_inc(mscored, 1)

            def pair_probs(p, ms):
                for m in ms:
                    pe.wait_ge(mexp_done, p * 4 + m + 1)
                    for k in range(NT):
                        mm = pe.transpose(ps[:, 4 + m, k * P:(k + 1) * P], mprobs[:, m, k * P:(k + 1) * P], ident)
                    mm.then_inc(mp_turned, 1)

            def pair_rows(p, ms):
                pe.wait_ge(v_ready, FREE + p + 1)
                for m in ms:
                    pe.wait_ge(mpt_ready, p * 4 + m + 1)
                    for k in range(NT):
                        mm = pe.matmul(ps[:, 4 + m, 0:VD], mprobs_t[:, m % 2, k, :], v_sb[:, k, m // TT * VD:(m // TT + 1) * VD],
                                       start=k == 0, stop=k == NT - 1)
                    mm.then_inc(mout_done, 1)

            def pair_columns(p):
                pe.wait_ge(om_ready, p * 4 + 4)
                for m in range(4):
                    mm = pe.transpose(ps[:, 7, m * P:(m + 1) * P], om[:, m, :], ident)
                mm.then_inc(om_turned, 1)

            pair_queries(0, C_HEADS, 0)
            pe.wait_ge(n_ckv.lo_done, n_ckv.all_groups)
            pe.wait_ge(kr_staged, 2 * NT)
            for h in range(2):
                for i in range(NT):
                    mm = pe.transpose(ps[:, 4 + h, i * P:(i + 1) * P], kr[:, i, h, :], ident)
            mm.then_inc(kr_turned, 1)
            pair_keys(0, 0)
            pair_keys(0, 1)
            pair_turn(0)
            pair_values(0)
            pe.wait_ge(kr_lo_done, 1)
            with pe.Fori(0, PAIRS - 1) as i:
                pair_scores(i)
                pair_queries(i + 1, C_HEADS + RING, i)
                pair_probs(i, (0, 1))
                pair_keys(i + 1, 0)
                pair_rows(i, (0, 1))
                pair_probs(i, (2, 3))
                pair_keys(i + 1, 1)
                pair_rows(i, (2, 3))
                pair_turn(i + 1)
                pair_values(i + 1)
                pair_columns(i)
            pair_scores(PAIRS - 1)
            for ms in ((0, 1), (2, 3)):
                pair_probs(PAIRS - 1, ms)
                pair_rows(PAIRS - 1, ms)
            pair_columns(PAIRS - 1)
            pe.wait_ge(om_lo_done, FREE + PAIRS)
            for n in range(D // W):
                pe.wait_ge(yout_taken[1], n + 1)
                panel_by_tokens(pe, C_MLA_OUT + n * CH, 0, PLAIN_ORDER, 0, om_hi, om_lo, pair(n % 2), W)
            spread_rows(1)


_OUTS = [((1, SEQ, D), "float32")]


def kernel(**inputs):
    import concourse.bacc as bacc
    from concourse.bass_utils import run_bass_kernel_spmd

    nc = bacc.Bacc("TRN2", target_bir_lowering=False, num_devices=1)
    arrays, t = {}, {}
    for name, a in inputs.items():
        a = np.ascontiguousarray(a)
        arrays[f"in_{name}"] = a
        t[name] = nc.dram_tensor(f"in_{name}", a.shape, mybir.dt.from_np(a.dtype), kind="ExternalInput").ap()
    consts = {name: nc.inline_tensor(a, name=f"const_{name}").ap() for name, a in shape_constants().items()}
    out = nc.dram_tensor("out", (1, SEQ, D), F32, kind="ExternalOutput").ap()
    two_block_kernel(nc, t, out, consts)
    r = run_bass_kernel_spmd(nc, [arrays], core_ids=[0])
    return r.results[0]["out"]
```

```python
import math
from contextlib import ExitStack

import numpy as np

import concourse.bass as bass
from concourse import mybir

F32 = mybir.dt.float32
F32R = mybir.dt.float32r
ALU = mybir.AluOpType
ACT = mybir.ActivationFunctionType
AX_X = mybir.AxisListType.X

P = 128
KIB = 1024
D = 2048
KT = D // P
SEQ = 256
TT = SEQ // P
NT = 2 * TT
HD = 64
HEADS_A, KV_A, HEADS_B, HEADS_C = 8, 2, 8, 16
IN_W = 5376
IN_HEADS = IN_W // HD
PANEL_HEADS = 448 // HD
AQ, AK, AV = 0, 512, 640
BQ, BK, BV = 768, 1280, 1792
CQ, CK, CV = 2304, 3328, 4352
D_FF = 5632
FT = D_FF // P
N_UP = D_FF // 512
N_BUCKETS, T5_MAX = 32, 2048
N_TAB = HEADS_A + HEADS_C
EPS = 1e-6
NEG = -1e30
W = 512
W_IN = 448
RING = 4
CK_T = 2
CH = KT // CK_T
PAIR = 2
SHIFT_BUFS = 4
FREE = 1
Q_RANK, KV_RANK, NOPE, ROPE, VD, MLA_H = 512, 512, 128, 64, 128, 16
RT = Q_RANK // P
MLA_W = Q_RANK + KV_RANK + ROPE + D
QH = NOPE + ROPE
MLA_ORDER = [0, 3, 1, 2, 4, 5, 6]
PAIRS = MLA_H // 2
POOL_G, POOL_WINDOWS = 4, (2, 4, 8, 16)
GRID_W = 64
MLA_SCALE = (NOPE + ROPE) ** -0.5
LAT, CTX = 0, 1

def turn_order(n_weights, ada_after):
    return [c for j in range(n_weights)
            for c in [(False, j)] + [(True, m) for m, after in enumerate(ada_after) if after == j]]


def evenly(n_weights, n_ada):
    return [RING + m * (n_weights - RING - 2) // n_ada for m in range(n_ada)]


NORM_PANELS = -(-CV // W_IN)
IN_PANELS = 4
UP_PAIRS = 2
POOL_W = 2 * CH + RT // CK_T
POOL_ADA = [RING + 3 * m // 4 for m in range(2 * CH)]
IN_ORDER = turn_order(IN_PANELS * CH, evenly(IN_PANELS * CH, CH))
UP_ORDER = turn_order(2 * UP_PAIRS * CH, evenly(2 * UP_PAIRS * CH, CH))
DOWN_ORDER = turn_order(2 * FT // CK_T, evenly(2 * FT // CK_T, 2 * CH))
POOL_ORDER = turn_order(2 * POOL_W, POOL_ADA + [POOL_W + j for j in POOL_ADA])
POOL_OUT_ORDER = turn_order(2 * CH, evenly(2 * CH, 2 * CH))
PANEL_ORDER = turn_order(CH, [])
PLAIN_ORDER = turn_order(2 * CH, [])
HEADS_ORDER = turn_order(2 * RT // CK_T, [])
IN_TURNS, UP_TURNS = IN_W // W_IN // IN_PANELS, (N_UP - 1) // UP_PAIRS
C_IN = 0
C_OUT = C_IN + IN_TURNS * len(IN_ORDER)
C_UP = C_OUT + D // W * CH
C_UP_LOOP = C_UP + CH
C_UP_LAST = C_UP_LOOP + UP_TURNS * len(UP_ORDER)
C_DOWN = C_UP_LAST + CH
C_POOL = C_DOWN + D // W // 2 * len(DOWN_ORDER)
C_POOL_OUT = C_POOL + POOL_G // 2 * len(POOL_ORDER)
C_MLA = C_POOL_OUT + D // W // 2 * len(POOL_OUT_ORDER)
C_HEADS = C_MLA + (MLA_W // W_IN) * CH
C_MLA_OUT = C_HEADS + (MLA_H // 2) * 4
N_CHUNKS = C_MLA_OUT + (D // W) * CH
ADA_PANELS = 3 * D // W
ADA_UP = IN_TURNS
ADA_DOWN = ADA_UP + UP_TURNS
ADA_POOL = ADA_DOWN + D // W
ADA_POOL_OUT = ADA_POOL + 2 * POOL_G
assert ADA_POOL == ADA_PANELS and ADA_POOL_OUT + D // W == 2 * ADA_PANELS
STREAM = (IN_ORDER * IN_TURNS + PLAIN_ORDER * (D // W // 2) + PANEL_ORDER + UP_ORDER * UP_TURNS + PANEL_ORDER
          + DOWN_ORDER * (D // W // 2) + POOL_ORDER * (POOL_G // 2) + POOL_OUT_ORDER * (D // W // 2))


IN_TURN, UP_TURN, DOWN_TURN, POOL_OUT_TURN = IN_PANELS * CH - 1, 2 * UP_PAIRS * CH - 1, FT // CK_T + 3, 2 * CH - 1


def is_ada(c):
    return c < len(STREAM) and STREAM[c][0]


def ada_behind(c):
    n = 0
    while is_ada(c + n + 1):
        n += 1
    return n


def place(order, j):
    return order.index((False, j)) if (False, j) in order else len(order)


VEC_TILES = 6
V_CONV = [(0, 0), (1, 0), (2, 0)]
V_CONV_B = (3, 0)
V_ATTN, V_FFN, V_QN, V_KVN = (0, 88), (0, 104), (0, 120), (0, 124)
V_MIX, V_PRE0 = (1, 88), (1, 104)
V_PRE1, V_POST0 = (2, 88), (2, 104)
V_POST1, V_POOL_B = (3, 88), (3, 104)
V_ADA_B, V_POOL_S = [(4, 0), (4, 48)], (4, 96)
V_GAINS = (4, 112)
V_C, V_CCTX = (5, 0), (5, 16)


def vectors(t):
    return ([(V_CONV[m], D_FF * 2 // P, t["conv_w"][0, m]) for m in range(3)]
            + [(V_CONV_B, D_FF * 2 // P, t["conv_b"][0]), (V_ATTN, KT, t["attn_norm"][0]), (V_FFN, KT, t["ffn_norm"][0]),
               (V_QN, RT, t["mla_q_norm_2"][0]), (V_KVN, RT, t["mla_kv_norm_2"][0]), (V_MIX, KT, t["mix_out_gain"][0]),
               (V_PRE0, KT, t["pre_norm_2"][0]), (V_PRE1, KT, t["pre_norm_2"][1]),
               (V_POST0, KT, t["post_norm_2"][0]), (V_POST1, KT, t["post_norm_2"][1]),
               (V_POOL_B, KT, t["pool_b_grp_2"][0].rearrange("g c -> (g c)")), (V_POOL_S, KT, t["pool_scale_2"][0]),
               (V_ADA_B[0], 3 * KT, t["ada_b_2"][0]), (V_ADA_B[1], 3 * KT, t["ada_b_2"][1]),
               (V_C, KT, t["c_2"][0]), (V_CCTX, KT, t["c_ctx_2"])])


GAINS = ["a_q_gain", "a_k_gain", "c_q_gain", "c_k_gain"]


def shape_constants():
    dist = 255 - np.arange(384)
    max_exact = N_BUCKETS // 2
    large = max_exact + (np.log(np.maximum(dist, 1).astype(np.float32) / np.float32(max_exact))
                         / np.float32(math.log(T5_MAX / max_exact)) * np.float32(N_BUCKETS - max_exact)).astype(np.int32)
    bucket = np.where(dist < max_exact, np.maximum(dist, 0), np.minimum(large, N_BUCKETS - 1))
    onehot = np.zeros((N_BUCKETS + 1, 2, 384), np.float32)
    seen_a = (dist >= 0) & (dist <= 127)
    times_c = np.where(dist >= 0, (dist <= 128).astype(int) + (dist % 4 == 0) + (dist % 16 == 0), 0)
    for n, seen in enumerate((seen_a, times_c > 0)):
        onehot[bucket[seen], n, np.nonzero(seen)[0]] = 1.0
    onehot[N_BUCKETS, 0] = np.where(seen_a, 0.0, NEG)
    onehot[N_BUCKETS, 1] = np.where(times_c > 0, np.log(np.maximum(times_c, 1)), NEG)
    i = np.arange(P)
    ident = np.concatenate([np.eye(P), -np.ones((P, P))], 1).astype(np.float32)
    before = np.where(i[:, None] < i[None, :], 0.0, NEG)
    stick = np.concatenate([before, np.zeros((P, P)), before, np.where(i[:, None] >= i[None, :], -1.0, 0.0)], 1)
    pool = np.zeros((POOL_G, SEQ, SEQ), np.float64)
    for g, win in enumerate(POOL_WINDOWS):
        left = win // 2
        right = win - 1 - left
        for t in range(SEQ):
            lo, hi = max(t - left, 0), min(t + right + 1, SEQ)
            pool[g, lo:hi, t] = 1.0 / (hi - lo)
            pool[g, t, t] -= 1.0
    pool = pool.reshape(POOL_G, TT, P, SEQ).transpose(2, 0, 1, 3)
    t = np.arange(SEQ)
    n = ROPE // 4
    freqs = np.float32(10000.0) ** (-np.arange(n, dtype=np.float32) / np.float32(n))
    ang = np.stack([(t // GRID_W).astype(np.float32)[:, None] * freqs, (t % GRID_W).astype(np.float32)[:, None] * freqs], 1)
    cos, sin = np.cos(ang), np.sin(ang)
    rope = np.stack([np.stack([cos, cos], 2), np.stack([-sin, sin], 2)], 1).reshape(TT, P, 2 * ROPE).transpose(1, 0, 2)
    f = lambda a: np.ascontiguousarray(a, dtype=np.float32)
    return {"onehot": f(onehot), "ident": ident, "stick": f(stick), "pool": f(pool), "rope": f(rope)}


class NormSignals:

    NAMES = ("squared", "mean", "root", "scaled", "turned", "shifted", "hi_done", "lo_done")

    def __init__(self, sem):
        self.squared, self.mean, self.root, self.scaled, self.turned, self.shifted, self.hi_done, self.lo_done = (
            sem(f"norm_{name}") for name in self.NAMES)
        self.rows = self.means = self.scaled_rows = self.groups = self.shifts = 0


class Norm:

    def __init__(self, sig, src, xn, stats, hi, lo, nk, scale, shift=None, tmp=None, own_means=False, parts=None, by_panels=None):
        self.src, self.xn, self.hi, self.lo, self.nk, self.scale, self.shift, self.tmp = src, xn, hi, lo, nk, scale, shift, tmp
        self.nt = len(src)
        self.parts = parts or [(0, self.nt)]
        self.by_panels = by_panels
        self.per = 4 // self.nt if self.nt <= 4 else 1
        self.groups = nk // self.per
        self.ss, self.ms, self.rstd = stats
        self.squared, self.mean, self.root, self.scaled = sig.squared, sig.mean, sig.root, sig.scaled
        self.turned, self.shifted, self.hi_done, self.lo_done = sig.turned, sig.shifted, sig.hi_done, sig.lo_done
        self.rows0, self.means0, self.scaled0, self.groups0, self.groups_shifted0 = (
            sig.rows, sig.means, sig.scaled_rows, sig.groups, sig.shifts)
        self.all_groups = self.groups0 + self.groups
        if not own_means:
            sig.rows += sum(b - a for part, (a, b) in enumerate(self.parts) if part != by_panels)
            sig.means += len(self.parts)
        sig.scaled_rows += self.nt
        sig.groups += self.groups
        sig.shifts += self.groups if shift else 0


def two_block_kernel(nc, t, out, consts):
    ctx = ExitStack()
    with ctx:
        sem = lambda name: ctx.enter_context(nc.semaphore(name))
        base = (nc.sbuf_base + 31) // 32 * 32
        fence_bytes = nc.sbuf_bytes_remaining - 64
        ctx.enter_context(nc.sbuf_tensor("fence", [P, fence_bytes // 4], F32))
        end = base + fence_bytes

        class Place:

            def __init__(self, at):
                self.at = at

            def __call__(self, name, shape, dtype=F32):
                size = 4
                for n in shape[1:]:
                    size *= n
                got = nc.alloc_sbuf_tensor_at(name, shape, dtype, offset=self.at)
                self.at += (size + 31) // 32 * 32
                assert self.at <= end, (name, self.at, end)
                return got

        keep = Place(base)
        raw = keep("raw", [P, RING, CK_T, W])
        hi = keep("hi", [P, RING, CK_T, W], F32R)
        lo = keep("lo", [P, RING, CK_T, W], F32R)
        xres = keep("xres", [P, TT, D])
        ident2 = keep("ident2", [P, 2 * P])
        ident, negones = ident2[:, 0:P], ident2[:, P:2 * P]
        cols = keep("cols", [P, VEC_TILES * P])
        adat = keep("adat", [P, 2, 3 * KT, 2])
        csil = keep("csil", [P, 2, KT])
        ada_acc = keep("ada_acc", [P, PAIR, 2, W])
        ss = keep("ss", [P, 16])
        ms = keep("ms", [P, 16])
        rstd = keep("rstd", [P, 16])
        halves = keep("halves", [P, TT * PANEL_HEADS])
        head_eps = keep("head_eps", [P, TT * PANEL_HEADS])
        hscale = keep("hscale", [P, 2, KT])
        gate_turned_rows = keep("gate_turned_rows", [2 * KT, P])
        panel_sums = keep("panel_sums", [P, NT, D // W])
        region = keep.at

        def at(kib):
            return Place(region + int(kib * KIB))

        pl = at(0)
        h_hi = pl("h_hi", [P, KT, SEQ], F32R)
        h_lo = pl("h_lo", [P, KT, SEQ], F32R)
        proj = pl("proj", [P, TT, IN_W])
        bias = pl("bias", [P, N_TAB, SEQ])
        stage = pl("stage", [P, PAIR, TT, 2, HD])
        qkt = pl("qkt", [HD, PAIR, 2, SEQ])
        logits = pl("logits", [P, PAIR, 3 * P])
        probs = pl("probs", [P, PAIR, 3 * P])
        probs_t = pl("probs_t", [P, PAIR, 3 * P])
        stick = pl("stick", [P, 4 * P])
        mx = pl("mx", [P, PAIR, TT])
        nm = pl("nm", [P, PAIR, TT])
        sums = pl("sums", [P, PAIR, TT])
        esink = pl("esink", [P, PAIR, TT])
        recip = pl("recip", [P, PAIR, TT])
        sinks = pl("sinks", [P, HEADS_A])
        gqk = pl("gqk", [HD, 2])
        hss = pl("hss", [P, TT, IN_HEADS])
        hrs = pl("hrs", [P, TT, IN_HEADS])
        vec_rows = pl("vec_rows", [P, VEC_TILES, P])
        onehot = pl("onehot", [N_BUCKETS + 1, 2, 384])
        table = pl("table", [N_BUCKETS + 1, N_TAB])
        ext = pl("ext", [HEADS_C, 2, 384])
        squares = pl("squares", [P, TT, W_IN])
        pb = at(0)
        b_z = pb("b_z", [P, HEADS_B, 3 * P])
        b_w = pb("b_w", [P, HEADS_B, 3 * P])
        xn_first = at(32)("xn_first", [P, TT, D])
        xn_mix = at(74)("xn_mix", [P, TT, D])
        xn_ffn = at(32)("xn_ffn", [P, TT, D])
        pl = at(32)
        g_hi = pl("g_hi", [P, FT, SEQ], F32R)
        g_lo = pl("g_lo", [P, FT, SEQ], F32R)
        ustage = pl("ustage", [P, 2, TT, W])
        conv = [ustage[:, w, :, :].rearrange("p a (b n) -> p (a b) n", n=SEQ) for w in range(2)]
        product = conv[0]
        y = at(0)("y", [P, KT, NT * P])
        xn4 = at(0)("xn4", [P, NT, D])
        pl = at(32)
        h4_hi = pl("h4_hi", [P, KT, NT * P], F32R)
        h4_lo = pl("h4_lo", [P, KT, NT * P], F32R)
        u = pl("u", [P, NT, W])
        pt_hi = pl("pt_hi", [P, 4, NT * P], F32R)
        pt_lo = pl("pt_lo", [P, 4, NT * P], F32R)
        poolm = pl("poolm", [P, POOL_G, TT, SEQ])
        gsilu = [u[:, m, :] for m in range(2)]
        shift_tmp = at(112)("shift_tmp", [P, SHIFT_BUFS, NT * P])
        y_hi = at(32)("y_hi", [P, KT, NT * P], F32R)
        y_lo = at(64)("y_lo", [P, KT, NT * P], F32R)
        ctx_res = at(0)("ctx_res", [P, TT, D])
        gate_rows = at(16)("gate_rows", [P, 2, D])
        yout = at(96)("yout", [P, NT, D])
        pl = at(64)
        proj_l = pl("proj_l", [P, TT, MLA_W])
        proj_c_at = pl.at
        proj_c = pl("proj_c", [P, TT, 2 * W_IN])
        k4_hi = at(0)("k4_hi", [P, KT, NT * P], F32R)
        k4_lo = at(32)("k4_lo", [P, KT, NT * P], F32R)
        xn4b = at(96)("xn4b", [P, NT, D])
        shift_tmpb = at(80)("shift_tmpb", [P, SHIFT_BUFS, NT * P])
        pl = at(96)
        cq_hi = pl("cq_hi", [P, RT, SEQ], F32R)
        cq_lo = pl("cq_lo", [P, RT, SEQ], F32R)
        ckv_hi = pl("ckv_hi", [P, RT, NT * P], F32R)
        ckv_lo = pl("ckv_lo", [P, RT, NT * P], F32R)
        rope = pl("rope", [P, TT, 2, ROPE])
        rot = pl.at
        kr = pl("kr", [P, NT, 2, P])
        kr_t = pl("kr_t", [P, TT, 2, 2, ROPE // 4])
        kr_lo = pl("kr_lo", [P, 2, NT * P], F32R)
        pl = Place(rot)
        q_rope = pl("q_rope", [P, TT, 2, ROPE])
        q_swap = pl("q_swap", [P, TT, 2, ROPE])
        mmx = pl("mmx", [P, 4])
        mnm = pl("mnm", [P, 4])
        msum = pl("msum", [P, 4])
        mrec = pl("mrec", [P, 4])
        pl = Place(proj_c_at)
        kr_hi = pl("kr_hi", [P, 2, NT * P], F32R)
        om = pl("om", [P, 4, VD])
        pl = at(0)
        om_hi = pl("om_hi", [P, MLA_H, SEQ], F32R)
        om_lo = pl("om_lo", [P, MLA_H, SEQ], F32R)
        q_nope = pl("q_nope", [P, TT, 2, NOPE])
        qn_hi = pl("qn_hi", [P, 2, SEQ], F32R)
        qn_lo = pl("qn_lo", [P, 2, SEQ], F32R)
        qr_hi = pl("qr_hi", [P, SEQ], F32R)
        qr_lo = pl("qr_lo", [P, SEQ], F32R)
        kn_hi = pl("kn_hi", [P, 2, NT * P], F32R)
        kn_lo = pl("kn_lo", [P, 2, NT * P], F32R)
        v_sb = pl("v_sb", [P, NT, 2 * VD])
        mprobs = pl("mprobs", [P, 4, NT * P])
        mprobs_t = pl("mprobs_t", [P, 2, NT, P])
        assert pl.at <= region + 64 * KIB
        yout2 = at(64)("yout2", [P, TT, D])
        gate_rows2 = at(96)("gate_rows2", [P, D])

        ps = ctx.enter_context(nc.psum_tensor("ps", [P, 8, W], F32))
        bias_rows = nc.dram_tensor("bias_rows", (N_TAB, P, 3 * P), F32).ap()
        gates = nc.dram_tensor("gates", (2, 2 * KT, P), F32).ap()

        def turned_u(m):
            return ps[:, 6 + m // 2, (m % 2) * SEQ:(m % 2 + 1) * SEQ]

        def col(vec, k):
            return cols[:, vec[0] * P + vec[1] + k:vec[0] * P + vec[1] + k + 1]

        def cols_of(vec, n):
            return cols[:, vec[0] * P + vec[1]:vec[0] * P + vec[1] + n]

        raw_loaded = [sem(f"raw_loaded{s}") for s in range(RING)]
        hi_split = sem("hi_split")
        lo_split = sem("lo_split")
        chunks_used = sem("chunks_used")
        x_loaded = [sem(f"x_loaded{i}") for i in range(TT)]
        consts_loaded, vecs_loaded = sem("consts_loaded"), sem("vecs_loaded")
        more_vecs_loaded = sem("more_vecs_loaded")
        vecs_cleared, vecs_turned, cols_ready = sem("vecs_cleared"), sem("vecs_turned"), sem("cols_ready")
        consts_set, table_loaded = sem("consts_set"), sem("table_loaded")
        c_silu = sem("c_silu")
        ext_done, ext_ready, bias_stored, bias_loaded = sem("ext_done"), sem("ext_ready"), sem("bias_stored"), sem("bias_loaded")
        proj_taken = sem("proj_taken")
        ada_added, ada_turned, ada_taken = sem("ada_added"), sem("ada_turned"), sem("ada_taken")
        heads_squared, heads_mean, heads_root, heads_scaled = (
            sem(n) for n in ("heads_squared", "heads_mean", "heads_root", "heads_scaled"))
        staged = sem("staged")
        qk_turned, qk_ready, scored, logits_ready, exp_done, p_turned, pt_ready, pv_done, out_taken = (
            sem(n) for n in ("qk_turned", "qk_ready", "scored", "logits_ready", "exp_done", "p_turned", "pt_ready", "pv_done", "out_taken"))
        max_ready, negmax_ready, den_ready, recip_ready = (sem(n) for n in ("max_ready", "negmax_ready", "den_ready", "recip_ready"))
        b_abs, b_exp, b_ln, b_soft, b_summed, b_exponent = (
            sem(n) for n in ("b_abs", "b_exp", "b_ln", "b_soft", "b_summed", "b_exponent"))
        b_weights = sem("b_weights")
        x_squared, x_summed = sem("x_squared"), sem("x_summed")
        attn_added, ffn_added = sem("attn_added"), sem("ffn_added")
        u_staged = [sem("gate_staged"), sem("up_staged")]
        u_turned = [sem("gate_turned"), sem("up_turned")]
        taps = [sem("gate_taps"), sem("up_taps")]
        tap2 = [sem("gate_tap2"), sem("up_tap2")]
        gate_silu, gated, g_hi_done, g_lo_done = sem("gate_silu"), sem("gated"), sem("g_hi_done"), sem("g_lo_done")

        stats = lambda a, n: (ss[:, a:a + n], ms[:, a:a + n], rstd[:, a:a + n])
        norm_signals = NormSignals(sem)
        n_first = Norm(norm_signals, [xres[:, i, :] for i in range(TT)], xn_first, stats(0, TT), h_hi, h_lo, KT,
                       lambda k, s: col(V_ATTN, k))
        MIX = [(AQ, HEADS_A * HD, 0), (CQ, HEADS_C * HD, 1024), (BQ, HEADS_B * HD, 512)]

        def load_chunk(sp, c, slot, src, width):
            sp.wait_ge(lo_split, c + 1)
            sp.dma_start(raw[:, slot, :, 0:width], src.rearrange("(k p) n -> p k n", p=P)).then_inc(raw_loaded[slot], 16)

        def load_panel(sp, c, slot0, w, col0, width, nk=KT):
            for j in range(nk // CK_T):
                load_chunk(sp, c + j, (slot0 + j) % RING, w[j * CK_T * P:(j + 1) * CK_T * P, bass.ds(col0, width)], width)

        def split_hi(act, c, slot, turn, ada):
            act.wait_ge(raw_loaded[slot], 16 * (turn + 1))
            act.wait_ge(chunks_used, c + 1)
            act.activation(hi[:, slot, :, :], raw[:, slot, :, :], ACT.Copy).then_inc(hi_split, 1 + ada)

        def split_lo(dve, c, slot):
            dve.wait_ge(hi_split, c + 1)
            dve.tensor_tensor(lo[:, slot, :, :], raw[:, slot, :, :], hi[:, slot, :, :].bitcast(F32),
                              ALU.subtract).then_inc(lo_split, 1)

        def his(act, first, i, step, a, b):
            for j in range(a, b):
                c = first + j
                if isinstance(i, int) and c + i * step >= N_CHUNKS:
                    continue
                if not is_ada(c):
                    split_hi(act, i * step + c, c % RING, i * (step // RING) + c // RING, ada_behind(c))

        def ada_chunk(dve, c, slot, turn, n, j, a, turned):
            dve.wait_ge(raw_loaded[slot], 16 * (turn + 1))
            done = (n * CH + j) * 3
            for k in range(CK_T):
                for v in range(2):
                    kt = j * CK_T + k
                    acc = ada_acc[:, a, v, :]
                    if kt == 0:
                        if v == 0:
                            dve.wait_ge(ada_turned, turned)
                        ins = dve.tensor_scalar(acc, raw[:, slot, k, :], csil[:, v, kt:kt + 1], None, ALU.mult)
                    else:
                        if k == 0 and v == 1:
                            dve.wait_ge(lo_split, c + RING)
                        else:
                            dve.wait_ge(ada_added, done + k + v)
                        ins = dve.scalar_tensor_tensor(acc, raw[:, slot, k, :], csil[:, v, kt:kt + 1], acc, ALU.mult, ALU.add)
                    ins.then_inc(lo_split if (k, v) == (CK_T - 1, 1) else ada_added, 1)

        def los(dve, first, i, step, a, b, ada0=0, ada_step=0, slot=None):
            for j in range(a, b):
                c = first + j
                if isinstance(i, int) and c + i * step >= N_CHUNKS:
                    continue
                if is_ada(c):
                    m = STREAM[c][1]
                    n = i * ada_step + ada0 + m // CH
                    ada_chunk(dve, i * step + c, c % RING, i * (step // RING) + c // RING, n, m % CH,
                              m // CH % PAIR if slot is None else slot, n + 1 if slot is None else n + 2)
                else:
                    split_lo(dve, i * step + c, c % RING)

        def by_tokens(pe, c, slot, a_hi, a_lo, kt0, outs, width, first, last, ada=0):
            pe.wait_ge(lo_split, c + RING + 1)
            for k in range(CK_T):
                for tok, bank in outs:
                    for s, (a, w) in enumerate(((a_hi, hi), (a_hi, lo), (a_lo, hi))):
                        mm = pe.matmul(ps[:, bank, 0:width], a[:, kt0 + k, tok * P:(tok + 1) * P], w[:, slot, k, 0:width],
                                       start=first and k == 0 and s == 0, stop=last and k == CK_T - 1 and s == 2)
            mm.then_inc(chunks_used, 1 + ada)

        def by_channels(pe, c, slot, a_hi, a_lo, kt0, bank0, first, last, ada=0):
            pe.wait_ge(lo_split, c + RING + 1)
            for k in range(CK_T):
                for n in range(W // P):
                    for s, (w, a) in enumerate(((hi, a_hi), (hi, a_lo), (lo, a_hi))):
                        mm = pe.matmul(ps[:, bank0 + n, :], w[:, slot, k, n * P:(n + 1) * P], a[:, kt0 + k, :],
                                       start=first and k == 0 and s == 0, stop=last and k == CK_T - 1 and s == 2)
            mm.then_inc(chunks_used, 1 + ada)

        def panel_by_tokens(pe, first, i, order, j0, a_hi, a_lo, outs, width, nk=KT, before=None):
            n = nk // CK_T
            for j in range(n):
                if before is not None:
                    before(j0 + j)
                at = first + place(order, j0 + j)
                by_tokens(pe, i * len(order) + at, at % RING, a_hi, a_lo, CK_T * j, outs, width, j == 0, j == n - 1, ada_behind(at))

        def turn_ada(pe, n, slots, bank):
            pe.wait_ge(ada_taken, n + FREE)
            for m, a in enumerate(slots):
                for q in range(W // P):
                    for v in range(2):
                        acc = ada_acc[:, a, v, q * P:(q + 1) * P]
                        at = (m * W // P + q) * 2 + v
                        mm = pe.matmul(ps[:, bank, at:at + 1], acc, negones[:, 0:1], start=True, stop=True)
            mm.then_inc(ada_turned, len(slots))

        def take_ada(dve, n, layer, bank, count=1):
            dve.wait_ge(ada_turned, n + count + PAIR)
            w = count * W // P
            dve.tensor_scalar(adat[:, layer, bass.ds((n - layer * ADA_PANELS) * 4, w), :],
                              ps[:, bank, 0:2 * w].rearrange("p (a b) -> p a b", b=2), -1.0, None, ALU.mult)\
               .then_inc(ada_taken, count)

        def pair(half):
            return [(i, PAIR * half + i) for i in range(TT)]

        def used(n):
            return RING + n

        def norm_squares(act, n, wait, part=0, junk=None):
            tiles = [i for p in n.parts for i in range(*p)]
            for i in range(*n.parts[part]):
                wait(act, i)
                if tiles.index(i):
                    act.wait_ge(n.squared, n.rows0 + tiles.index(i))
                w = P * n.nk
                to = ps[:, 4:4 + (w + W - 1) // W, :].rearrange("p a b -> p (a b)")[:, 0:w] if junk is None else junk
                act.activation(to, n.src[i], ACT.Square, accum_out=n.ss[:, i:i + 1]).then_inc(n.squared, 1)

        def panel_squares(act, done, norm, n):
            act.wait_ge(done, n + PAIR + 1)
            for tok in range(TT):
                count = n * TT + tok + norm * TT * (D // W)
                act.wait_ge(x_squared, count + FREE)
                act.activation(ps[:, 6, :], xres[:, tok, bass.ds(n * W, W)], ACT.Square, accum_out=panel_sums[:, tok, bass.ds(n, 1)])\
                   .then_inc(x_squared, 1)

        def norm_mean(dve, n, part=0):
            sl = slice(*n.parts[part])
            if part == n.by_panels:
                joined = [n_ffn, n_pool].index(n) + 1
                dve.wait_ge(x_squared, joined * TT * (D // W) + FREE)
                dve.reduce_sum(n.ss[:, sl], panel_sums[:, 0:TT, :], AX_X).then_inc(x_summed, 1)
                dve.wait_ge(x_summed, joined)
            else:
                dve.wait_ge(n.squared, n.rows0 + sum(b - a for a, b in n.parts[:part + 1]))
            dve.tensor_scalar(n.ms[:, sl], n.ss[:, sl], 1.0 / (P * n.nk), EPS, ALU.mult, ALU.add).then_inc(n.mean, 1)

        def norm_root(pool, n, part=0):
            sl = slice(*n.parts[part])
            pool.wait_ge(n.mean, n.means0 + part + 1)
            pool.tensor_tensor(n.rstd[:, sl], n.ms[:, sl], halves[:, sl], ALU.pow).then_inc(n.root, 1)

        def norm_apply(dve, n, part=0):
            dve.wait_ge(n.root, n.means0 + part + 1)
            for i in range(*n.parts[part]):
                dve.tensor_scalar(n.xn(i) if callable(n.xn) else n.xn[:, i, :], n.src[i], n.rstd[:, i:i + 1], None,
                                  ALU.mult).then_inc(n.scaled, 1)

        TURN_BANKS = 4

        def norm_turn(pe, n, first=0, end=None):
            for g in range(first, n.groups if end is None else end):
                if g == 0 and len(n.parts) > 1:
                    pe.wait_ge(n.scaled, n.scaled0 + n.nt)
                if g >= TURN_BANKS:
                    pe.wait_ge(n.lo_done, n.groups0 + g - TURN_BANKS + 1)
                for m in range(n.per):
                    for i in range(n.nt):
                        if g == 0 and m == 0 and len(n.parts) == 1:
                            pe.wait_ge(n.scaled, n.scaled0 + i + 1)
                        src = n.xn(i) if callable(n.xn) else n.xn[:, i, :]
                        k = g * n.per + m
                        mm = pe.transpose(ps[:, 4 + g % TURN_BANKS, (m * n.nt + i) * P:(m * n.nt + i + 1) * P],
                                          src[:, k * P:(k + 1) * P], ident)
                mm.then_inc(n.turned, 1)

        def norm_ahead(pe, n, j, needed=True):
            each = -(-(n.groups - TURN_BANKS) // (RING - 1))
            end = lambda j: min(TURN_BANKS + j * each, n.groups)
            if j < RING:
                norm_turn(pe, n, end(j - 1) if j else 0, end(j))
            if needed:
                pe.wait_ge(n.lo_done, n.groups0 + -(-(j + 1) * CK_T // n.per))

        def norm_parts(n, g):
            w = n.nt * P
            for m in range(n.per):
                yield g * n.per + m, ps[:, 4 + g % TURN_BANKS, m * w:(m + 1) * w]

        def norm_hi(act, n):
            for g in range(n.groups):
                if n.shift:
                    act.wait_ge(n.turned, n.groups0 + g + 1)
                    if g >= SHIFT_BUFS:
                        act.wait_ge(n.lo_done, n.groups0 + g - SHIFT_BUFS + 1)
                    for m in range(n.per):
                        for s in range(n.nt // TT):
                            sl = slice((m * n.nt + s * TT) * P, (m * n.nt + (s + 1) * TT) * P)
                            k = g * n.per + m
                            ins = act.activation(n.tmp[:, g % SHIFT_BUFS, sl], ps[:, 4 + g % TURN_BANKS, sl], ACT.Identity,
                                                 scale=n.scale(k, s), bias=n.shift(k, s))
                    ins.then_inc(n.shifted, 1)
                else:
                    act.wait_ge(n.turned, n.groups0 + g + 1)
                    for k, src in norm_parts(n, g):
                        ins = act.activation(n.hi[:, k, :], src, ACT.Identity, scale=n.scale(k, 0))
                    ins.then_inc(n.hi_done, 1)

        def norm_lo(dve, n):
            for g in range(n.groups):
                dve.wait_ge(n.turned, n.groups0 + g + 1)
                dve.wait_ge(n.hi_done, n.groups0 + g + 1)
                for k, src in norm_parts(n, g):
                    ins = dve.scalar_tensor_tensor(n.lo[:, k, :], src, n.scale(k, 0), n.hi[:, k, :].bitcast(F32),
                                                   ALU.mult, ALU.subtract)
                ins.then_inc(n.lo_done, 1)

        def norm_shift_split(dve, n):
            copy = lambda g: n.tmp[:, g % SHIFT_BUFS, :].rearrange("p (m n) -> p m n", m=n.per)
            part = lambda v, g: v[:, g * n.per:(g + 1) * n.per, :]

            def high(g):
                dve.wait_ge(n.shifted, n.groups_shifted0 + g + 1)
                dve.tensor_copy(part(n.hi, g), copy(g)).then_inc(n.hi_done, 1)

            high(0)
            for g in range(n.groups):
                if g + 1 < n.groups:
                    high(g + 1)
                dve.wait_ge(n.hi_done, n.groups0 + g + 1)
                dve.tensor_tensor(part(n.lo, g), copy(g), part(n.hi, g).bitcast(F32), ALU.subtract).then_inc(n.lo_done, 1)

        m_squared, m_mean, m_root = sem("mix_groups_squared"), sem("mix_groups_mean"), sem("mix_groups_root")
        n_mix = Norm(norm_signals, [xn_mix[:, i, :] for i in range(TT)], xn_mix, stats(2, 6), h_hi, h_lo, KT,
                     lambda k, s: col(V_MIX, k), own_means=True)
        n_ffn = Norm(norm_signals, [xres[:, i, :] for i in range(TT)], xn_ffn, stats(8, TT), h_hi, h_lo, KT,
                     lambda k, s: col(V_FFN, k), by_panels=0)

        N_SOFT = HEADS_A + HEADS_C
        N_HEADS = N_SOFT + HEADS_B

        class Head:

            def __init__(self, n, s, slot, kind, q, k, v, member):
                self.n, self.s, self.slot, self.kind, self.q, self.k, self.v, self.member = n, s, slot, kind, q, k, v, member

        def head(m, i=0):
            if m < HEADS_A:
                g = m // (HEADS_A // KV_A)
                return Head(m + HEADS_B, m, m % PAIR, "a", AQ + m * HD, AK + g * HD, AV + g * HD, m)
            if m < N_SOFT:
                c = m - HEADS_A
                return Head(i * 2 + m + HEADS_B, i * 2 + m, m % PAIR, "c",
                            i * 2 * HD + CQ + c * HD, i * 2 * HD + CK + c * HD, i * 2 * HD + CV + c * HD, c)

        def stick_head(b):
            return Head(b, N_SOFT + b, b % PAIR, "b", BQ + b * HD, BK + b * HD, BV + b * HD, b)

        lead = [stick_head(b) for b in range(HEADS_B)] + [head(m) for m in range(3)]
        pairs = [slice(2 * p, 2 * p + 2) for p in range(HEADS_B // 2)]
        C_LOOP = (HEADS_C - 4) // 2

        def soft_steps(eng, step):
            for m in range(HEADS_A):
                step(head(m), head(m + 2), head(m + 3))
            with eng.Fori(0, C_LOOP) as i:
                for m in range(HEADS_A, HEADS_A + 2):
                    step(head(m, i), head(m + 2, i), head(m + 3, i))
            for m in range(HEADS_A + 2 * C_LOOP, N_SOFT):
                step(head(m), head(m + 2), head(m + 3))

        ctx_loaded, poolm_loaded, ctx_again, rope_loaded = (
            sem(n) for n in ("ctx_loaded", "poolm_loaded", "ctx_again", "rope_loaded"))
        ada_biased, scales_ready, gains_ready = sem("ada_biased"), sem("scales_ready"), sem("gains_ready")
        u_ready, pooled, pt_hi_done, pt_lo_done, grouped, gate_silu4, y_gated = (
            sem(n) for n in ("u_ready", "pooled", "pt_hi_done", "pt_lo_done", "grouped", "gate_silu4", "y_gated"))
        y_hi_done, y_lo_done = sem("y_hi_done"), sem("y_lo_done")
        yout_taken = [sem("yout_taken"), sem("yout2_taken")]
        gates_turned, gates_out, gates_stored, gates_loaded = (
            sem(n) for n in ("gates_turned", "gates_out", "gates_stored", "gates_loaded"))
        yout_squared, yout_summed, yout_mean, yout_root, yout_added = (
            [sem(f"{n}{m}") for m in range(2)] for n in ("yout_squared", "yout_summed", "yout_mean", "yout_root", "yout_added"))
        mla_taken, mla_ctx_taken = sem("mla_taken"), sem("mla_ctx_taken")
        gate_silu5 = sem("gate_silu5")
        kr_cleared, kr_swapped, kr_staged, kr_turned, kr_hi_done, kr_lo_done = (
            sem(n) for n in ("kr_cleared", "kr_swapped", "kr_staged", "kr_turned", "kr_hi_done", "kr_lo_done"))
        q_nope_ready, q_swapped, q_rope_ready, q_turned, q_hi_done, q_lo_done = (
            sem(n) for n in ("q_nope_ready", "q_swapped", "q_rope_ready", "q_turned", "q_hi_done", "q_lo_done"))
        kn_summed, kn_hi_done, kn_lo_done, v_ready = (sem(n) for n in ("kn_summed", "kn_hi_done", "kn_lo_done", "v_ready"))
        mscored, mmax_ready, mneg_ready, mexp_done, mrec_ready = (
            sem(n) for n in ("mscored", "mmax_ready", "mneg_ready", "mexp_done", "mrec_ready"))
        mp_turned, mpt_ready, mout_done, om_ready, om_turned, om_hi_done, om_lo_done = (
            sem(n) for n in ("mp_turned", "mpt_ready", "mout_done", "om_ready", "om_turned", "om_hi_done", "om_lo_done"))
        out_stored = sem("out_stored")

        n_pool = Norm(norm_signals, [xres[:, i, :] for i in range(TT)] + [xn4[:, i, :] for i in range(TT, NT)], xn4, stats(0, NT),
                      h4_hi, h4_lo, KT, lambda k, s: hscale[:, s, k:k + 1], lambda k, s: adat[:, 0, k, s:s + 1], shift_tmp,
                      parts=[(TT, NT), (0, TT)], by_panels=1)
        n_mla, n_mla_ctx = (
            Norm(norm_signals, src, lambda i, s=s: xn4b[:, s * TT + i, :], stats(s * TT, TT), k4_hi[:, :, s * SEQ:(s + 1) * SEQ],
                 k4_lo[:, :, s * SEQ:(s + 1) * SEQ], KT, lambda k, _, s=s: hscale[:, s, k:k + 1],
                 lambda k, _, s=s: adat[:, 1, k, s:s + 1], shift_tmpb)
            for s, src in ((LAT, [xres[:, i, :] for i in range(TT)]), (CTX, [yout[:, i, :] for i in range(TT, NT)])))
        KVC = Q_RANK + KV_RANK - W_IN
        cq_rows = [proj_l[:, i, 0:Q_RANK] for i in range(TT)]
        ckv_rows = ([proj_l[:, i, Q_RANK:Q_RANK + KV_RANK] for i in range(TT)]
                    + [proj_c[:, i, Q_RANK - W_IN:KVC] for i in range(TT)])
        n_cq = Norm(norm_signals, cq_rows, lambda i: cq_rows[i], stats(4, TT), cq_hi, cq_lo, RT, lambda k, s: col(V_QN, k))
        n_ckv = Norm(norm_signals, ckv_rows, lambda i: ckv_rows[i], stats(8, NT), ckv_hi, ckv_lo, RT, lambda k, s: col(V_KVN, k))
        YOUT = [[yout[:, i, :] for i in range(NT)], [yout2[:, i, :] for i in range(TT)]]
        GATES = [[gate_rows[:, s, :] for s in range(2)], [gate_rows2[:, :]]]
        y_stats = [stats(0, NT), stats(4, TT)]
        GATE0 = Q_RANK + KV_RANK + ROPE

        VECS = vectors(t)
        ACT_VECS, SP_VECS, POOL_VECS = slice(0, 4), slice(4, 10), slice(10, None)
        block = ctx.enter_context(nc.Block())

        @block.sync
        def _(sp):
            for i in range(TT):
                sp.dma_start(xres[:, i, :], t["x"][0, i * P:(i + 1) * P, :]).then_inc(x_loaded[i], 16)
            sp.wait_ge(vecs_cleared, 1)
            for (tile, row), n, src in VECS[SP_VECS]:
                sp.dma_start(vec_rows[row:row + n, tile, :], src.rearrange("(r p) -> r p", p=P)).then_inc(vecs_loaded, 16)
            for m, name in enumerate(GAINS):
                r = V_GAINS[1] + m
                sp.dma_start(vec_rows[r:r + 1, V_GAINS[0], 0:HD], t[name]).then_inc(vecs_loaded, 16)

            def load_turn(first, i, order, weights, ada=None):
                for at, (of_ada, m) in enumerate(order):
                    c = first + at
                    if of_ada:
                        layer, col0 = ada
                        src, width = t["ada_w_2"][layer][m % CH * CK_T * P:(m % CH + 1) * CK_T * P,
                                                         bass.ds(col0 + m // CH * W, W)], W
                    else:
                        src, width = weights(m)
                    load_chunk(sp, i * len(order) + c, c % RING, src, width)

            def rows(w, j, col0, width):
                return w[j * CK_T * P:(j + 1) * CK_T * P, bass.ds(col0, width)], width

            def first_panels(i):
                load_turn(C_IN, i, IN_ORDER, lambda j: rows(t["w_in"][0], j % CH, (i * IN_PANELS + j // CH) * W_IN, W_IN), (0, i * W))

            first_panels(0)
            sp.wait_ge(bias_stored, 2 * 16)
            sp.dma_start(bias[:, :, :], bass.AP(bias_rows.tensor, P - 1, [[3 * P - 1, P], [3 * P * P, N_TAB], [1, SEQ]]))\
              .then_inc(bias_loaded, 16)
            with sp.Fori(1, IN_TURNS) as i:
                first_panels(i)
            with sp.Fori(0, D // W // 2) as i:
                load_turn(C_OUT, i, PLAIN_ORDER, lambda j: rows(t["w_out"][0], j % CH, i * 2 * W + j // CH * W, W))
            load_panel(sp, C_UP, 0, t["w_up"][0], 0, W)
            with sp.Fori(0, UP_TURNS) as i:
                load_turn(C_UP_LOOP, i, UP_ORDER,
                          lambda j: rows(t["w_up"][0], j % CH, (i * UP_PAIRS + (j // CH + 1) // 2) * W + (1 - j // CH % 2) * D_FF, W),
                          (0, (i + ADA_UP) * W))
            load_panel(sp, C_UP_LAST, 0, t["w_up"][0], 2 * D_FF - W, W)
            n = FT // CK_T
            with sp.Fori(0, D // W // 2) as i:
                load_turn(C_DOWN, i, DOWN_ORDER, lambda j: rows(t["w_down"][0], j % n, i * 2 * W + j // n * W, W),
                          (0, (i * 2 + ADA_DOWN) * W))
            def pool_weights(i, j):
                g, m = i * 2 + j // POOL_W, j % POOL_W
                if m < CH:
                    return rows(t["pool_w_in_2"][0], m, g * W, W)
                if m - CH in (4, 5):
                    r = (m - CH - 4) * CK_T * P
                    return t["pool_w_grp_2"][0, bass.ds(g, 1), r:r + CK_T * P, :].rearrange("g c d -> (g c) d"), W
                return rows(t["pool_w_in_2"][0], m - CH - 2 * (m - CH > 5), g * W + D, W)

            with sp.Fori(0, POOL_G // 2) as i:
                load_turn(C_POOL, i, POOL_ORDER, lambda j: pool_weights(i, j), (1, i * 4 * W))
            with sp.Fori(0, D // W // 2) as i:
                load_turn(C_POOL_OUT, i, POOL_OUT_ORDER, lambda j: rows(t["pool_w_out_2"][0], j % CH, i * 2 * W + j // CH * W, W),
                          (1, (i * 2 + ADA_POOL_OUT - ADA_PANELS) * W))
            for p, n in enumerate(MLA_ORDER):
                load_panel(sp, C_MLA + p * CH, 0, t["mla_w_in_2"][0], n * W_IN, W_IN)
            with sp.Fori(0, MLA_H // 2) as i:
                load_panel(sp, i * 4 + C_HEADS, 0, t["mla_w_uq_2"][0], i * 2 * QH, 2 * QH, RT)
                load_panel(sp, i * 4 + C_HEADS + 2, 2, t["mla_w_ukv_2"][0], i * W, W, RT)
            with sp.Fori(0, D // W) as i:
                load_panel(sp, i * CH + C_MLA_OUT, 0, t["mla_w_out_2"][0], i * W, W)
            for i in range(TT):
                sp.wait_ge(yout_added[1], i + 1)
                sp.dma_start(out[0, i * P:(i + 1) * P, :], xres[:, i, :]).then_inc(out_stored, 16)
            sp.wait_ge(out_stored, 16 * TT)

        @block.gpsimd
        def _(pool):
            pool.memset(vec_rows[:, :, :], 0.0).then_inc(vecs_cleared, 1)
            pool.wait_ge(vecs_cleared, 1)
            for (tile, row), n, src in VECS[POOL_VECS]:
                pool.dma_start(vec_rows[row:row + n, tile, :], src.rearrange("(r p) -> r p", p=P)).then_inc(more_vecs_loaded, 16)
            pool.wait_ge(consts_set, 4)
            norm_root(pool, n_first)
            by_head = lambda c: c[:, :].rearrange("p (t h) -> p t h", t=TT)
            with pool.Fori(0, NORM_PANELS) as n:
                some = bass.ds(n * PANEL_HEADS, PANEL_HEADS)
                pool.wait_ge(heads_squared, TT * (n + 1) + FREE)
                pool.tensor_tensor(hss[:, :, some], hss[:, :, some], by_head(head_eps), ALU.add).then_inc(heads_mean, 1)
                pool.wait_ge(heads_mean, n + 1)
                pool.tensor_tensor(hrs[:, :, some], hss[:, :, some], by_head(halves), ALU.pow).then_inc(heads_root, 1)

            def stage_head(h):
                pool.wait_ge(qk_turned, h.n + 1)
                for m, c0 in enumerate((h.q, h.k)):
                    pool.tensor_copy(stage[:, h.slot, :, m, :], proj[:, :, bass.ds(c0, HD)]).then_inc(staged, 1)

            for b in range(HEADS_B):
                stage_head(stick_head(b))
            pool.wait_ge(heads_scaled, TT)
            for m in range(HEADS_A):
                stage_head(head(m))
            pool.wait_ge(heads_scaled, 2 * TT)
            with pool.Fori(0, HEADS_C // 2) as i:
                for m in range(HEADS_A, HEADS_A + 2):
                    stage_head(head(m, i))
            for m, sl in enumerate((slice(0, 2 * TT), slice(2 * TT, 3 * TT))):
                pool.wait_ge(m_mean, m + 1)
                pool.tensor_tensor(n_mix.rstd[:, sl], n_mix.ms[:, sl], halves[:, sl], ALU.pow).then_inc(m_root, 1)
            norm_root(pool, n_ffn)
            for part in range(2):
                norm_root(pool, n_pool, part)

            def yout_roots(m):
                pool.wait_ge(yout_mean[m], 1)
                _, mean, root = y_stats[m]
                pool.tensor_tensor(root, mean, halves[:, 0:len(YOUT[m])], ALU.pow).then_inc(yout_root[m], 1)

            yout_roots(0)
            norm_root(pool, n_mla)
            norm_root(pool, n_mla_ctx)
            norm_root(pool, n_cq)
            norm_root(pool, n_ckv)
            yout_roots(1)

        @block.scalar
        def _(act):
            for dst, src in ((ident2, "ident"), (stick, "stick"), (onehot, "onehot")):
                act.dma_start(dst[:], consts[src]).then_inc(consts_loaded, 16)
            act.dma_start(table[0:N_BUCKETS, :], t["rel_bias_table"]).then_inc(table_loaded, 16)
            act.dma_start(sinks[:, :], bass.AP(t["a_sinks"].tensor, 0, [[0, P], [1, HEADS_A]])).then_inc(table_loaded, 16)
            act.wait_ge(vecs_cleared, 1)
            for (tile, row), n, src in VECS[ACT_VECS]:
                act.dma_start(vec_rows[row:row + n, tile, :], src.rearrange("(r p) -> r p", p=P)).then_inc(vecs_loaded, 16)
            act.sem_inc(proj_taken, PAIR)
            act.sem_inc(qk_ready, PAIR)
            act.sem_inc(exp_done, PAIR)
            act.sem_inc(yout_taken[0], PAIR)
            act.sem_inc(yout_taken[1], PAIR)
            act.sem_inc(mla_taken, PAIR)
            for s in (heads_squared, x_squared, u_staged[0], u_staged[1], g_hi_done):
                act.sem_inc(s, FREE)
            norm_squares(act, n_first, lambda e, i: e.wait_ge(x_loaded[i], 16))
            act.wait_ge(cols_ready, 3)
            act.activation(csil[:, :, :].rearrange("p a b -> p (a b)"), cols_of(V_C, 2 * KT), ACT.Silu).then_inc(c_silu, 1)
            act.wait_ge(consts_set, 4)
            his(act, C_IN, 0, 0, 0, RING)
            act.wait_ge(ext_ready, 2)
            for to, e, n in ((0, 0, HEADS_A), (HEADS_A, 1, HEADS_C)):
                act.dma_start(bias_rows[to:to + n, :, :], ext[0:n, e, :].unsqueeze(1).to_broadcast([n, P, 3 * P]))\
                   .then_inc(bias_stored, 16)
            norm_hi(act, n_first)

            def in_turn(i, squared_panels):
                for q in range(IN_PANELS):
                    step, at, end = len(IN_ORDER), place(IN_ORDER, q * CH), place(IN_ORDER, (q + 1) * CH)
                    his(act, C_IN, i, step, at + RING + (3 if q else 0), end + RING)
                    act.wait_ge(chunks_used, i * step + used(C_IN + end))
                    act.activation(proj[:, :, bass.ds((i * IN_PANELS + q) * W_IN, W_IN)], ps[:, 2 * (q % 2):2 * (q % 2) + 2, 0:W_IN],
                                   ACT.Copy).then_inc(proj_taken, 1)
                    if q >= squared_panels:
                        if q < IN_PANELS - 1:
                            his(act, C_IN, i, step, end + RING, end + RING + 3)
                        continue
                    n = i * IN_PANELS + q
                    act.wait_ge(proj_taken, n + PAIR + 1)
                    for tt in range(TT):
                        act.wait_ge(heads_squared, TT * n + tt + FREE)
                        for h in range(PANEL_HEADS):
                            ins = act.activation(squares[:, tt, h * HD:(h + 1) * HD], proj[:, tt, bass.ds(n * W_IN + h * HD, HD)],
                                                 ACT.Square, accum_out=hss[:, tt, bass.ds(n * PANEL_HEADS + h, 1)])
                        ins.then_inc(heads_squared, 1)
                        if tt == 0 and q < IN_PANELS - 1:
                            his(act, C_IN, i, step, end + RING, end + RING + 3)
            with act.Fori(0, IN_TURNS - 1) as i:
                in_turn(i, IN_PANELS)
            in_turn(IN_TURNS - 1, NORM_PANELS - (IN_TURNS - 1) * IN_PANELS)
            def turned(h):
                act.wait_ge(qk_turned, h.n + PAIR + 1)
                act.wait_ge(scored, h.n + 1)
                act.activation(qkt[:, h.slot, 0, :], ps[0:HD, h.slot, 0:SEQ], ACT.Identity,
                               scale=HD ** -0.5 if h.kind == "b" else gqk[:, int(h.kind == "c"):int(h.kind == "c") + 1])
                act.activation(qkt[:, h.slot, 1, :], ps[HD:2 * HD, h.slot, 0:SEQ], ACT.Identity).then_inc(qk_ready, 1)

            def soft_exp(h):
                act.wait_ge(negmax_ready, h.s + 1)
                act.wait_ge(p_turned, h.s + 1)
                act.wait_ge(recip_ready, h.s + 1)
                for i, sl in enumerate((slice(0, P), slice(P, 3 * P))):
                    ins = act.activation(probs[:, h.slot, sl], logits[:, h.slot, sl], ACT.Exp, bias=nm[:, h.slot, i:i + 1],
                                         accum_out=sums[:, h.slot, i:i + 1])
                    if h.kind == "a":
                        ins = act.activation(esink[:, h.slot, i:i + 1], sinks[:, h.member:h.member + 1], ACT.Exp,
                                             bias=nm[:, h.slot, i:i + 1])
                ins.then_inc(exp_done, 1)

            def stick_exp(p):
                sl = pairs[p]
                act.wait_ge(logits_ready, PAIR + 2 * p + 2)
                act.activation(b_w[:, sl, :], b_z[:, sl, :], ACT.Abs).then_inc(b_abs, 1)
                act.wait_ge(b_abs, p + 1)
                act.activation(b_w[:, sl, :], b_w[:, sl, :], ACT.Exp, scale=-1.0).then_inc(b_exp, 1)

            def stick_ln():
                for p, sl in enumerate(pairs):
                    act.wait_ge(b_exp, p + 1)
                    act.activation(b_w[:, sl, :], b_w[:, sl, :], ACT.Ln, bias=1.0).then_inc(b_ln, 1)

            def step(h, two, three):
                if three:
                    turned(three)
                if two:
                    soft_exp(two)
                if h.kind == "a":
                    if h.member < len(pairs):
                        stick_exp(h.member)
                    elif h.member == len(pairs):
                        stick_ln()

            act.wait_ge(cols_ready, 4)
            for h in lead[:-1]:
                turned(h)
            soft_exp(head(0))
            turned(lead[-1])
            soft_exp(head(1))
            soft_steps(act, step)

            def mix_squares(g, n):
                c0, w, _ = MIX[g]
                act.wait_ge(out_taken, PAIR + n)
                for i in range(TT):
                    at = TT * g + i
                    if at:
                        act.wait_ge(m_squared, at)
                    act.activation(ps[:, 0:2, :].rearrange("p a b -> p (a b)")[:, 0:w], proj[:, i, c0:c0 + w], ACT.Square,
                                   accum_out=n_mix.ss[:, at:at + 1]).then_inc(m_squared, 1)

            for m in range(HEADS_B):
                act.wait_ge(b_exponent, m + PAIR + 1)
                act.activation(b_w[:, m, :], b_z[:, m, :], ACT.Exp).then_inc(b_weights, 1)
                if m == 1:
                    mix_squares(0, HEADS_A)
                    mix_squares(1, N_SOFT)
            mix_squares(2, N_HEADS)
            norm_hi(act, n_mix)
            with act.Fori(0, D // W // 2) as i:
                for half in range(2):
                    his(act, C_OUT, i, 2 * CH, half * CH + RING, (half + 1) * CH + RING)
                    panel_squares(act, attn_added, 0, i * 2 + half)
            norm_hi(act, n_ffn)

            def stage_u(n, which, used_chunks):
                act.wait_ge(chunks_used, used_chunks)
                act.wait_ge(g_lo_done, FREE + n) if which == 0 else act.wait_ge(gated, FREE + n)
                act.activation(ustage[:, which, :, :], ps[:, 2 * which:2 * which + 2, :], ACT.Copy).then_inc(u_staged[which], 1)

            def tap_two(i, which):
                act.wait_ge(u_turned[which], i + 1)
                for m in range(4):
                    ch = i * 4 + which * FT + m
                    ins = act.activation(conv[which][:, m, :], turned_u(m), ACT.Identity,
                                         scale=cols[:, bass.ds(ch + V_CONV[2][0] * P + V_CONV[2][1], 1)],
                                         bias=cols[:, bass.ds(ch + V_CONV_B[0] * P + V_CONV_B[1], 1)])
                ins.then_inc(tap2[which], 1)

            def up_and_gate(n, first, i, order, j0, last):
                step = len(order)
                ahead = lambda j: place(order, j0 + j) + RING
                done = lambda j: i * step + used(first + place(order, j0 + j))
                his(act, first, i, step, ahead(0), ahead(2))
                tap_two(n, 0)
                his(act, first, i, step, ahead(2), ahead(CH))
                act.wait_ge(taps[0], FREE + n * 2 + 2)
                act.activation(conv[0], conv[0], ACT.Silu).then_inc(gate_silu, 1)
                stage_u(n, 1, done(CH))
                if not last:
                    his(act, first, i, step, ahead(CH), ahead(CH + 2))
                tap_two(n, 1)
                if not last:
                    his(act, first, i, step, ahead(CH + 2), ahead(CH + 5))
                act.wait_ge(gated, FREE + n + 1)
                act.activation(g_hi[:, bass.ds(n * 4, 4), :], product[:, :, :], ACT.Copy).then_inc(g_hi_done, 1)
                if not last:
                    his(act, first, i, step, ahead(CH + 5), ahead(2 * CH))
                    stage_u(n + 1, 0, done(2 * CH))

            his(act, C_UP, 0, 0, RING, CH + RING)
            stage_u(0, 0, used(C_UP + CH))
            with act.Fori(0, UP_TURNS) as i:
                for e in range(UP_PAIRS):
                    up_and_gate(i * UP_PAIRS + e, C_UP_LOOP, i, UP_ORDER, e * 2 * CH, False)
            up_and_gate(N_UP - 1, C_UP_LAST, 0, PANEL_ORDER, 0, True)
            act.dma_start(xn4[:, TT:, :], t["ctx_2"][0].rearrange("(t p) d -> p t d", p=P)).then_inc(ctx_loaded, 16)
            step, mid = len(DOWN_ORDER), place(DOWN_ORDER, FT // CK_T) + RING
            for i in range(D // W // 2):
                his(act, C_DOWN, i, step, RING, mid)
                panel_squares(act, ffn_added, 1, i * 2)
                his(act, C_DOWN, i, step, mid, step)
                if i == D // W // 2 - 1:
                    norm_squares(act, n_pool, lambda e, i: e.wait_ge(ctx_loaded, 16), 0, xn4[:, 0, :])
                his(act, C_DOWN, i, step, step, RING + step)
                panel_squares(act, ffn_added, 1, i * 2 + 1)
            act.wait_ge(ffn_added, PAIR + D // W)
            act.dma_start(poolm[:, :, :, :], consts["pool"]).then_inc(poolm_loaded, 16)
            act.wait_ge(scales_ready, 2)
            norm_hi(act, n_pool)

            def pool_group(i, e):
                step, n = len(POOL_ORDER), i * 2 + e
                ahead = lambda j: place(POOL_ORDER, e * POOL_W + j) + RING
                done = lambda j: i * step + used(C_POOL + place(POOL_ORDER, e * POOL_W + j) + 1)
                his(act, C_POOL, i, step, ahead(0), ahead(CH))
                act.wait_ge(chunks_used, done(CH - 1))
                act.wait_ge(y_gated, FREE + n * 4)
                act.activation(u[:, :, :], ps[:, 0:4, :], ACT.Copy).then_inc(u_ready, 1)
                his(act, C_POOL, i, step, ahead(CH), ahead(CH + 2))
                act.wait_ge(pt_lo_done, FREE + n)
                for m in range(4):
                    act.wait_ge(pooled, n * 4 + m + 1)
                    act.activation(pt_hi[:, m, :], ps[:, m, :], ACT.Copy).then_inc(pt_hi_done, 1)
                his(act, C_POOL, i, step, ahead(CH + 2), ahead(POOL_W))
                act.wait_ge(chunks_used, done(POOL_W - 1))
                for m in range(4):
                    act.wait_ge(y_gated, FREE + n * 4 + m - 1) if m >= 1 else act.wait_ge(y_gated, FREE + n * 4)
                    act.activation(gsilu[m % 2], ps[:, 4 + m, :], ACT.Silu).then_inc(gate_silu4, 1)

            with act.Fori(0, POOL_G // 2) as i:
                for e in range(2):
                    pool_group(i, e)
            for k in range(KT):
                act.wait_ge(y_gated, FREE + k + 1)
                act.activation(y_hi[:, k, :], y[:, k, :], ACT.Copy).then_inc(y_hi_done, 1)

            def gates_to_dram(layer):
                act.wait_ge(gates_turned, layer + 1)
                if layer:
                    act.wait_ge(gates_stored, 16)
                act.activation(gate_turned_rows[:, :], ps[0:2 * KT, 4 + 3 * layer, 0:P], ACT.Copy).then_inc(gates_out, 1)
                act.wait_ge(gates_out, layer + 1)
                act.dma_start(gates[layer], gate_turned_rows[:, :]).then_inc(gates_stored, 16)

            def gates_from_dram(layer):
                act.wait_ge(gates_stored, 16 * (layer + 1))
                for s, v in enumerate(GATES[layer]):
                    act.dma_start(v, bass.AP(gates.tensor, (layer * 2 + s) * D, [[0, P], [1, D]])).then_inc(gates_loaded, 16)

            gates_to_dram(0)
            act.wait_ge(y_lo_done, KT)
            gates_from_dram(0)
            act.dma_start(ctx_res[:, :, :], t["ctx_2"][0].rearrange("(t p) d -> p t d", p=P)).then_inc(ctx_again, 16)
            def yout_squares(m, n, bank0):
                for tok, v in enumerate(YOUT[m]):
                    act.activation(v[:, bass.ds(n * W, W)], ps[:, bank0 + tok, :], ACT.Square,
                                   accum_out=panel_sums[:, tok, bass.ds(n, 1)]).then_inc(yout_squared[m], 1)

            with act.Fori(0, D // W // 2) as i:
                step = len(POOL_OUT_ORDER)
                for half in range(2):
                    at, end = (place(POOL_OUT_ORDER, (half + m) * CH) for m in range(2))
                    his(act, C_POOL_OUT, i, step, at + RING, end + RING - half)
                    act.wait_ge(chunks_used, i * step + used(C_POOL_OUT + end))
                    yout_squares(0, i * 2 + half, 4 * half)
                    if half:
                        his(act, C_POOL_OUT, i, step, end + RING - 1, end + RING)

            norm_squares(act, n_mla, lambda e, i: e.wait_ge(yout_added[0], i + 1))
            act.wait_ge(scales_ready, 4)
            norm_hi(act, n_mla)

            def mla_his(p, a, b):
                his(act, C_MLA + p * CH, 0, 0, RING + a, RING + b)

            for p, n in enumerate(MLA_ORDER):
                if p == 1:
                    norm_hi(act, n_mla_ctx)
                    act.dma_start(rope[:, :, :, :].rearrange("p t a e -> p t (a e)"), consts["rope"]).then_inc(rope_loaded, 16)
                if p == 5:
                    mla_his(p, 0, 2)
                    norm_hi(act, n_cq)
                    mla_his(p, 2, 5)
                    norm_hi(act, n_ckv)
                    mla_his(p, 5, CH)
                else:
                    mla_his(p, 0, RING)
                    if p == 0:
                        act.wait_ge(n_mla.lo_done, n_mla.all_groups)
                        norm_squares(act, n_mla_ctx, lambda e, i: e.wait_ge(yout_added[0], NT))
                    if p == 4:
                        norm_squares(act, n_cq, lambda e, i: e.wait_ge(mla_ctx_taken, 2))
                        act.wait_ge(n_cq.squared, n_cq.rows0 + TT)
                        norm_squares(act, n_ckv, lambda e, i: None)
                    if p == 6:
                        act.wait_ge(kr_turned, 1)
                        act.activation(kr_hi[:, :, :], ps[:, 4:6, :], ACT.Copy).then_inc(kr_hi_done, 1)
                    mla_his(p, RING, CH)
                act.wait_ge(chunks_used, used(C_MLA + (p + 1) * CH))
                if p == 1:
                    act.wait_ge(n_mla_ctx.lo_done, n_mla_ctx.all_groups)
                act.activation(proj_l[:, :, n * W_IN:(n + 1) * W_IN], ps[:, 2 * (p % 2):2 * (p % 2) + 2, 0:W_IN], ACT.Copy)\
                   .then_inc(mla_taken, 1)
                if p == 2:
                    gates_to_dram(1)

            def pair_values(p, ahead, i=0):
                act.wait_ge(chunks_used, p * 4 + used(C_HEADS + 2))
                act.activation(q_nope[:, :, :, :], ps[:, 0:2, 0:2 * QH].rearrange("p t (h e) -> p t h e", h=2)[:, :, :, 0:NOPE],
                               ACT.Copy).then_inc(q_nope_ready, 1)
                his(act, C_HEADS, i, 4, ahead, ahead + 2)
                act.wait_ge(kn_summed, p + 1)
                act.activation(kn_hi[:, :, :], ps[:, 2:4, :], ACT.Copy).then_inc(kn_hi_done, 1)
                act.wait_ge(q_turned, p + 1)
                act.activation(qn_hi[:, :, :].rearrange("p a b -> p (a b)"), ps[:, 0, :], ACT.Copy)
                act.activation(qr_hi[:, :], ps[:, 1, 0:SEQ], ACT.Copy).then_inc(q_hi_done, 1)
                his(act, C_HEADS, i, 4, ahead + 2, ahead + 4)

            def pair_exps(p):
                for m in range(4):
                    act.wait_ge(mneg_ready, p * 4 + m + 1)
                    act.activation(mprobs[:, m, :], ps[:, 4 + m, :], ACT.Exp, scale=MLA_SCALE, bias=mnm[:, m:m + 1],
                                   accum_out=msum[:, m:m + 1]).then_inc(mexp_done, 1)

            def pair_out(p):
                act.wait_ge(om_turned, p + 1)
                act.activation(om_hi[:, bass.ds(p * 2, 2), :].rearrange("p a b -> p (a b)"), ps[:, 7, :], ACT.Copy)\
                   .then_inc(om_hi_done, 1)

            pair_values(0, RING)
            act.wait_ge(mla_taken, PAIR + len(MLA_ORDER))
            for i in range(TT):
                act.activation(proj_l[:, i, GATE0:], proj_l[:, i, GATE0:], ACT.Silu).then_inc(gate_silu5, 1)
            with act.Fori(0, PAIRS - 1) as i:
                pair_exps(i)
                pair_values(i + 1, 2 * RING, i)
                pair_out(i)
            pair_exps(PAIRS - 1)
            pair_out(PAIRS - 1)
            gates_from_dram(1)
            for n in range(D // W):
                his(act, C_MLA_OUT + n * CH, 0, 0, RING, RING + CH)
                act.wait_ge(chunks_used, used(C_MLA_OUT + (n + 1) * CH))
                yout_squares(1, n, 2 * (n % 2))

        @block.vector
        def _(dve):
            dve.sem_inc(lo_split, RING)
            for s in (logits_ready, pt_ready, out_taken, recip_ready, b_exponent, attn_added, ffn_added):
                dve.sem_inc(s, PAIR)
            for s in (ada_taken, taps[0], taps[1], gated, g_lo_done, pt_lo_done, grouped, y_gated, q_lo_done, v_ready, om_lo_done):
                dve.sem_inc(s, FREE)
            dve.memset(halves[:, :], -0.5).then_inc(consts_set, 1)
            dve.memset(head_eps[:, :], HD * EPS).then_inc(consts_set, 1)
            dve.memset(raw[:, :, :, W_IN:], 0.0).then_inc(consts_set, 1)
            dve.memset(table[N_BUCKETS:N_BUCKETS + 1, :], 1.0).then_inc(consts_set, 1)
            norm_mean(dve, n_first)
            norm_apply(dve, n_first)
            dve.wait_ge(vecs_turned, 1)
            dve.tensor_copy(cols[:, 4 * P:6 * P], ps[:, 1, 0:2 * P]).then_inc(cols_ready, 2)
            dve.tensor_copy(cols[:, 0:4 * P], ps[:, 0, :]).then_inc(cols_ready, 1)
            dve.wait_ge(cols_ready, 3)
            for m in range(2):
                g0 = V_GAINS[0] * P + V_GAINS[1] + 2 * m
                ins = dve.tensor_tensor(gqk[:, m:m + 1], cols[0:HD, g0:g0 + 1], cols[0:HD, g0 + 1:g0 + 2], ALU.mult)
            ins.then_inc(cols_ready, 1)
            dve.wait_ge(ext_done, 1)
            dve.tensor_copy(ext[0:HEADS_A, 0, :], ps[0:HEADS_A, 2, 0:384]).then_inc(ext_ready, 1)
            dve.tensor_copy(ext[:, 1, :], ps[0:HEADS_C, 3, 0:384]).then_inc(ext_ready, 1)
            los(dve, C_IN, 0, 0, 0, RING)
            norm_lo(dve, n_first)

            dve.wait_ge(c_silu, 1)
            with dve.Fori(0, IN_TURNS) as i:
                order = IN_ORDER
                los(dve, C_IN, i, len(order), RING, len(order) + RING, 0, 1, 0)
                take_ada(dve, i, 0, 5)
            dve.wait_ge(heads_root, NORM_PANELS)
            def scale_heads(c0, n, i):
                v = proj[:, i, c0:c0 + n * HD].rearrange("p (h e) -> p h e", e=HD)
                dve.tensor_tensor(v, v, hrs[:, i, c0 // HD:c0 // HD + n].unsqueeze(2).to_broadcast([P, n, HD]), ALU.mult)\
                   .then_inc(heads_scaled, 1)

            for i in range(TT):
                scale_heads(AQ, HEADS_A + KV_A, i)

            def soft_logits(h):
                slot, n, s = h.slot, h.n, h.s
                table = bias[:, bass.ds(s, 1), :].rearrange("p a b -> p (a b)")
                dve.wait_ge(scored, n + PAIR + 1)
                dve.wait_ge(exp_done, s + 1)
                dve.scalar_tensor_tensor(logits[:, slot, 0:P], ps[:, 2 + slot, 0:P], HD ** 0.5, table[:, P:2 * P], ALU.mult, ALU.add)
                dve.scalar_tensor_tensor(logits[:, slot, P:3 * P], ps[:, 2 + slot, P:3 * P], HD ** 0.5, table, ALU.mult, ALU.add)\
                   .then_inc(logits_ready, 1)
                dve.wait_ge(logits_ready, n + PAIR + 1)
                dve.reduce_max(mx[:, slot, 0:1], logits[:, slot, 0:P], AX_X)
                dve.reduce_max(mx[:, slot, 1:2], logits[:, slot, P:3 * P], AX_X).then_inc(max_ready, 1)
                dve.wait_ge(max_ready, s + 1)
                if h.kind == "a":
                    dve.tensor_scalar(nm[:, slot, :], mx[:, slot, :], sinks[:, h.member:h.member + 1], -1.0, ALU.max, ALU.mult)\
                       .then_inc(negmax_ready, 1)
                else:
                    dve.tensor_scalar(nm[:, slot, :], mx[:, slot, :], -1.0, None, ALU.mult).then_inc(negmax_ready, 1)

            def stick_z(h):
                dve.wait_ge(scored, h.n + PAIR + 1)
                dve.tensor_tensor(b_z[:, h.member, :], ps[:, 2 + h.slot, 0:3 * P], stick[:, 0:3 * P], ALU.add).then_inc(logits_ready, 1)

            def soft_turned(h):
                dve.wait_ge(p_turned, h.s + PAIR + 1)
                dve.wait_ge(pv_done, h.s + 1)
                dve.tensor_copy(probs_t[:, h.slot, :], ps[:, 4 + h.slot, 0:3 * P]).then_inc(pt_ready, 1)

            def soft_recip(h):
                dve.wait_ge(exp_done, h.s + PAIR + 1)
                if h.kind == "a":
                    dve.tensor_tensor(sums[:, h.slot, :], sums[:, h.slot, :], esink[:, h.slot, :], ALU.add).then_inc(den_ready, 1)
                    dve.wait_ge(den_ready, h.s + 1)
                dve.reciprocal(recip[:, h.slot, :], sums[:, h.slot, :]).then_inc(recip_ready, 1)

            def soft_out(h):
                dve.wait_ge(pv_done, h.s + PAIR + 1)
                dve.wait_ge(recip_ready, h.s + PAIR + 1)
                dve.tensor_tensor(proj[:, :, bass.ds(h.q, HD)], ps[:, 6 + h.slot, 0:2 * HD].rearrange("p (a b) -> p a b", a=2),
                                  recip[:, h.slot, :].unsqueeze(2).to_broadcast([P, TT, HD]), ALU.mult).then_inc(out_taken, 1)

            def stick_soft(p):
                sl = pairs[p]
                dve.wait_ge(b_ln, p + 1)
                dve.scalar_tensor_tensor(b_w[:, sl, :], b_z[:, sl, :], 0.0, b_w[:, sl, :], ALU.max, ALU.add).then_inc(b_soft, 1)

            def step(h, two, three):
                soft_recip(h)
                soft_turned(h)
                if two:
                    soft_logits(two)
                soft_out(h)
                if h.kind == "a" and h.member >= HEADS_A - len(pairs) // 2:
                    for p in range(2):
                        stick_soft((h.member - HEADS_A + len(pairs) // 2) * 2 + p)

            for b in range(HEADS_B):
                stick_z(stick_head(b))
                if b in (1, 3):
                    scale_heads(CQ, 2 * HEADS_C, b // 2)
            dve.wait_ge(bias_loaded, 16)
            soft_logits(head(0))
            soft_logits(head(1))
            soft_steps(dve, step)

            def mix_scale(g):
                c0, w, to = MIX[g]
                for i in range(TT):
                    ins = dve.tensor_scalar(xn_mix[:, i, to:to + w], proj[:, i, c0:c0 + w], n_mix.rstd[:, TT * g + i:TT * g + i + 1],
                                            None, ALU.mult)
                    if g == 2:
                        ins.then_inc(n_mix.scaled, 1)

            def mix_mean(groups):
                dve.wait_ge(m_squared, TT * (groups[-1] + 1))
                for g in groups:
                    sl = slice(TT * g, TT * (g + 1))
                    ins = dve.tensor_scalar(n_mix.ms[:, sl], n_mix.ss[:, sl], 1.0 / MIX[g][1], EPS, ALU.mult, ALU.add)
                ins.then_inc(m_mean, 1)

            for m in range(HEADS_B):
                dve.wait_ge(b_summed, m + PAIR + 1)
                dve.tensor_tensor(b_z[:, m, :], b_z[:, m, :], ps[:, 4 + m % PAIR, 0:3 * P], ALU.add).then_inc(b_exponent, 1)
            mix_mean((0, 1))
            for m in range(HEADS_B):
                h = stick_head(m)
                dve.wait_ge(pv_done, h.s + PAIR + 1)
                dve.tensor_copy(proj[:, :, h.q:h.q + HD], ps[:, 6 + h.slot, 0:2 * HD].rearrange("p (a b) -> p a b", a=2))\
                   .then_inc(out_taken, 1)
            dve.wait_ge(m_root, 1)
            mix_scale(0)
            mix_scale(1)
            mix_mean((2,))
            dve.wait_ge(m_root, 2)
            mix_scale(2)
            norm_lo(dve, n_mix)

            def add_panel(done, c, half, col0):
                dve.wait_ge(chunks_used, c)
                v = xres[:, :, bass.ds(col0, W)]
                dve.tensor_tensor(v, ps[:, 2 * half:2 * half + 2, :], v, ALU.add).then_inc(done, 1)

            with dve.Fori(0, D // W // 2) as i:
                for half in range(2):
                    end = (half + 1) * CH
                    los(dve, C_OUT, i, 2 * CH, half * CH + RING, end + RING - 1)
                    add_panel(attn_added, i * 2 * CH + used(C_OUT + end), half, i * 2 * W + half * W)
                    los(dve, C_OUT, i, 2 * CH, end + RING - 1, end + RING)
            norm_mean(dve, n_ffn)
            norm_apply(dve, n_ffn)
            norm_lo(dve, n_ffn)
            def older_taps(i, which):
                dve.wait_ge(tap2[which], i + 1)
                for back in (1, 2):
                    vec = V_CONV[2 - back]
                    for m in range(4):
                        ch = i * 4 + which * FT + m
                        ins = dve.scalar_tensor_tensor(conv[which][:, m, back:SEQ], turned_u(m)[:, 0:SEQ - back],
                                                       cols[:, bass.ds(ch + vec[0] * P + vec[1], 1)], conv[which][:, m, back:SEQ],
                                                       ALU.mult, ALU.add)
                    ins.then_inc(taps[which], 1)
                    dve.wait_ge(taps[which], FREE + i * 2 + back)

            def up_and_gate(n, first, i, order, j0, last):
                ahead = lambda j: place(order, j0 + j) + RING
                split = lambda a, b: los(dve, first, i, len(order), a, b, ADA_UP, 1, 1)
                split(ahead(0), ahead(2))
                older_taps(n, 0)
                split(ahead(2), ahead(CH) if last else ahead(CH + 2))
                older_taps(n, 1)
                dve.wait_ge(gate_silu, n + 1)
                dve.tensor_tensor(product[:, :, :], conv[0], conv[1], ALU.mult).then_inc(gated, 1)
                if not last:
                    split(ahead(CH + 2), ahead(CH + 4))
                dve.wait_ge(g_hi_done, FREE + n + 1)
                dve.tensor_tensor(g_lo[:, bass.ds(n * 4, 4), :], product[:, :, :], g_hi[:, bass.ds(n * 4, 4), :].bitcast(F32),
                                  ALU.subtract).then_inc(g_lo_done, 1)
                if not last:
                    split(ahead(CH + 4), ahead(2 * CH))

            los(dve, C_UP, 0, 0, RING, CH + RING)
            with dve.Fori(0, UP_TURNS) as i:
                for e in range(UP_PAIRS):
                    up_and_gate(i * UP_PAIRS + e, C_UP_LOOP, i, UP_ORDER, e * 2 * CH, False)
                take_ada(dve, i + ADA_UP, 0, 5)
            up_and_gate(N_UP - 1, C_UP_LAST, 0, PANEL_ORDER, 0, True)
            n = FT // CK_T
            for i in range(D // W // 2):
                order = DOWN_ORDER
                mid = place(order, DOWN_TURN) + 1 + RING
                end = place(order, n) + RING
                los(dve, C_DOWN, i, len(order), RING, end, ADA_DOWN, 2)
                add_panel(ffn_added, i * len(order) + used(C_DOWN + end - RING), 0, i * 2 * W)
                los(dve, C_DOWN, i, len(order), end, mid, ADA_DOWN, 2)
                take_ada(dve, i * 2 + ADA_DOWN, 0, 5)
                los(dve, C_DOWN, i, len(order), mid, len(order), ADA_DOWN, 2)
                if i == D // W // 2 - 1:
                    norm_mean(dve, n_pool, 0)
                    norm_apply(dve, n_pool, 0)
                los(dve, C_DOWN, i, len(order), len(order), len(order) + RING - 1)
                take_ada(dve, i * 2 + ADA_DOWN + 1, 0, 5)
                add_panel(ffn_added, i * len(order) + used(C_DOWN + len(order)), 1, i * 2 * W + W)
                los(dve, C_DOWN, i, len(order), len(order) + RING - 1, len(order) + RING)
            def scales(layer, pre):
                v = adat[:, layer, :, :]
                dve.wait_ge(ada_taken, FREE + (layer + 1) * ADA_PANELS)
                dve.tensor_tensor(v, v, cols_of(V_ADA_B[layer], 3 * KT).unsqueeze(2).to_broadcast([P, 3 * KT, 2]), ALU.add)\
                   .then_inc(ada_biased, 1)
                dve.wait_ge(ada_biased, layer + 1)
                for s in range(2):
                    dve.scalar_tensor_tensor(hscale[:, s, :], adat[:, layer, KT:2 * KT, s], 1.0, cols_of(pre, KT),
                                             ALU.add, ALU.mult).then_inc(scales_ready, 1)

            def gate_gains(layer, post):
                for s in range(2):
                    dve.tensor_tensor(hscale[:, s, :], adat[:, layer, 2 * KT:, s], cols_of(post, KT), ALU.mult)\
                       .then_inc(gains_ready, 1)

            def yout_gated(m, n, bank0):
                nt = len(YOUT[m])
                for tok in range(nt):
                    dve.wait_ge(yout_squared[m], n * nt + tok + 1)
                    ins = dve.tensor_tensor(YOUT[m][tok][:, bass.ds(n * W, W)], ps[:, bank0 + tok, :],
                                            GATES[m][tok // TT][:, bass.ds(n * W, W)], ALU.mult)
                ins.then_inc(yout_taken[m], 1)

            def yout_mean_square(m):
                total, mean, root = y_stats[m]
                nt = len(YOUT[m])
                dve.wait_ge(yout_squared[m], nt * (D // W))
                dve.reduce_sum(total, panel_sums[:, 0:nt, :], AX_X).then_inc(yout_summed[m], 1)
                dve.wait_ge(yout_summed[m], 1)
                dve.tensor_scalar(mean, total, 1.0 / D, EPS, ALU.mult, ALU.add).then_inc(yout_mean[m], 1)

            def yout_join(m, i, to, residual):
                dve.wait_ge(yout_taken[m], PAIR + D // W)
                dve.wait_ge(yout_root[m], 1)
                dve.scalar_tensor_tensor(to, YOUT[m][i], y_stats[m][2][:, i:i + 1], residual, ALU.mult, ALU.add)\
                   .then_inc(yout_added[m], 1)

            scales(0, V_PRE0)
            norm_mean(dve, n_pool, 1)
            norm_apply(dve, n_pool, 1)
            norm_shift_split(dve, n_pool)
            gate_gains(0, V_POST0)

            def pool_group(i, e):
                step, n = len(POOL_ORDER), i * 2 + e
                place_of = lambda j: place(POOL_ORDER, e * POOL_W + j)
                split = lambda a, b: los(dve, C_POOL, i, step, a, b, ADA_POOL, 4)
                ada0 = i * 4 + ADA_POOL + 2 * e
                split(place_of(0) + RING, place_of(CH + 2) + RING)
                for m in range(4):
                    dve.wait_ge(pt_hi_done, n * 4 + m + 1)
                    ins = dve.tensor_tensor(pt_lo[:, m, :], ps[:, m, :], pt_hi[:, m, :].bitcast(F32), ALU.subtract)
                ins.then_inc(pt_lo_done, 1)
                split(place_of(CH + 2) + RING, place_of(CH + 6) + RING)
                dve.wait_ge(chunks_used, i * step + used(C_POOL + place_of(CH + 5) + 1))
                for m in range(4):
                    ch = n * 4 + m
                    ins = dve.tensor_scalar(y[:, bass.ds(ch, 1), :].rearrange("p a b -> p (a b)"), ps[:, m, :],
                                            cols[:, bass.ds(ch + V_POOL_B[0] * P + V_POOL_B[1], 1)],
                                            cols[:, bass.ds(ch + V_POOL_S[0] * P + V_POOL_S[1], 1)], ALU.add, ALU.mult)
                ins.then_inc(grouped, 1)
                split(place_of(CH + 6) + RING, place_of(POOL_W) + 2)
                take_ada(dve, ada0, 1, 0, PAIR)
                split(place_of(POOL_W) + 2, place_of(POOL_W) + RING)
                dve.wait_ge(grouped, FREE + n + 1)
                for m in range(4):
                    v = y[:, bass.ds(n * 4 + m, 1), :].rearrange("p a b -> p (a b)")
                    dve.wait_ge(gate_silu4, n * 4 + m + 1)
                    dve.tensor_tensor(v, v, gsilu[m % 2], ALU.mult).then_inc(y_gated, 1)

            with dve.Fori(0, POOL_G // 2) as i:
                for e in range(2):
                    pool_group(i, e)
            for k in range(KT):
                dve.wait_ge(y_hi_done, k + 1)
                dve.tensor_tensor(y_lo[:, k, :], y[:, k, :], y_hi[:, k, :].bitcast(F32), ALU.subtract).then_inc(y_lo_done, 1)
            for i in range(D // W // 2):
                step = len(POOL_OUT_ORDER)
                mid = place(POOL_OUT_ORDER, CH) + RING
                los(dve, C_POOL_OUT, i, step, RING, mid, ADA_POOL_OUT, 2)
                dve.wait_ge(gates_loaded, 16 * 2)
                yout_gated(0, i * 2, 0)
                los(dve, C_POOL_OUT, i, step, mid, step + 2, ADA_POOL_OUT, 2)
                take_ada(dve, i * 2 + ADA_POOL_OUT, 1, 0, PAIR)
                los(dve, C_POOL_OUT, i, step, step + 2, step + RING - 1)
                yout_gated(0, i * 2 + 1, 4)
                if i == D // W // 2 - 1:
                    yout_mean_square(0)
                los(dve, C_POOL_OUT, i, step, step + RING - 1, step + RING)
            scales(1, V_PRE1)
            for i in range(TT):
                yout_join(0, i, xres[:, i, :], xres[:, i, :])
            dve.wait_ge(ctx_again, 16)
            yout_join(0, TT, yout[:, TT, :], ctx_res[:, 0, :])
            norm_mean(dve, n_mla)
            yout_join(0, TT + 1, yout[:, TT + 1, :], ctx_res[:, 1, :])
            norm_apply(dve, n_mla)
            norm_shift_split(dve, n_mla)

            def mla_los(p, a, b):
                los(dve, C_MLA + p * CH, 0, 0, RING + a, RING + b)

            mla_los(0, 0, RING)
            norm_mean(dve, n_mla_ctx)
            norm_apply(dve, n_mla_ctx)
            mla_los(0, RING, CH)
            norm_shift_split(dve, n_mla_ctx)
            gate_gains(1, V_POST1)
            dve.memset(kr[:, :, :, :], 0.0).then_inc(kr_cleared, 1)
            mla_los(1, 0, CH)
            for p in (2, 3):
                mla_los(p, 0, CH)
                n = MLA_ORDER[p]
                dve.wait_ge(chunks_used, used(C_MLA + (p + 1) * CH))
                dve.tensor_copy(proj_c[:, :, (n - 1) * W_IN:n * W_IN], ps[:, 2 + 2 * n:4 + 2 * n, 0:W_IN])\
                   .then_inc(mla_ctx_taken, 1)
            mla_los(4, 0, RING)
            norm_mean(dve, n_cq)
            norm_mean(dve, n_ckv)
            norm_apply(dve, n_cq)
            norm_apply(dve, n_ckv)
            mla_los(4, RING, CH)
            mla_los(5, 0, 2)
            norm_lo(dve, n_cq)
            mla_los(5, 2, 5)
            norm_lo(dve, n_ckv)
            mla_los(5, 5, CH)
            dve.wait_ge(mla_taken, PAIR + 4)
            dve.wait_ge(rope_loaded, 16)
            dve.wait_ge(mla_ctx_taken, 2)
            dve.wait_ge(kr_cleared, 1)
            for i in range(TT):
                x4 = proj_l[:, i, GATE0 - ROPE:GATE0].rearrange("p (r h n) -> p r h n", r=2, h=2)
                sin4 = rope[:, i, 1, :].rearrange("p (r h n) -> p r h n", r=2, h=2)
                for h in range(2):
                    dve.tensor_tensor(kr_t[:, i, :, h, :], x4[:, :, 1 - h, :], sin4[:, :, h, :], ALU.mult).then_inc(kr_swapped, 1)
                dve.tensor_tensor(kr[:, i, 0, 0:ROPE], proj_l[:, i, GATE0 - ROPE:GATE0], rope[:, i, 0, :], ALU.mult).then_inc(kr_swapped, 1)
                dve.wait_ge(kr_swapped, 3 * i + 3)
                for h in (1, 0):
                    dve.tensor_tensor(kr[:, i, h, h * ROPE:(h + 1) * ROPE], kr[:, i, 0, 0:ROPE],
                                      kr_t[:, i, :, :, :].rearrange("p r h n -> p (r h n)"), ALU.add).then_inc(kr_staged, 1)
                for h in range(2):
                    dve.tensor_copy(kr[:, TT + i, h, h * ROPE:(h + 1) * ROPE], proj_c[:, i, KVC:KVC + ROPE]).then_inc(kr_staged, 1)
            mla_los(6, 0, CH)

            def pair_rope(p):
                dve.wait_ge(q_nope_ready, p + 1)
                for tt in range(TT):
                    x3 = ps[:, tt, 0:2 * QH].rearrange("p (h e) -> p h e", h=2)[:, :, NOPE:]
                    x5 = x3.rearrange("p h (r a n) -> p h r a n", r=2, a=2)
                    o5 = q_swap[:, tt, :, :].rearrange("p h (r a n) -> p h r a n", r=2, a=2)
                    sin5 = rope[:, tt, 1, :].rearrange("p (r a n) -> p r a n", r=2, a=2)
                    for a in range(2):
                        dve.tensor_tensor(o5[:, :, :, a, :], x5[:, :, :, 1 - a, :],
                                          sin5[:, :, a, :].unsqueeze(1).to_broadcast([P, 2, 2, ROPE // 4]), ALU.mult)
                    dve.tensor_tensor(q_rope[:, tt, :, :], x3, rope[:, tt, 0, :].unsqueeze(1).to_broadcast([P, 2, ROPE]), ALU.mult)\
                       .then_inc(q_swapped, 1)
                dve.wait_ge(q_swapped, p * 2 + 2)
                dve.tensor_tensor(q_rope[:, :, :, :], q_rope[:, :, :, :], q_swap[:, :, :, :], ALU.add).then_inc(q_rope_ready, 1)

            def pair_kn_lo(p):
                dve.wait_ge(kn_hi_done, p + 1)
                dve.tensor_tensor(kn_lo[:, :, :], ps[:, 2:4, :], kn_hi[:, :, :].bitcast(F32), ALU.subtract).then_inc(kn_lo_done, 1)

            def pair_q_lo(p):
                dve.wait_ge(q_hi_done, p + 1)
                dve.tensor_tensor(qn_lo[:, :, :].rearrange("p a b -> p (a b)"), ps[:, 0, :],
                                  qn_hi[:, :, :].rearrange("p a b -> p (a b)").bitcast(F32), ALU.subtract)
                dve.tensor_tensor(qr_lo[:, :], ps[:, 1, 0:SEQ], qr_hi[:, :].bitcast(F32), ALU.subtract).then_inc(q_lo_done, 1)

            def pair_v(p):
                dve.wait_ge(chunks_used, p * 4 + used(C_HEADS + 4))
                dve.tensor_copy(v_sb[:, :, :].rearrange("p a b -> p (a b)"), ps[:, 2:4, :].rearrange("p a b -> p (a b)"))\
                   .then_inc(v_ready, 1)

            def pair_max(p):
                for m in range(4):
                    dve.wait_ge(mscored, p * 4 + m + 1)
                    dve.reduce_max(mmx[:, m:m + 1], ps[:, 4 + m, :], AX_X).then_inc(mmax_ready, 1)
                    dve.wait_ge(mmax_ready, p * 4 + m + 1)
                    dve.tensor_scalar(mnm[:, m:m + 1], mmx[:, m:m + 1], -MLA_SCALE, None, ALU.mult).then_inc(mneg_ready, 1)

            def pair_turned(p, ms):
                for m in ms:
                    dve.wait_ge(mexp_done, p * 4 + m + 1)
                    dve.reciprocal(mrec[:, m:m + 1], msum[:, m:m + 1]).then_inc(mrec_ready, 1)
                    dve.wait_ge(mp_turned, p * 4 + m + 1)
                    dve.tensor_copy(mprobs_t[:, m % 2, :, :].rearrange("p a b -> p (a b)"), ps[:, 4 + m, :]).then_inc(mpt_ready, 1)

            def pair_gate(p, ms):
                for m in ms:
                    h, tt = m // TT, m % TT
                    dve.wait_ge(mout_done, p * 4 + m + 1)
                    dve.wait_ge(mrec_ready, p * 4 + m + 1)
                    dve.scalar_tensor_tensor(om[:, m, :], ps[:, 4 + m, 0:VD], mrec[:, m:m + 1],
                                             proj_l[:, tt, bass.ds(p * 2 * VD + GATE0 + h * VD, VD)], ALU.mult, ALU.mult)\
                       .then_inc(om_ready, 1)

            def pair_out_lo(p):
                dve.wait_ge(om_hi_done, p + 1)
                v = om_hi[:, bass.ds(p * 2, 2), :].rearrange("p a b -> p (a b)")
                dve.tensor_tensor(om_lo[:, bass.ds(p * 2, 2), :].rearrange("p a b -> p (a b)"), ps[:, 7, :], v.bitcast(F32),
                                  ALU.subtract).then_inc(om_lo_done, 1)

            dve.wait_ge(kr_turned, 1)
            pair_rope(0)
            los(dve, C_HEADS, 0, 4, RING, RING + 2)
            pair_kn_lo(0)
            pair_q_lo(0)
            pair_v(0)
            los(dve, C_HEADS, 0, 4, RING + 2, RING + 4)
            dve.wait_ge(kr_hi_done, 1)
            dve.tensor_tensor(kr_lo[:, :, :], ps[:, 4:6, :], kr_hi[:, :, :].bitcast(F32), ALU.subtract).then_inc(kr_lo_done, 1)
            dve.wait_ge(gate_silu5, TT)
            with dve.Fori(0, PAIRS - 1) as i:
                pair_max(i)
                pair_turned(i, (0, 1))
                pair_rope(i + 1)
                los(dve, C_HEADS, i, 4, 2 * RING, 2 * RING + 2)
                pair_gate(i, (0, 1))
                pair_turned(i, (2, 3))
                pair_kn_lo(i + 1)
                pair_gate(i, (2, 3))
                pair_q_lo(i + 1)
                pair_v(i + 1)
                los(dve, C_HEADS, i, 4, 2 * RING + 2, 2 * RING + 4)
                pair_out_lo(i)
            pair_max(PAIRS - 1)
            for ms in ((0, 1), (2, 3)):
                pair_turned(PAIRS - 1, ms)
                pair_gate(PAIRS - 1, ms)
            pair_out_lo(PAIRS - 1)
            dve.wait_ge(gates_loaded, 16 * 3)
            for n in range(D // W):
                los(dve, C_MLA_OUT + n * CH, 0, 0, RING, RING + CH)
                yout_gated(1, n, 2 * (n % 2))
            yout_mean_square(1)
            for i in range(TT):
                yout_join(1, i, xres[:, i, :], xres[:, i, :])

        @block.tensor
        def _(pe):
            pe.sem_inc(chunks_used, RING)
            for s in (ada_turned, qk_turned, scored, p_turned, pv_done, b_summed):
                pe.sem_inc(s, PAIR)
            pe.wait_ge(consts_loaded, 16 * 3)
            pe.wait_ge(vecs_loaded, 16 * (len(VECS) - len(VECS[POOL_VECS]) + len(GAINS)))
            pe.wait_ge(more_vecs_loaded, 16 * len(VECS[POOL_VECS]))
            for v in range(VEC_TILES):
                mm = pe.transpose(ps[:, v // 4, (v % 4) * P:(v % 4 + 1) * P], vec_rows[:, v, :], ident)
            mm.then_inc(vecs_turned, 1)
            pe.wait_ge(table_loaded, 32)
            pe.wait_ge(consts_set, 4)
            pe.matmul(ps[0:HEADS_A, 2, 0:384], table[:, 0:HEADS_A], onehot[:, 0, :], start=True, stop=True)
            pe.matmul(ps[0:HEADS_C, 3, 0:384], table[:, HEADS_A:N_TAB], onehot[:, 1, :], start=True, stop=True).then_inc(ext_done, 1)

            pe.wait_ge(ext_ready, 2)

            def in_turn(i, peeled=False):
                def before(j):
                    if peeled and j < CH:
                        norm_ahead(pe, n_first, j)
                    if j == IN_TURN:
                        pe.wait_ge(lo_split, i * len(IN_ORDER) + C_IN + IN_ORDER.index((True, CH - 1)) + RING + 1)
                        turn_ada(pe, i, (0,), 5)

                for q in range(IN_PANELS):
                    pe.wait_ge(proj_taken, i * IN_PANELS + q + 1)
                    panel_by_tokens(pe, C_IN, i, IN_ORDER, q * CH, h_hi, h_lo, pair(q % 2), W_IN, before=before)

            in_turn(0, True)
            with pe.Fori(1, IN_TURNS) as i:
                in_turn(i)

            def turn_qk(h):
                pe.wait_ge(staged, h.n * 2 + 2)
                pe.wait_ge(qk_ready, h.n + 1)
                for i in range(TT):
                    mm = pe.transpose(ps[:, h.slot, i * P:(i + 1) * P], stage[:, h.slot, i, :, :].rearrange("p a b -> p (a b)"), ident)
                mm.then_inc(qk_turned, 1)

            def scores(h):
                pe.wait_ge(qk_ready, h.n + PAIR + 1)
                pe.wait_ge(logits_ready, h.n + 1)
                q, k, bank = qkt[:, h.slot, 0, :], qkt[:, h.slot, 1, :], 2 + h.slot
                if h.kind == "b":
                    pe.matmul(ps[:, bank, 0:2 * P], k[:, 0:P], q, start=True, stop=True)
                    pe.matmul(ps[:, bank, 2 * P:3 * P], k[:, P:2 * P], q[:, P:2 * P], start=True, stop=True).then_inc(scored, 1)
                else:
                    pe.matmul(ps[:, bank, 0:P], q[:, 0:P], k[:, 0:P], start=True, stop=True)
                    pe.matmul(ps[:, bank, P:3 * P], q[:, P:2 * P], k, start=True, stop=True).then_inc(scored, 1)

            def soft_turn(h):
                pe.wait_ge(exp_done, h.s + PAIR + 1)
                pe.wait_ge(pt_ready, h.s + 1)
                for b in range(3):
                    mm = pe.transpose(ps[:, 4 + h.slot, b * P:(b + 1) * P], probs[:, h.slot, b * P:(b + 1) * P], ident)
                mm.then_inc(p_turned, 1)

            def head_out(h, weights):
                pe.wait_ge(out_taken, h.s + 1)
                v = [proj[:, i, bass.ds(h.v, HD)] for i in range(TT)]
                bank = 6 + h.slot
                pe.matmul(ps[:, bank, 0:HD], weights[:, 0:P], v[0], start=True, stop=True)
                pe.matmul(ps[:, bank, HD:2 * HD], weights[:, P:2 * P], v[0], start=True, stop=False)
                pe.matmul(ps[:, bank, HD:2 * HD], weights[:, 2 * P:3 * P], v[1], start=False, stop=True).then_inc(pv_done, 1)

            def step(h, two, three):
                soft_turn(h)
                if two:
                    scores(two)
                if three:
                    turn_qk(three)
                pe.wait_ge(pt_ready, h.s + PAIR + 1)
                head_out(h, probs_t[:, h.slot, :])

            turn_qk(lead[0])
            turn_qk(lead[1])
            for h, ahead in zip(lead[:-2], lead[2:]):
                scores(h)
                turn_qk(ahead)
            scores(lead[-2])
            soft_steps(pe, step)

            def stick_sum(m):
                pe.wait_ge(b_soft, m // 2 + 1)
                pe.wait_ge(b_exponent, m + 1)
                bank = 4 + m % PAIR
                pe.matmul(ps[:, bank, 0:3 * P], stick[:, 3 * P:4 * P], b_w[:, m, :], start=True, stop=False)
                pe.matmul(ps[:, bank, P:2 * P], negones, b_w[:, m, 2 * P:3 * P], start=False, stop=True).then_inc(b_summed, 1)

            pe.wait_ge(pt_ready, PAIR + N_SOFT)
            for m in range(HEADS_B):
                stick_sum(m)
            for m in range(HEADS_B):
                pe.wait_ge(b_weights, m + 1)
                head_out(stick_head(m), b_w[:, m, :])

            for n in range(D // W):
                pe.wait_ge(attn_added, n + 1)
                panel_by_tokens(pe, C_OUT + n * CH, 0, PLAIN_ORDER, 0, h_hi, h_lo, pair(n % 2), W,
                                before=lambda j: norm_ahead(pe, n_mix, j) if n == 0 else None)
            def turn_u(i, which):
                pe.wait_ge(u_staged[which], FREE + i + 1)
                pe.wait_ge(taps[1 - which], FREE + i * 2 + 2 * which)
                for m in range(4):
                    for tok in range(TT):
                        mm = pe.transpose(turned_u(m)[:, tok * P:(tok + 1) * P], ustage[:, which, tok, m * P:(m + 1) * P], ident)
                mm.then_inc(u_turned[which], 1)

            def gate_panel(n, first, i, order, j0, before=None):
                pe.wait_ge(u_staged[0], FREE + n)
                panel_by_tokens(pe, first, i, order, j0, h_hi, h_lo, pair(0), W, before=before)

            def up_panel(n, first, i, order, j0):
                pe.wait_ge(u_staged[1], FREE + n)
                panel_by_tokens(pe, first, i, order, j0, h_hi, h_lo, pair(1), W,
                                before=lambda j: turn_u(n, 0) if j == j0 + 2 else None)

            gate_panel(0, C_UP, 0, PANEL_ORDER, 0, lambda j: norm_ahead(pe, n_ffn, j))
            with pe.Fori(0, UP_TURNS) as i:
                for e in range(UP_PAIRS):
                    n, j0 = i * UP_PAIRS + e, e * 2 * CH

                    def before(j):
                        if j == j0 + CH + 2:
                            turn_u(n, 1)
                        if j == UP_TURN:
                            pe.wait_ge(lo_split, i * len(UP_ORDER) + C_UP_LOOP + UP_ORDER.index((True, CH - 1)) + RING + 1)
                            turn_ada(pe, i + ADA_UP, (1,), 5)

                    up_panel(n, C_UP_LOOP, i, UP_ORDER, j0)
                    gate_panel(n + 1, C_UP_LOOP, i, UP_ORDER, j0 + CH, before)
            up_panel(N_UP - 1, C_UP_LAST, 0, PANEL_ORDER, 0)
            turn_u(N_UP - 1, 1)
            n = FT // CK_T
            with pe.Fori(0, D // W // 2) as i:
                def ada_before(j):
                    if j < n and j * CK_T % 4 == 0:
                        pe.wait_ge(g_lo_done, FREE + j * CK_T // 4 + 1)
                    for m, at in enumerate((DOWN_TURN, 2 * n - 1)):
                        if j == at:
                            pe.wait_ge(lo_split, i * len(DOWN_ORDER) + C_DOWN + DOWN_ORDER.index((True, m * CH + CH - 1)) + RING + 1)
                            turn_ada(pe, i * 2 + ADA_DOWN + m, (m,), 5)

                for half in range(2):
                    pe.wait_ge(ffn_added, i * 2 + half + 1)
                    panel_by_tokens(pe, C_DOWN, i, DOWN_ORDER, half * n, g_hi, g_lo, pair(half), W, FT, before=ada_before)
            pe.wait_ge(poolm_loaded, 16)
            streams = [(i, i) for i in range(NT)]

            def pool_group(i, e):
                n, step = i * 2 + e, len(POOL_ORDER)
                ada0 = i * 4 + ADA_POOL + 2 * e
                pe.wait_ge(grouped, FREE + n)
                pe.wait_ge(ada_taken, FREE + ada0)
                panel_by_tokens(pe, C_POOL, i, POOL_ORDER, e * POOL_W, h4_hi, h4_lo, streams, W,
                                before=lambda j: norm_ahead(pe, n_pool, j) if (i, e) == (0, 0) else None)

                def chunk(j, *a):
                    at = C_POOL + place(POOL_ORDER, e * POOL_W + CH + j)
                    by_channels(pe, i * step + at, at % RING, *a, ada_behind(at))

                pe.wait_ge(y_gated, FREE + n * 4)
                for j in range(2):
                    chunk(j, h4_hi, h4_lo, CK_T * j, 4, j == 0, False)
                pe.wait_ge(u_ready, n + 1)
                for m in range(4):
                    for s in range(2):
                        for k in range(TT):
                            c0 = k * (P - max(POOL_WINDOWS) // 2)
                            mm = pe.matmul(ps[:, m, s * SEQ + c0:(s + 1) * SEQ], u[:, TT * s + k, m * P:(m + 1) * P],
                                           poolm[:, bass.ds(n, 1), k, c0:].rearrange("p a b -> p (a b)"),
                                           start=k == 0, stop=k == TT - 1)
                    mm.then_inc(pooled, 1)
                for j in range(2, 4):
                    chunk(j, h4_hi, h4_lo, CK_T * j, 4, False, False)
                pe.wait_ge(pt_lo_done, FREE + n + 1)
                for j in range(4, 6):
                    chunk(j, pt_hi, pt_lo, CK_T * (j - 4), 0, j == 4, j == 5)
                for j in range(6, 10):
                    if j == 9:
                        pe.wait_ge(grouped, FREE + n + 1)
                        pe.wait_ge(lo_split, i * step + C_POOL + POOL_ORDER.index((True, (2 * e + 2) * CH - 1)) + RING + 1)
                        turn_ada(pe, ada0, range(PAIR), 0)
                    chunk(j, h4_hi, h4_lo, CK_T * (j - 2), 4, False, j == 9)

            for n in range(POOL_G):
                pool_group(n // 2, n % 2)

            def turn_gates(layer, bank):
                pe.wait_ge(gains_ready, 2 * layer + 2)
                pe.transpose(ps[0:2 * KT, bank, 0:P], hscale[:, :, :].rearrange("p s k -> p (s k)"), ident).then_inc(gates_turned, 1)

            def pool_out_turn(i, peeled):
                step = len(POOL_OUT_ORDER)

                def before(j):
                    if j < CH:
                        pe.wait_ge(y_lo_done, (j + 1) * CK_T)
                    if peeled and j == 0:
                        turn_gates(0, 4)
                    if j == POOL_OUT_TURN:
                        pe.wait_ge(lo_split, i * step + C_POOL_OUT + POOL_OUT_ORDER.index((True, 2 * CH - 1)) + RING + 1)
                        pe.wait_ge(yout_taken[0], PAIR + i * 2 + 1)
                        turn_ada(pe, i * 2 + ADA_POOL_OUT, range(PAIR), 0)

                for half in range(2):
                    if half and peeled:
                        pe.wait_ge(gates_out, 1)
                    pe.wait_ge(yout_taken[0], i * 2 + half + 1)
                    if half == 0:
                        pe.wait_ge(ada_taken, FREE + i * 2 + ADA_POOL_OUT)
                    panel_by_tokens(pe, C_POOL_OUT, i, POOL_OUT_ORDER, half * CH, y_hi, y_lo, [(n, 4 * half + n) for n in range(NT)], W,
                                    before=before)

            for i in range(D // W // 2):
                pool_out_turn(i, i == 0)
            def mla_ahead(p, j):
                if p == 0:
                    norm_ahead(pe, n_mla, j)
                if p == 1:
                    norm_ahead(pe, n_mla_ctx, j, False)
                if (p, j) == (5, 2):
                    norm_turn(pe, n_cq)
                if (p, j) == (5, 5):
                    pe.wait_ge(n_cq.lo_done, n_cq.all_groups)
                    norm_turn(pe, n_ckv)
                if (p, j) == (6, RING):
                    pe.wait_ge(n_ckv.lo_done, n_ckv.all_groups)
                    pe.wait_ge(kr_staged, 2 * NT)
                    for h in range(2):
                        for i in range(NT):
                            mm = pe.transpose(ps[:, 4 + h, i * P:(i + 1) * P], kr[:, i, h, :], ident)
                    mm.then_inc(kr_turned, 1)

            for p, n in enumerate(MLA_ORDER):
                pe.wait_ge(mla_taken, p + 1)
                if n == 1:
                    pe.wait_ge(n_mla_ctx.lo_done, n_mla_ctx.all_groups)
                    turn_gates(1, 7)
                if n == 2:
                    pe.wait_ge(gates_out, 2)
                ctx_too = [(TT + i, 2 + 2 * n + i) for i in range(TT)] if n in (1, 2) else []
                panel_by_tokens(pe, C_MLA + p * CH, 0, PLAIN_ORDER, 0, k4_hi, k4_lo, pair(p % 2) + ctx_too, W_IN,
                                before=lambda j: mla_ahead(p, j))

            def pair_queries(p, first, i):
                pe.wait_ge(q_lo_done, FREE + p)
                panel_by_tokens(pe, first, i, HEADS_ORDER, 0, cq_hi, cq_lo, pair(0), 2 * QH, RT)

            def pair_keys(p, h):
                if h == 0:
                    pe.wait_ge(lo_split, p * 4 + C_HEADS + RING + 4)
                    pe.wait_ge(v_ready, FREE + p)
                for k in range(RT):
                    for s, (w, a) in enumerate(((hi, ckv_hi), (hi, ckv_lo), (lo, ckv_hi))):
                        mm = pe.matmul(ps[:, 2 + h, :], w[:, 2 + k // CK_T, k % CK_T, h * 2 * P:h * 2 * P + P], a[:, k, :],
                                       start=k == 0 and s == 0, stop=k == RT - 1 and s == 2)
                if h == 1:
                    mm.then_inc(kn_summed, 1)

            def pair_turn(p):
                pe.wait_ge(q_nope_ready, p + 1)
                pe.wait_ge(q_rope_ready, p + 1)
                for h in range(2):
                    for tt in range(TT):
                        pe.transpose(ps[:, 0, h * SEQ + tt * P:h * SEQ + (tt + 1) * P], q_nope[:, tt, h, :], ident)
                for tt in range(TT):
                    mm = pe.transpose(ps[:, 1, tt * P:(tt + 1) * P], q_rope[:, tt, :, :].rearrange("p h e -> p (h e)"), ident)
                mm.then_inc(q_turned, 1)

            def pair_values(p):
                pe.wait_ge(kn_lo_done, p + 1)
                for n in range(NT):
                    for k in range(RT):
                        for s, (a, w) in enumerate(((ckv_hi, hi), (ckv_hi, lo), (ckv_lo, hi))):
                            v = w[:, 2 + k // CK_T, k % CK_T, :].rearrange("p (h e) -> p h e", h=2)[:, :, NOPE:]
                            mm = pe.matmul(ps[:, 2 + n // 2, (n % 2) * 2 * VD:(n % 2 + 1) * 2 * VD].rearrange("p (h e) -> p h e", h=2),
                                           a[:, k, n * P:(n + 1) * P], v, start=k == 0 and s == 0, stop=k == RT - 1 and s == 2)
                mm.then_inc(chunks_used, 2)

            def pair_scores(p):
                pe.wait_ge(q_lo_done, FREE + p + 1)
                for m in range(4):
                    if m == 3:
                        pe.wait_ge(om_lo_done, FREE + p)
                    h, q = m // TT, slice(m % TT * P, m % TT * P + P)
                    for s, (a, k) in enumerate(((qn_hi, kn_hi), (qn_hi, kn_lo), (qn_lo, kn_hi))):
                        pe.matmul(ps[:, 4 + m, :], a[:, h, q], k[:, h, :], start=s == 0, stop=False)
                    for s, (a, k) in enumerate(((qr_hi, kr_hi), (qr_hi, kr_lo), (qr_lo, kr_hi))):
                        mm = pe.matmul(ps[:, 4 + m, :], a[:, q], k[:, h, :], start=False, stop=s == 2)
                    mm.then_inc(mscored, 1)

            def pair_probs(p, ms):
                for m in ms:
                    pe.wait_ge(mexp_done, p * 4 + m + 1)
                    for k in range(NT):
                        mm = pe.transpose(ps[:, 4 + m, k * P:(k + 1) * P], mprobs[:, m, k * P:(k + 1) * P], ident)
                    mm.then_inc(mp_turned, 1)

            def pair_rows(p, ms):
                pe.wait_ge(v_ready, FREE + p + 1)
                for m in ms:
                    pe.wait_ge(mpt_ready, p * 4 + m + 1)
                    for k in range(NT):
                        mm = pe.matmul(ps[:, 4 + m, 0:VD], mprobs_t[:, m % 2, k, :], v_sb[:, k, m // TT * VD:(m // TT + 1) * VD],
                                       start=k == 0, stop=k == NT - 1)
                    mm.then_inc(mout_done, 1)

            def pair_columns(p):
                pe.wait_ge(om_ready, p * 4 + 4)
                for m in range(4):
                    mm = pe.transpose(ps[:, 7, m * P:(m + 1) * P], om[:, m, :], ident)
                mm.then_inc(om_turned, 1)

            pe.wait_ge(mla_taken, PAIR + len(MLA_ORDER))
            pair_queries(0, C_HEADS, 0)
            pair_keys(0, 0)
            pair_keys(0, 1)
            pair_turn(0)
            pair_values(0)
            pe.wait_ge(kr_lo_done, 1)
            with pe.Fori(0, PAIRS - 1) as i:
                pair_scores(i)
                pair_queries(i + 1, C_HEADS + RING, i)
                pair_probs(i, (0, 1))
                pair_keys(i + 1, 0)
                pair_rows(i, (0, 1))
                pair_probs(i, (2, 3))
                pair_keys(i + 1, 1)
                pair_rows(i, (2, 3))
                pair_turn(i + 1)
                pair_values(i + 1)
                pair_columns(i)
            pair_scores(PAIRS - 1)
            for ms in ((0, 1), (2, 3)):
                pair_probs(PAIRS - 1, ms)
                pair_rows(PAIRS - 1, ms)
            pair_columns(PAIRS - 1)
            pe.wait_ge(om_lo_done, FREE + PAIRS)
            for n in range(D // W):
                pe.wait_ge(yout_taken[1], n + 1)
                panel_by_tokens(pe, C_MLA_OUT + n * CH, 0, PLAIN_ORDER, 0, om_hi, om_lo, pair(n % 2), W)


_OUTS = [((1, SEQ, D), "float32")]


def kernel(**inputs):
    import concourse.bacc as bacc
    from concourse.bass_utils import run_bass_kernel_spmd

    nc = bacc.Bacc("TRN2", target_bir_lowering=False, num_devices=1)
    arrays, t = {}, {}
    for name, a in inputs.items():
        a = np.ascontiguousarray(a)
        arrays[f"in_{name}"] = a
        t[name] = nc.dram_tensor(f"in_{name}", a.shape, mybir.dt.from_np(a.dtype), kind="ExternalInput").ap()
    consts = {name: nc.inline_tensor(a, name=f"const_{name}").ap() for name, a in shape_constants().items()}
    out = nc.dram_tensor("out", (1, SEQ, D), F32, kind="ExternalOutput").ap()
    two_block_kernel(nc, t, out, consts)
    r = run_bass_kernel_spmd(nc, [arrays], core_ids=[0])
    return r.results[0]["out"]
```
